# Optimizing a Trainium2 kernel written in Bass

```python
import math
import jax
import jax.numpy as jnp
from jax import lax
import numpy as np
import jax, jax.numpy as jnp

D_MODEL = 1024
BATCH = 1
SEQ = 512
DEPTH = 2

N_EVEN = (DEPTH + 1) // 2
N_ODD = DEPTH // 2
Q_BLOCK = 128
RMS_EPS = 1e-6
NEG_INF = -1e30
FOX_HEADS = 8
FOX_HEAD_DIM = 64
FOX_WIDTH = FOX_HEADS * FOX_HEAD_DIM
FORGET_BIAS_MEAN = 3.0
MLA_HEADS = 8
MLA_NOPE_DIM = 64
MLA_ROPE_DIM = 32
MLA_V_DIM = 64
MLA_Q_RANK = 384
MLA_KV_RANK = 256
ROPE_THETA = 10000.0
EVEN_IN_WIDTH = 3 * FOX_WIDTH + FOX_HEADS + MLA_Q_RANK + MLA_KV_RANK + MLA_ROPE_DIM
EVEN_MIX_WIDTH = FOX_WIDTH + MLA_HEADS * MLA_V_DIM
DIFF_HEADS = 8
DIFF_HEAD_DIM = 64
DIFF_V_DIM = 2 * DIFF_HEAD_DIM
ODD_IN_WIDTH = 4 * DIFF_HEADS * DIFF_HEAD_DIM + DIFF_HEADS * DIFF_V_DIM
ODD_MIX_WIDTH = DIFF_HEADS * DIFF_V_DIM
D_FF = 2816
CONV_WIDTH = 3


def _rms_norm(x, g):
    xf = x.astype(jnp.float32)
    y = xf * lax.rsqrt(jnp.mean(xf * xf, axis=-1, keepdims=True) + RMS_EPS)
    return (y * g.astype(jnp.float32)).astype(x.dtype)

def _rope_tables(seq, dim, dtype):
    inv = ROPE_THETA ** (-jnp.arange(0, dim, 2, dtype=jnp.float32) / dim)
    ang = jnp.arange(seq, dtype=jnp.float32)[:, None] * inv[None, :]
    return jnp.cos(ang).astype(dtype), jnp.sin(ang).astype(dtype)

def _apply_rope(x, cos, sin):
    x1, x2 = jnp.split(x, 2, axis=-1)
    return jnp.concatenate([x1 * cos - x2 * sin, x1 * sin + x2 * cos], axis=-1)

def _alibi_slopes(n):
    return 2.0 ** (-8.0 * jnp.arange(1, n + 1, dtype=jnp.float32) / n)

def _causal_mask(s0, seq):
    qpos = s0 + jnp.arange(Q_BLOCK)
    kpos = jnp.arange(seq)
    return qpos[:, None] >= kpos[None, :], (qpos[:, None] - kpos[None, :]).astype(jnp.float32)

def _merge_blocks(o):
    o = jnp.moveaxis(o, 0, 1)
    return o.reshape(o.shape[0], -1, o.shape[3] * o.shape[4])

def _fox_attention(q, k, v, log_f):
    seq, dh = q.shape[1], q.shape[3]
    c = jnp.cumsum(log_f, axis=1).transpose(0, 2, 1)
    scale = dh ** -0.5

    def block(i):
        s0 = i * Q_BLOCK
        qb = lax.dynamic_slice_in_dim(q, s0, Q_BLOCK, axis=1)
        cq = lax.dynamic_slice_in_dim(c, s0, Q_BLOCK, axis=2)
        mask, _ = _causal_mask(s0, seq)
        logits = jnp.einsum('bqhd,bkhd->bhqk', qb, k).astype(jnp.float32) * scale
        logits = logits + cq[..., :, None] - c[..., None, :]
        logits = jnp.where(mask, logits, NEG_INF)
        p = jax.nn.softmax(logits, axis=-1).astype(v.dtype)
        return jnp.einsum('bhqk,bkhd->bqhd', p, v)

    return _merge_blocks(lax.map(block, jnp.arange(seq // Q_BLOCK)))

def _mla_attention(q_nope, q_rope, k_nope, k_rope, v):
    seq = q_nope.shape[1]
    scale = (MLA_NOPE_DIM + MLA_ROPE_DIM) ** -0.5

    def block(i):
        s0 = i * Q_BLOCK
        qn = lax.dynamic_slice_in_dim(q_nope, s0, Q_BLOCK, axis=1)
        qr = lax.dynamic_slice_in_dim(q_rope, s0, Q_BLOCK, axis=1)
        mask, _ = _causal_mask(s0, seq)
        logits = (jnp.einsum('bqhd,bkhd->bhqk', qn, k_nope)
                  + jnp.einsum('bqhr,bkr->bhqk', qr, k_rope)).astype(jnp.float32) * scale
        logits = jnp.where(mask, logits, NEG_INF)
        p = jax.nn.softmax(logits, axis=-1).astype(v.dtype)
        return jnp.einsum('bhqk,bkhd->bqhd', p, v)

    return _merge_blocks(lax.map(block, jnp.arange(seq // Q_BLOCK)))

def _diff_attention(q1, q2, k1, k2, v, lam, slopes):
    seq, dh = q1.shape[1], q1.shape[3]
    scale = dh ** -0.5

    def block(i):
        s0 = i * Q_BLOCK
        q1b = lax.dynamic_slice_in_dim(q1, s0, Q_BLOCK, axis=1)
        q2b = lax.dynamic_slice_in_dim(q2, s0, Q_BLOCK, axis=1)
        mask, dist = _causal_mask(s0, seq)
        alibi = -slopes[:, None, None] * dist[None]
        l1 = jnp.einsum('bqhd,bkhd->bhqk', q1b, k1).astype(jnp.float32) * scale + alibi
        l2 = jnp.einsum('bqhd,bkhd->bhqk', q2b, k2).astype(jnp.float32) * scale + alibi
        p = (jax.nn.softmax(jnp.where(mask, l1, NEG_INF), axis=-1)
             - lam * jax.nn.softmax(jnp.where(mask, l2, NEG_INF), axis=-1)).astype(v.dtype)
        return jnp.einsum('bhqk,bkhd->bqhd', p, v)

    return _merge_blocks(lax.map(block, jnp.arange(seq // Q_BLOCK)))

def _even_mixer(h, w_in, b_forget, q_norm, w_uq, kv_norm, w_ukv, w_out, cos, sin):
    bsz, seq, _ = h.shape
    proj = h @ w_in
    cuts = np.cumsum([FOX_WIDTH, FOX_WIDTH, FOX_WIDTH, FOX_HEADS, MLA_Q_RANK, MLA_KV_RANK]).tolist()
    fq, fk, fv, fg, c_q, c_kv, k_r = jnp.split(proj, cuts, axis=-1)
    shp = (bsz, seq, FOX_HEADS, FOX_HEAD_DIM)
    log_f = jax.nn.log_sigmoid((fg + b_forget).astype(jnp.float32))
    fox_out = _fox_attention(fq.reshape(shp), fk.reshape(shp), fv.reshape(shp), log_f)
    q = (_rms_norm(c_q, q_norm) @ w_uq).reshape(bsz, seq, MLA_HEADS, MLA_NOPE_DIM + MLA_ROPE_DIM)
    q_nope, q_rope = jnp.split(q, [MLA_NOPE_DIM], axis=-1)
    q_rope = _apply_rope(q_rope, cos[:, None, :], sin[:, None, :])
    kv = (_rms_norm(c_kv, kv_norm) @ w_ukv).reshape(bsz, seq, MLA_HEADS, MLA_NOPE_DIM + MLA_V_DIM)
    k_nope, v = jnp.split(kv, [MLA_NOPE_DIM], axis=-1)
    k_rope = _apply_rope(k_r, cos, sin)
    mla_out = _mla_attention(q_nope, q_rope, k_nope, k_rope, v)
    return jnp.concatenate([fox_out, mla_out], axis=-1) @ w_out

def _odd_mixer(h, w_in, lq1, lk1, lq2, lk2, subln, w_out, slopes, lambda_init):
    bsz, seq, _ = h.shape
    qk_w = DIFF_HEADS * 2 * DIFF_HEAD_DIM
    q, k, v = jnp.split(h @ w_in, [qk_w, 2 * qk_w], axis=-1)
    q = q.reshape(bsz, seq, DIFF_HEADS, 2, DIFF_HEAD_DIM)
    k = k.reshape(bsz, seq, DIFF_HEADS, 2, DIFF_HEAD_DIM)
    v = v.reshape(bsz, seq, DIFF_HEADS, DIFF_V_DIM)
    f32 = jnp.float32
    lam = (jnp.exp(jnp.sum(lq1.astype(f32) * lk1.astype(f32)))
           - jnp.exp(jnp.sum(lq2.astype(f32) * lk2.astype(f32))) + lambda_init)
    o = _diff_attention(q[..., 0, :], q[..., 1, :], k[..., 0, :], k[..., 1, :], v, lam, slopes)
    o = o.reshape(bsz, seq, DIFF_HEADS, DIFF_V_DIM)
    o = _rms_norm(o, subln) * (1.0 - lambda_init)
    return o.reshape(bsz, seq, ODD_MIX_WIDTH) @ w_out

def _causal_dwconv(a, w, b):
    seq = a.shape[1]
    ap = jnp.pad(a, ((0, 0), (CONV_WIDTH - 1, 0), (0, 0)))
    out = b
    for tap in range(CONV_WIDTH):
        out = out + ap[:, tap:tap + seq] * w[tap]
    return out

def _conv_ffn(h, w_up, conv_w, conv_b, w_down):
    gate, val = jnp.split(h @ w_up, [D_FF], axis=-1)
    act = jax.nn.gelu(_causal_dwconv(gate, conv_w, conv_b), approximate=True)
    return (act * val) @ w_down

def first_inputs(seed: int = 0) -> dict:
    key = jax.random.key(seed)
    ks = jax.random.split(key, 23)
    f32 = jnp.float32

    def nrm(k, shape, scale):
        return jax.random.normal(k, shape, f32) * scale

    def gain(k, shape):
        return 1.0 + nrm(k, shape, 0.1)

    return {
        'x': nrm(ks[0], (BATCH, SEQ, D_MODEL), 1.0),
        'norm_mix_pre': gain(ks[1], (DEPTH, D_MODEL)),
        'norm_mix_post': gain(ks[2], (DEPTH, D_MODEL)),
        'norm_ffn_pre': gain(ks[3], (DEPTH, D_MODEL)),
        'norm_ffn_post': gain(ks[4], (DEPTH, D_MODEL)),
        'even_w_in': nrm(ks[5], (N_EVEN, D_MODEL, EVEN_IN_WIDTH), D_MODEL ** -0.5),
        'even_b_forget': FORGET_BIAS_MEAN + nrm(ks[6], (N_EVEN, FOX_HEADS), 0.5),
        'even_q_norm': gain(ks[7], (N_EVEN, MLA_Q_RANK)),
        'even_w_uq': nrm(ks[8], (N_EVEN, MLA_Q_RANK, MLA_HEADS * (MLA_NOPE_DIM + MLA_ROPE_DIM)), MLA_Q_RANK ** -0.5),
        'even_kv_norm': gain(ks[9], (N_EVEN, MLA_KV_RANK)),
        'even_w_ukv': nrm(ks[10], (N_EVEN, MLA_KV_RANK, MLA_HEADS * (MLA_NOPE_DIM + MLA_V_DIM)), MLA_KV_RANK ** -0.5),
        'even_w_out': nrm(ks[11], (N_EVEN, EVEN_MIX_WIDTH, D_MODEL), EVEN_MIX_WIDTH ** -0.5),
        'odd_w_in': nrm(ks[12], (N_ODD, D_MODEL, ODD_IN_WIDTH), D_MODEL ** -0.5),
        'odd_lambda_q1': nrm(ks[13], (N_ODD, DIFF_HEAD_DIM), 0.1),
        'odd_lambda_k1': nrm(ks[14], (N_ODD, DIFF_HEAD_DIM), 0.1),
        'odd_lambda_q2': nrm(ks[15], (N_ODD, DIFF_HEAD_DIM), 0.1),
        'odd_lambda_k2': nrm(ks[16], (N_ODD, DIFF_HEAD_DIM), 0.1),
        'odd_subln': gain(ks[17], (N_ODD, DIFF_V_DIM)),
        'odd_w_out': nrm(ks[18], (N_ODD, ODD_MIX_WIDTH, D_MODEL), ODD_MIX_WIDTH ** -0.5),
        'ffn_w_up': nrm(ks[19], (DEPTH, D_MODEL, 2 * D_FF), D_MODEL ** -0.5),
        'ffn_conv_w': nrm(ks[20], (DEPTH, CONV_WIDTH, D_FF), CONV_WIDTH ** -0.5),
        'ffn_conv_b': nrm(ks[21], (DEPTH, D_FF), 0.02),
        'ffn_w_down': nrm(ks[22], (DEPTH, D_FF, D_MODEL), D_FF ** -0.5),
    }

def first_block(x, norm_mix_pre, norm_mix_post, norm_ffn_pre, norm_ffn_post,
              even_w_in, even_b_forget, even_q_norm, even_w_uq, even_kv_norm, even_w_ukv, even_w_out,
              odd_w_in, odd_lambda_q1, odd_lambda_k1, odd_lambda_q2, odd_lambda_k2, odd_subln, odd_w_out,
              ffn_w_up, ffn_conv_w, ffn_conv_b, ffn_w_down):
    cos, sin = _rope_tables(x.shape[1], MLA_ROPE_DIM, x.dtype)
    slopes = _alibi_slopes(DIFF_HEADS)
    for layer in range(DEPTH):
        i = layer // 2
        h = _rms_norm(x, norm_mix_pre[layer])
        if layer % 2 == 0:
            m = _even_mixer(h, even_w_in[i], even_b_forget[i], even_q_norm[i], even_w_uq[i],
                            even_kv_norm[i], even_w_ukv[i], even_w_out[i], cos, sin)
        else:
            lambda_init = 0.8 - 0.6 * math.exp(-0.3 * layer)
            m = _odd_mixer(h, odd_w_in[i], odd_lambda_q1[i], odd_lambda_k1[i], odd_lambda_q2[i],
                           odd_lambda_k2[i], odd_subln[i], odd_w_out[i], slopes, lambda_init)
        x = x + _rms_norm(m, norm_mix_post[layer])
        h = _rms_norm(x, norm_ffn_pre[layer])
        f = _conv_ffn(h, ffn_w_up[layer], ffn_conv_w[layer], ffn_conv_b[layer], ffn_w_down[layer])
        x = x + _rms_norm(f, norm_ffn_post[layer])
    return x


DEPTH_2 = 1

N_MIXERS = 2
DN_HEAD_DIM = 128
DN_HEADS = D_MODEL // DN_HEAD_DIM
DN_WIDTH = DN_HEADS * DN_HEAD_DIM
DN_CONV = 4
DN_CHUNK = 64
DN_IN = 4 * DN_WIDTH + 2 * DN_HEADS
SWA_HEAD_DIM = 64
SWA_HEADS = D_MODEL // SWA_HEAD_DIM
SWA_KV_HEADS = SWA_HEADS // 8
SWA_GROUP = SWA_HEADS // SWA_KV_HEADS
SWA_QKV = (SWA_HEADS + 2 * SWA_KV_HEADS) * SWA_HEAD_DIM
WINDOW = 128
SWA_BLOCK = WINDOW
NUM_BUCKETS = 32
MAX_DISTANCE = 128
D_FF_2 = 4 * D_MODEL
N_DN_LAYERS = (DEPTH_2 + N_MIXERS - 1) // N_MIXERS
N_SWA_LAYERS = DEPTH_2 // N_MIXERS


def rms_norm(x, w):
    xf = x.astype(jnp.float32)
    y = xf * lax.rsqrt(jnp.mean(xf * xf, axis=-1, keepdims=True) + RMS_EPS)
    return (y * w.astype(jnp.float32)).astype(x.dtype)

def l2_normalize(t):
    return t * lax.rsqrt(jnp.sum(t * t, axis=-1, keepdims=True) + RMS_EPS)

def causal_depthwise_conv(x, w):
    k = w.shape[0]
    return lax.conv_general_dilated(
        x, w[:, None, :].astype(x.dtype), window_strides=(1,), padding=[(k - 1, 0)],
        dimension_numbers=('NWC', 'WIO', 'NWC'), feature_group_count=x.shape[-1])

def chunk_gated_delta_rule(q, k, v, beta, g):
    B, S, H, DK = q.shape
    DV = v.shape[-1]
    C = DN_CHUNK
    N = S // C

    def to_chunks(t):
        return t.reshape(B, N, C, H, -1).transpose(0, 3, 1, 2, 4)

    q = to_chunks(q) * (DK ** -0.5)
    k = to_chunks(k)
    v = to_chunks(v)
    beta = beta.reshape(B, N, C, H).transpose(0, 3, 1, 2)
    gc = jnp.cumsum(g.reshape(B, N, C, H).transpose(0, 3, 1, 2), axis=-1)
    causal = jnp.tril(jnp.ones((C, C), dtype=bool))
    strict = jnp.tril(jnp.ones((C, C), dtype=bool), -1)
    decay = jnp.exp(jnp.where(causal, gc[..., :, None] - gc[..., None, :], -jnp.inf))
    k_beta = k * beta[..., None]
    lower = jnp.where(strict, jnp.einsum('bhnid,bhnjd->bhnij', k_beta, k) * decay, 0.0)
    eye = jnp.eye(C, dtype=jnp.float32)
    rhs = jnp.concatenate([v * beta[..., None], k_beta * jnp.exp(gc)[..., None]], axis=-1)
    sol = lax.linalg.triangular_solve(lower + eye, rhs, left_side=True, lower=True, unit_diagonal=True)
    u, w = sol[..., :DV], sol[..., DV:]
    attn = jnp.einsum('bhnid,bhnjd->bhnij', q, k) * decay
    q_dec = q * jnp.exp(gc)[..., None]
    k_dec = k * jnp.exp(gc[..., -1:] - gc)[..., None]
    g_last = jnp.exp(gc[..., -1])
    xs = tuple(jnp.moveaxis(t, 2, 0) for t in (q_dec, k_dec, u, w, attn, g_last))

    def step(state, inp):
        q_c, k_c, u_c, w_c, a_c, gl = inp
        v_new = u_c - jnp.einsum('bhck,bhkv->bhcv', w_c, state)
        o_c = jnp.einsum('bhck,bhkv->bhcv', q_c, state) + jnp.einsum('bhij,bhjv->bhiv', a_c, v_new)
        state = state * gl[..., None, None] + jnp.einsum('bhck,bhcv->bhkv', k_c, v_new)
        return state, o_c

    s0 = jnp.zeros((B, H, DK, DV), jnp.float32)
    _, o = lax.scan(step, s0, xs)
    return o.transpose(1, 0, 3, 2, 4).reshape(B, S, H, DV)

def gated_deltanet(h, w_in, conv_w, a_log, dt_bias, norm_w, w_out):
    B, S, _ = h.shape
    proj = h @ w_in
    qkv = jax.nn.silu(causal_depthwise_conv(proj[..., :3 * DN_WIDTH], conv_w))
    z = proj[..., 3 * DN_WIDTH:4 * DN_WIDTH]
    b = proj[..., 4 * DN_WIDTH:4 * DN_WIDTH + DN_HEADS]
    a = proj[..., 4 * DN_WIDTH + DN_HEADS:]
    q, k, v = jnp.split(qkv.astype(jnp.float32), 3, axis=-1)
    q = l2_normalize(q.reshape(B, S, DN_HEADS, DN_HEAD_DIM))
    k = l2_normalize(k.reshape(B, S, DN_HEADS, DN_HEAD_DIM))
    v = v.reshape(B, S, DN_HEADS, DN_HEAD_DIM)
    beta = jax.nn.sigmoid(b.astype(jnp.float32))
    g = -jnp.exp(a_log.astype(jnp.float32)) * jax.nn.softplus(a.astype(jnp.float32) + dt_bias.astype(jnp.float32))
    o = chunk_gated_delta_rule(q, k, v, beta, g)
    zf = z.reshape(B, S, DN_HEADS, DN_HEAD_DIM).astype(jnp.float32)
    o = o * lax.rsqrt(jnp.mean(o * o, axis=-1, keepdims=True) + RMS_EPS) * norm_w.astype(jnp.float32) * jax.nn.silu(zf)
    return o.reshape(B, S, DN_WIDTH).astype(h.dtype) @ w_out

def t5_causal_bucket(dist):
    n = jnp.maximum(dist, 0)
    max_exact = NUM_BUCKETS // 2
    large = max_exact + (jnp.log(jnp.maximum(n, 1).astype(jnp.float32) / max_exact)
                         / math.log(MAX_DISTANCE / max_exact) * (NUM_BUCKETS - max_exact)).astype(jnp.int32)
    large = jnp.minimum(large, NUM_BUCKETS - 1)
    return jnp.where(n < max_exact, n, large)

def sliding_window_sink_attention(h, w_qkv, b_qkv, sinks, w_out, b_out, rel_bias):
    B, S, _ = h.shape
    NB = S // SWA_BLOCK
    qkv = h @ w_qkv + b_qkv
    q = qkv[..., :SWA_HEADS * SWA_HEAD_DIM].reshape(B, NB, SWA_BLOCK, SWA_KV_HEADS, SWA_GROUP, SWA_HEAD_DIM)
    k = qkv[..., SWA_HEADS * SWA_HEAD_DIM:(SWA_HEADS + SWA_KV_HEADS) * SWA_HEAD_DIM]
    v = qkv[..., (SWA_HEADS + SWA_KV_HEADS) * SWA_HEAD_DIM:]
    k = k.reshape(B, NB, SWA_BLOCK, SWA_KV_HEADS, SWA_HEAD_DIM)
    v = v.reshape(B, NB, SWA_BLOCK, SWA_KV_HEADS, SWA_HEAD_DIM)
    pad = ((0, 0), (1, 0), (0, 0), (0, 0), (0, 0))
    kk = jnp.concatenate([jnp.pad(k[:, :-1], pad), k], axis=2)
    vv = jnp.concatenate([jnp.pad(v[:, :-1], pad), v], axis=2)
    logits = jnp.einsum('bnqhgd,bnkhd->bnhgqk', q, kk).astype(jnp.float32) * (SWA_HEAD_DIM ** -0.5)
    qi = jnp.arange(SWA_BLOCK)[:, None]
    kj = jnp.arange(2 * SWA_BLOCK)[None, :]
    dist = qi + SWA_BLOCK - kj
    bias = rel_bias[t5_causal_bucket(dist)].astype(jnp.float32)
    bias = bias.transpose(2, 0, 1).reshape(SWA_KV_HEADS, SWA_GROUP, SWA_BLOCK, 2 * SWA_BLOCK)
    key_pos = jnp.arange(NB)[:, None] * SWA_BLOCK - SWA_BLOCK + kj
    valid = ((dist >= 0) & (dist < WINDOW))[None] & (key_pos >= 0)[:, None, :]
    logits = jnp.where(valid[None, :, None, None], logits + bias, -jnp.inf)
    sink = sinks.astype(jnp.float32).reshape(SWA_KV_HEADS, SWA_GROUP)[None, None, :, :, None, None]
    m = jnp.maximum(jnp.max(logits, axis=-1, keepdims=True), sink)
    p = jnp.exp(logits - m)
    p = p / (jnp.sum(p, axis=-1, keepdims=True) + jnp.exp(sink - m))
    out = jnp.einsum('bnhgqk,bnkhd->bnqhgd', p.astype(vv.dtype), vv)
    out = out.reshape(B, S, SWA_HEADS * SWA_HEAD_DIM)
    return out @ w_out + b_out

def squared_relu_mlp(h, w_up, w_down):
    return jnp.square(jax.nn.relu(h @ w_up)) @ w_down

def second_inputs(seed: int = 0) -> dict:
    key = jax.random.key(seed)
    ks = jax.random.split(key, 18)
    f32 = jnp.float32

    def nrm(k, shape, scale):
        return jax.random.normal(k, shape, f32) * scale

    x = nrm(ks[0], (BATCH, SEQ, D_MODEL), 1.0)
    norm_mix = 1.0 + nrm(ks[1], (DEPTH_2, D_MODEL), 0.02)
    norm_mlp = 1.0 + nrm(ks[2], (DEPTH_2, D_MODEL), 0.02)
    norm_final = 1.0 + nrm(ks[3], (D_MODEL,), 0.02)
    dn_w_in = nrm(ks[4], (N_DN_LAYERS, D_MODEL, DN_IN), D_MODEL ** -0.5)
    dn_conv_w = nrm(ks[5], (N_DN_LAYERS, DN_CONV, 3 * DN_WIDTH), DN_CONV ** -0.5)
    dn_a_log = jnp.log(jax.random.uniform(ks[6], (N_DN_LAYERS, DN_HEADS), f32, 1.0, 16.0))
    dt = jnp.exp(jax.random.uniform(ks[7], (N_DN_LAYERS, DN_HEADS), f32, math.log(1e-3), math.log(1e-1)))
    dn_dt_bias = dt + jnp.log(-jnp.expm1(-dt))
    dn_norm_w = 1.0 + nrm(ks[8], (N_DN_LAYERS, DN_HEAD_DIM), 0.02)
    dn_w_out = nrm(ks[9], (N_DN_LAYERS, DN_WIDTH, D_MODEL), DN_WIDTH ** -0.5)
    swa_w_qkv = nrm(ks[10], (N_SWA_LAYERS, D_MODEL, SWA_QKV), D_MODEL ** -0.5)
    swa_b_qkv = nrm(ks[11], (N_SWA_LAYERS, SWA_QKV), 0.02)
    swa_sinks = nrm(ks[12], (N_SWA_LAYERS, SWA_HEADS), 0.5)
    swa_w_out = nrm(ks[13], (N_SWA_LAYERS, SWA_HEADS * SWA_HEAD_DIM, D_MODEL), (SWA_HEADS * SWA_HEAD_DIM) ** -0.5)
    swa_b_out = nrm(ks[14], (N_SWA_LAYERS, D_MODEL), 0.02)
    rel_bias = nrm(ks[15], (NUM_BUCKETS, SWA_HEADS), 0.5)
    mlp_w_up = nrm(ks[16], (DEPTH_2, D_MODEL, D_FF_2), D_MODEL ** -0.5)
    mlp_w_down = nrm(ks[17], (DEPTH_2, D_FF_2, D_MODEL), D_FF_2 ** -0.5)
    return {'x': x, 'norm_mix': norm_mix, 'norm_mlp': norm_mlp, 'norm_final': norm_final,
            'dn_w_in': dn_w_in, 'dn_conv_w': dn_conv_w, 'dn_a_log': dn_a_log, 'dn_dt_bias': dn_dt_bias,
            'dn_norm_w': dn_norm_w, 'dn_w_out': dn_w_out,
            'swa_w_qkv': swa_w_qkv, 'swa_b_qkv': swa_b_qkv, 'swa_sinks': swa_sinks,
            'swa_w_out': swa_w_out, 'swa_b_out': swa_b_out, 'rel_bias': rel_bias,
            'mlp_w_up': mlp_w_up, 'mlp_w_down': mlp_w_down}

def second_block(x, norm_mix, norm_mlp, norm_final, dn_w_in, dn_conv_w, dn_a_log, dn_dt_bias, dn_norm_w,
              dn_w_out, swa_w_qkv, swa_b_qkv, swa_sinks, swa_w_out, swa_b_out, rel_bias,
              mlp_w_up, mlp_w_down):
    for i in range(DEPTH_2):
        h = rms_norm(x, norm_mix[i])
        j = i // N_MIXERS
        if i % N_MIXERS == 0:
            y = gated_deltanet(h, dn_w_in[j], dn_conv_w[j], dn_a_log[j], dn_dt_bias[j], dn_norm_w[j], dn_w_out[j])
        else:
            y = sliding_window_sink_attention(h, swa_w_qkv[j], swa_b_qkv[j], swa_sinks[j], swa_w_out[j],
                                              swa_b_out[j], rel_bias)
        x = x + y
        x = x + squared_relu_mlp(rms_norm(x, norm_mlp[i]), mlp_w_up[i], mlp_w_down[i])
    return rms_norm(x, norm_final)


def setup_inputs(seed=0):
    out = dict(first_inputs(seed))
    for name, value in second_inputs(seed + 1).items():
        if name != "x":
            out[name + "_2"] = value
    return out


def reference(
    x, norm_mix_pre, norm_mix_post, norm_ffn_pre, norm_ffn_post, even_w_in, even_b_forget,
    even_q_norm, even_w_uq, even_kv_norm, even_w_ukv, even_w_out, odd_w_in, odd_lambda_q1,
    odd_lambda_k1, odd_lambda_q2, odd_lambda_k2, odd_subln, odd_w_out, ffn_w_up, ffn_conv_w,
    ffn_conv_b, ffn_w_down, norm_mix_2, norm_mlp_2, norm_final_2, dn_w_in_2, dn_conv_w_2,
    dn_a_log_2, dn_dt_bias_2, dn_norm_w_2, dn_w_out_2, swa_w_qkv_2, swa_b_qkv_2, swa_sinks_2,
    swa_w_out_2, swa_b_out_2, rel_bias_2, mlp_w_up_2, mlp_w_down_2,
):
    x = first_block(
        x, norm_mix_pre, norm_mix_post, norm_ffn_pre, norm_ffn_post, even_w_in, even_b_forget,
        even_q_norm, even_w_uq, even_kv_norm, even_w_ukv, even_w_out, odd_w_in, odd_lambda_q1,
        odd_lambda_k1, odd_lambda_q2, odd_lambda_k2, odd_subln, odd_w_out, ffn_w_up, ffn_conv_w,
        ffn_conv_b, ffn_w_down,
    )
    return second_block(
        x, norm_mix_2, norm_mlp_2, norm_final_2, dn_w_in_2, dn_conv_w_2, dn_a_log_2,
        dn_dt_bias_2, dn_norm_w_2, dn_w_out_2, swa_w_qkv_2, swa_b_qkv_2, swa_sinks_2,
        swa_w_out_2, swa_b_out_2, rel_bias_2, mlp_w_up_2, mlp_w_down_2,
    )


_drawn_inputs = setup_inputs


def setup_inputs(seed=0):
    import zlib

    import numpy as np

    out = dict(_drawn_inputs(seed))
    spreads = {}
    factors = {'odd_lambda_k1': 2.72,
     'ffn_conv_b': 3.096,
     'norm_mix_2': 6.371,
     'norm_mlp_2': 18.443,
     'norm_final_2': 8.071,
     'dn_norm_w_2': 23.086}
    for name, (base, spread) in spreads.items():
        noise = np.random.default_rng([zlib.crc32(name.encode()), seed]).standard_normal(out[name].shape)
        drawn = base * np.exp(spread * noise) if base else spread * noise
        out[name] = jnp.asarray(drawn.astype(out[name].dtype))
    for name, factor in factors.items():
        out[name] = (out[name] * factor).astype(out[name].dtype)
    return out
```

```python
from contextlib import ExitStack, contextmanager

import numpy as np
import concourse.bass as bass
import concourse.mybir as mybir

F32 = mybir.dt.float32
F32R = mybir.dt.float32r
ACT = mybir.ActivationFunctionType
ALU = mybir.AluOpType
AX = mybir.AxisListType

P = 128
SEQ, DM = 512, 1024
KT = DM // P
TT = SEQ // P
H = 8
FF_T = 2816 // P
FF_GROUPS = (12, 10)
MLP_GROUP = 16
EPS = 1e-6
NEG = -1e30
FAR = 384
LAMBDA_INIT = 0.8 - 0.6 * float(np.exp(-0.3))
SLOT = 2048

STREAMS = [("even_in", 9, 2048), ("even_uq", 2, 1152), ("even_ukv", 1, 2048), ("even_out", 4, 2048)]
for _l in range(2):
    if _l == 1:
        STREAMS += [("odd_q", 4, 2048), ("odd_k", 4, 2048), ("odd_v", 4, 2048), ("odd_out", 4, 2048)]
    for _g in range(2):
        STREAMS += [(f"ffn{_l}_up{_g}", FF_GROUPS[_g], 2048), (f"ffn{_l}_down{_g}", KT, FF_GROUPS[_g] * P)]
STREAMS += [("dn_qkv", 12, 2048), ("dn_z", 4, 2048), ("dn_out", 4, 2048)]
STREAMS += [("mlp_up0", 8, 2048), ("mlp_down0", 8, 2048), ("mlp_up1", 8, 2048), ("mlp_down1", 4, 2048), ("mlp_down2", 4, 2048)]
UNITS = sum(u for _, u, _ in STREAMS)
UNIT0, _n = {}, 0
for _name, _u, _w in STREAMS:
    UNIT0[_name] = _n
    _n += _u
NUNITS = {name: u for name, u, _ in STREAMS}
WIDTH = {name: w for name, _, w in STREAMS}
TILES = {"even_in": 6 + 8 + 8, "even_uq": 8, "even_ukv": 8 + 4, "odd_v": 16}
for _name, _u, _w in STREAMS:
    TILES.setdefault(_name, _u if "down" in _name else 2 * _u)
TILE0, _n = {}, 0
for _name, _u, _w in STREAMS:
    TILE0[_name] = _n
    _n += TILES[_name]

VEC, _n = {}, 0
for _name, _w in [("mix_pre0", 8), ("mix_post0", 8), ("ffn_pre0", 8), ("ffn_post0", 8),
                  ("mix_pre1", 8), ("mix_post1", 8), ("ffn_pre1", 8), ("ffn_post1", 8),
                  ("mix2", 8), ("mlp2", 8), ("final", 8), ("q_norm", 3), ("kv_norm", 2),
                  ("conv0", 4 * FF_T), ("conv1", 4 * FF_T), ("dn_conv", 4 * 24), ("dn_norm", 1),
                  ("subln", 1), ("b_forget", 1), ("a_log", 8), ("dt_bias", 8), ("lam", 256)]:
    VEC[_name] = _n
    _n += _w
NVEC = _n


class Events:

    def __init__(self, nc, ctx, known):
        self.nc, self.ctx, self.known = nc, ctx, known
        self.sems, self.count, self.found, self.open = {}, {}, {}, None

    def sem(self, name):
        if name not in self.sems:
            self.sems[name] = self.ctx.enter_context(self.nc.semaphore(name))
            self.count[name] = 0
        return self.sems[name]

    def tick(self, name, event=None, by=1):
        s = self.sem(name)
        self.count[name] += by
        if event is not None:
            assert event not in self.found, event
            self.found[event] = (name, self.count[name], 0)
            if self.open is not None:
                self.open.append(event)
        return s, by

    def at(self, event, i=None):
        if self.known is None:
            return self.sem("first_build"), 1
        name, value, stride = self.known[event]
        if i is None:
            return self.sem(name), value
        return self.sem(name), i * stride + value

    @contextmanager
    def loop(self, eng, n):
        before, self.open = dict(self.count), []
        with eng.Fori(0, n) as i:
            yield i
        for name, c in self.count.items():
            per = c - before.get(name, 0)
            self.count[name] = before.get(name, 0) + n * per
            for e in self.open:
                if self.found[e][0] == name:
                    self.found[e] = (name, self.found[e][1], per)
        self.open = None


def build(nc, dram, known):
    ctx = ExitStack()
    with ctx:
        ev = Events(nc, ctx, known)
        tick, at = ev.tick, ev.at
        sem = ev.sem

        place = [((nc.sbuf_base + 63) // 64) * 64]

        def sb(name, shape, dt=F32, where=None):
            size = 4 * int(np.prod(shape[1:]))
            if where is None:
                where = place[0]
                place[0] += size
            assert where + size <= nc.sbuf_usable_end, (name, where + size - nc.sbuf_usable_end)
            return nc.alloc_sbuf_tensor_at(name, shape, dt, offset=where)

        x = sb("x", [P, KT, SEQ])
        h_at = place[0]
        hH = sb("hH", [P, KT, SEQ], F32R)
        hL = sb("hL", [P, KT, SEQ], F32R)
        raw = [sb(f"raw{s}", [P, SLOT]) for s in range(2)]
        wH = [sb(f"wH{s}", [P, SLOT], F32R) for s in range(2)]
        wL = [sb(f"wL{s}", [P, SLOT], F32R) for s in range(2)]
        y = sb("y", [P, KT, SEQ])
        const = sb("const", [P, 768])
        vec = sb("vec", [P, NVEC])
        sq = sb("sq", [P, 2, SEQ])
        ss = sb("ss", [P, SEQ])
        dg = sb("dg", [P, TT, P])
        small = sb("small", [P, 64])
        stat = sb("stat", [P, 64])
        base = place[0]
        ident, ones, window = const[:, 0:P], const[:, P:2 * P], const[:, 2 * P:]
        eps = small[:, 60:61]

        def stage(items):
            place[0] = base
            return [sb(*it) for it in items]

        xin, = stage([("xin", [P, TT, DM])])
        cqH, cqL, misc, rope, prob, gate_row = stage([
            ("cqH", [P, 5, SEQ], F32R), ("cqL", [P, 5, SEQ], F32R), ("misc", [P, SEQ]), ("rope", [P, 1056]),
            ("prob", [P, 2, 1280]), ("gate_row", [P, 64])])
        even2 = place[0]
        qF, kF, vF, cB = (sb(*it) for it in [("qF", [P, 4, SEQ]), ("kF", [P, 4, SEQ]), ("vF", [P, TT, 512]),
                                             ("cB", [P, H, SEQ])])
        place[0] = even2
        qM, kM, vM = (sb(*it) for it in [("qM", [P, H, SEQ]), ("kM", [P, H, SEQ]), ("vM", [P, TT, 512])])
        mH, mL, ft = stage([("mH", [P, MLP_GROUP, SEQ], F32R), ("mL", [P, MLP_GROUP, SEQ], F32R), ("ft", [P, 6, SEQ])])
        qO, kO, vO, dist, alibi, probO, lamt = stage([
            ("qO", [P, H, SEQ]), ("kO", [P, H, SEQ]), ("vO", [P, TT, DM]), ("dist", [P, SEQ]),
            ("alibi", [P, 2, SEQ]), ("probO", [P, 2, 2, 1280]), ("lamt", [P, 128])])
        qkv, zT, S, vN, dconst, wba, tok = stage([
            ("qkv", [P, 24, SEQ]), ("zT", [P, H, SEQ]), ("S", [P, H, P]), ("vN", [P, H, P]),
            ("dconst", [P, 8 * P]), ("wba", [P, P]), ("tok", [P, 16, 32])])
        wbaH, wbaL = sb("wbaH", [P, P], F32R), sb("wbaL", [P, P], F32R)
        rowsT, gl, zed = sb("rowsT", [P, P]), sb("gl", [P, H, 8]), sb("zed", [P, 4, 16])
        attnT = sb("attnT", [P, H, SEQ], F32, h_at)
        kdec = sb("kdec", [P, H, SEQ], F32, h_at + 4 * KT * SEQ)
        PT = y[:].rearrange("p (a j) n -> p a j n", a=2)

        bank = [ctx.enter_context(nc.psum_tensor(f"bank{b}", [P, 512], F32)) for b in range(8)]

        w_in = [sem(f"weights_loaded{s}") for s in range(2)]
        w_hi, w_split = sem("weights_hi"), sem("weights_split")
        mm_done, evac = sem("tile_done"), sem("tile_evacuated")
        block = ctx.enter_context(nc.Block())

        def v(name, k=0, n=1):
            return vec[:, VEC[name] + k:VEC[name] + k + n]

        def vr(name, i, n=1):
            return vec[:, bass.ds(i + VEC[name], n)]

        def ptile(h, i, buf):
            o = P * (i * (i + 1) // 2)
            return buf[:, o:o + P * (i + 1)]

        def looped(name, per):
            return NUNITS[name] // per

        def tmp(p):
            names = ["lt", "y", "x", "t1", "r", "e"]
            slots = [y[:, k, :] for k in range(KT)] + [sq[:, k, :] for k in range(2)] + [dg[:].rearrange("p t n -> p (t n)"), ss[:]]
            return {n: slots[6 * p + k] for k, n in enumerate(names)}

        @block.sync
        def _(sp):
            for k, (dst, src) in enumerate([(xin[:], "x"), (const[:], "const"), (vec[:], "vec")]):
                sp.dma_start(dst, dram[src]).then_inc(*tick(f"loaded_{src}", f"in.{src}", 16))

            def load(name, n, j, s):
                w = WIDTH[name]
                sp.dma_start(raw[s][:, 0:w].unsqueeze(1),
                             dram[name].rearrange("u p c -> p u c")[:, bass.ds(j, 1), :]).then_inc(w_in[s], 16)

            for name, units, _w in STREAMS:
                n0 = UNIT0[name]
                if name.startswith("even_") and name != "even_out":
                    for j in range(units):
                        n = n0 + j
                        if n >= 2:
                            sp.wait_ge(w_split, n - 1)
                        load(name, n, j, n % 2)
                else:
                    with sp.Fori(0, units // 2) as i:
                        for s in range(2):
                            sp.wait_ge(w_split, i * 2 + (n0 + s - 1))
                            load(name, n0 + s, i * 2 + s, s)
            for t in range(TT):
                sp.wait_ge(*at(f"out.copied{t}"))
                sp.dma_start(dram["out"][t * P:(t + 1) * P, :], xin[:, t, :]).then_inc(*tick("stored", f"out.stored{t}", 16))
            sp.wait_ge(*at(f"out.stored{TT - 1}"))

        @block.tensor
        def _(pe):
            mm = nc.tensor.matmul

            def three(out, w, xv, first, last, swap=False):
                (a, b), (c, d) = (xv, w) if swap else (w, xv)
                mm(out, a, c, start=first, stop=False)
                mm(out, a, d, start=False, stop=False)
                return mm(out, b, c, start=False, stop=last)

            def tile_wait(name, l):
                pe.wait_ge(evac, l + (TILE0[name] - 3))

            def begin(name):
                if TILE0[name]:
                    pe.wait_ge(evac, TILE0[name])

            def unit_tiles(s, kt, aH, aL, b0, tiles=2, cols=256, wait=None, k0=0):
                for tl in range(tiles):
                    if wait is not None:
                        wait(tl)
                    for k in range(kt):
                        c = slice(k * cols + tl * P, k * cols + tl * P + P)
                        last = three(bank[b0 + tl][:], (wH[s][:, c], wL[s][:, c]),
                                     (aH[:, k0 + k, :], aL[:, k0 + k, :]), k == 0, k == kt - 1)
                    last.then_inc(mm_done, 1)

            def stream2(name, aH=hH, aL=hL, more=None):
                n0 = UNIT0[name]
                begin(name)
                with ev.loop(pe, looped(name, 2)) as i:
                    for s in range(2):
                        pe.wait_ge(w_split, i * 2 + (n0 + s + 1))
                        unit_tiles(s, KT, aH, aL, 2 * s, wait=lambda tl: tile_wait(name, i * 4 + (2 * s + tl)))
                        if more is not None:
                            more(i, s)

            def stream_down(name, kt):
                n0 = UNIT0[name]
                begin(name)
                with ev.loop(pe, looped(name, 4)) as i:
                    for a in range(4):
                        pe.wait_ge(w_split, i * 4 + (n0 + a + 1))
                        tile_wait(name, i * 4 + a)
                        unit_tiles(a % 2, kt, mH, mL, a, tiles=1, cols=P)

            def unit_tokens(s, b0, l0, wait):
                for t in range(TT):
                    wait(l0 + t)
                    for k in range(KT):
                        c = slice(k * 256, k * 256 + 256)
                        last = three(bank[(b0 + t) % 4][:, 0:256], (wH[s][:, c], wL[s][:, c]),
                                     (hH[:, k, t * P:(t + 1) * P], hL[:, k, t * P:(t + 1) * P]),
                                     k == 0, k == KT - 1, swap=True)
                    last.then_inc(mm_done, 1)

            def sums(tag, k, col, first, ticked):
                pe.wait_ge(*at(f"{tag}.sq{k}"))
                for t in range(TT):
                    last = mm(bank[7][:, col + t:col + t + 1], sq[:, k % 2, t * P:(t + 1) * P], ones[:, 0:1],
                              start=first and t == 0, stop=ticked, skip_group_check=True)
                last.then_inc(*tick("sums_pe", f"{tag}.sum{k}"))

            def spread(tag, b=6):
                pe.wait_ge(*at(f"{tag}.diag"))
                mm(bank[b][:], ones, dg[:].rearrange("p t n -> p (t n)"), start=True, stop=True)\
                    .then_inc(*tick("spread_pe", f"{tag}.spread"))

            def norm_tiles(tag, kt):
                for k in range(kt):
                    sums(tag, k, 0, k == 0, k == kt - 1)
                spread(tag)

            def norm_summed(tag, name, per):
                pe.wait_ge(*at(f"{name}.tile3.ss", looped(name, per) - 1))
                for t in range(TT):
                    last = mm(bank[7][:, t:t + 1], ss[:, t * P:(t + 1) * P], ones[:, 0:1], start=True, stop=True)
                last.then_inc(*tick("sums_pe", f"{tag}.sum{KT - 1}"))
                spread(tag)

            def attention(name, q, k, val, pbuf, W, masked, rows, M):
                def scores(h):
                    for i in range(TT):
                        for w in range(W):
                            j = (h * TT + i) * W + w
                            if j >= 4:
                                pe.wait_ge(*at(f"{name}.biased{j - 4}"))
                            n = P * (i + 1)
                            last = mm(bank[j % 4][:, 0:n], q(h, w)[:, i * P:n], k(h, w)[:, 0:n],
                                      start=True, stop=not masked)
                            if masked:
                                last = mm(bank[j % 4][:, i * P:n], ident, window[:, FAR:], start=False, stop=True)
                            last.then_inc(*tick(f"{name}_pe", f"{name}.scores{j}"))

                def turn(h):
                    for i in range(TT):
                        ti = h * TT + i
                        pe.wait_ge(*at(f"{name}.prob{h}.{i}"))
                        if ti >= 2:
                            pe.wait_ge(*at(f"{name}.copied{ti - 2}"))
                        for j in range(i + 1):
                            last = nc.tensor.transpose(bank[4 + ti % 2][:, j * P:(j + 1) * P],
                                                       ptile(h, i, pbuf(h, 0))[:, j * P:(j + 1) * P], ident)
                        last.then_inc(*tick(f"{name}_pe", f"{name}.turned{ti}"))

                def values(h):
                    pe.wait_ge(*at(f"{name}.copied{h * TT + TT - 1}"))
                    if h >= 2:
                        pe.wait_ge(*at(f"{name}.out{h - 2}"))
                    for j in range(TT):
                        last = mm(bank[6 + h % 2][rows(h), j * P:], val(h, j), PT[:, h % 2, j, j * P:],
                                  start=j == 0, stop=j == TT - 1)
                    last.then_inc(*tick(f"{name}_pe", f"{name}.values{h}"))

                scores(0)
                scores(1)
                for h in range(H):
                    turn(h)
                    if h + 2 < H:
                        scores(h + 2)
                    values(h)

            pe.wait_ge(*at("in.x"))
            pe.wait_ge(*at("in.const"))
            for k in range(KT):
                if k >= 4:
                    pe.wait_ge(*at(f"x0.{k - 4}"))
                for t in range(TT):
                    last = nc.tensor.transpose(bank[k % 4][:, t * P:(t + 1) * P], xin[:, t, k * P:(k + 1) * P], ident)
                last.then_inc(*tick("input_pe", f"x0.turned{k}"))
            norm_tiles("mix_pre0", KT)

            pe.wait_ge(*at(f"mix_pre0.h{KT - 1}"))
            pe.wait_ge(*at(f"x0.{KT - 1}"))
            for u in range(7):
                pe.wait_ge(w_split, u + 1)
                b0 = 2 * (u % 2)

                def wait(tl):
                    if 2 * u + tl >= 4:
                        pe.wait_ge(evac, 2 * u + tl - 3)
                unit_tiles(u % 2, KT, hH, hL, b0, wait=wait)
                if u == 3:
                    for k in range(3):
                        sums("cq", k, 0, k == 0, k == 2)
                    for k in range(3, 5):
                        sums("cq", k, 4, k == 3, k == 4)
                if u == 5:
                    pe.wait_ge(*at("cq.diag"))
                    mm(bank[6][:], ones, dg[:].rearrange("p t n -> p (t n)"), start=True, stop=True)\
                        .then_inc(*tick("spread_pe", "cq.spread"))
                    pe.wait_ge(*at("ckv.diag"))
                    mm(bank[5][:], ones, ss[:], start=True, stop=True).then_inc(*tick("spread_pe", "ckv.spread"))
            for c in range(2):
                u = 7 + c
                pe.wait_ge(w_split, u + 1)
                unit_tokens(u % 2, 2, 14 + 4 * c, lambda l: pe.wait_ge(evac, l - 3))
            pe.wait_ge(*at("gate.rows"))
            pe.wait_ge(*at("cq.h4"))
            for h in range(H):
                if h >= 4:
                    pe.wait_ge(*at(f"gate.bias{h - 4}"))
                mm(bank[4 + h % 4][:], ident[0:H, h:h + 1].to_broadcast([H, P]), prob[0:H, 1, 512:1024],
                   start=True, stop=True).then_inc(*tick("gate_pe", f"gate.spread{h}"))
            pe.wait_ge(evac, TILE0["even_uq"])
            pe.wait_ge(*at(f"gate.bias{H - 1}"))

            def half(h):
                return slice(64 * (h % 2), 64 * (h % 2) + 64)
            attention("fox", lambda h, w: qF[half(h), h // 2, :], lambda h, w: kF[half(h), h // 2, :],
                      lambda h, j: vF[:, j, 64 * h:64 * h + 64], lambda h, w: prob[:, h % 2, :], 1, True, half, 64)

            pe.wait_ge(*at(f"fox.out{H - 1}"))
            for u in range(2):
                n = UNIT0["even_uq"] + u
                pe.wait_ge(w_split, n + 1)
                for hh in range(4):
                    l = 4 * u + hh
                    if l >= 4:
                        tile_wait("even_uq", l)
                    for k in range(3):
                        c = slice(k * 384 + hh * 96, k * 384 + hh * 96 + 96)
                        last = three(bank[l % 4][0:96, :], (wH[n % 2][:, c], wL[n % 2][:, c]),
                                     (cqH[:, k, :], cqL[:, k, :]), k == 0, k == 2)
                    last.then_inc(mm_done, 1)
            for r in range(H + 1):
                if r == 0:
                    pe.wait_ge(*at("in.rope"))
                    src = misc[0:96, :]
                else:
                    pe.wait_ge(evac, TILE0["even_uq"] + r)
                    src = qM[0:96, r - 1, :]
                if r >= 2:
                    pe.wait_ge(*at(f"rope.sin{r - 2}"))
                mm(bank[4 + r % 2][64:96, :], rope[0:96, 1024:1056], src, start=True, stop=True)\
                    .then_inc(*tick("rope_pe", f"rope.turned{r}"))
            n = UNIT0["even_ukv"]
            pe.wait_ge(w_split, n + 1)
            for h in range(H):
                tile_wait("even_ukv", h)
                for k in range(2):
                    c = slice(k * DM + h * P, k * DM + h * P + P)
                    last = three(bank[h % 4][:], (wH[n % 2][:, c], wL[n % 2][:, c]),
                                 (cqH[:, 3 + k, :], cqL[:, 3 + k, :]), k == 0, k == 1)
                last.then_inc(mm_done, 1)
            for t in range(TT):
                tile_wait("even_ukv", H + t)
                for k in range(2):
                    c = slice(k * DM, (k + 1) * DM)
                    wv = [w[n % 2][:, c].rearrange("p (h d) -> p h d", h=H)[:, :, 64:] for w in (wH, wL)]
                    tk = slice(t * P, (t + 1) * P)
                    last = three(bank[t % 4][:], wv, (cqH[:, 3 + k, tk], cqL[:, 3 + k, tk]), k == 0, k == 1, swap=True)
                last.then_inc(mm_done, 1)
            pe.wait_ge(evac, TILE0["even_out"])
            pe.wait_ge(*at("rope.k"))
            pe.wait_ge(*at(f"rope.q{H - 1}"))
            attention("mla", lambda h, w: qM[0:96, h, :], lambda h, w: kM[0:96, h, :],
                      lambda h, j: vM[:, j, 64 * h:64 * h + 64], lambda h, w: prob[:, h % 2, :], 1, False, half, 64)
            pe.wait_ge(*at(f"mla.out{H - 1}"))
            stream2("even_out")

            def ffn(l):
                norm_summed(f"mix_post{l}", "even_out" if l == 0 else "odd_out", 2)
                norm_tiles(f"ffn_pre{l}", KT)
                pe.wait_ge(*at(f"ffn_pre{l}.h{KT - 1}"))
                for g in range(2):
                    stream2(f"ffn{l}_up{g}")
                    pe.wait_ge(*at(f"ffn{l}_up{g}.lo1", looped(f"ffn{l}_up{g}", 2) - 1))
                    stream_down(f"ffn{l}_down{g}", FF_GROUPS[g])
                norm_summed(f"ffn_post{l}", f"ffn{l}_down1", 4)

            ffn(0)

            norm_tiles("mix_pre1", KT)
            pe.wait_ge(*at(f"mix_pre1.h{KT - 1}"))
            stream2("odd_q")
            stream2("odd_k")
            begin("odd_v")
            n0 = UNIT0["odd_v"]
            with ev.loop(pe, looped("odd_v", 2)) as i:
                for s in range(2):
                    pe.wait_ge(w_split, i * 2 + (n0 + s + 1))
                    unit_tokens(s, 0, 4 * s, lambda l: tile_wait("odd_v", i * 8 + l))
            begin("odd_out")

            def two(w):
                return slice(64 * w, 64 * w + 64)
            attention("diff", lambda h, w: qO[two(w), h, :], lambda h, w: kO[two(w), h, :],
                      lambda h, j: vO[:, j, P * h:P * h + P], lambda h, w: probO[:, h % 2, w, :], 2, False,
                      lambda h: slice(0, P), P)
            pe.wait_ge(*at(f"diff.out{H - 1}"))
            for h in range(H):
                sums("subln", h, 4 * h, True, True)
            for h in range(H):
                pe.wait_ge(*at(f"subln.diag{h}"))
                mm(bank[4 + h % 2][:], ones, y[:, h % 2, :], start=True, stop=True)\
                    .then_inc(*tick("spread_pe", f"subln.spread{h}"))
            pe.wait_ge(*at(f"subln.h{H - 1}"))
            stream2("odd_out")
            ffn(1)

            norm_tiles("mix2", KT)
            pe.wait_ge(*at(f"mix2.h{KT - 1}"))
            pe.wait_ge(*at("dn.wba"))
            for t in range(TT):
                for k in range(KT):
                    c = slice(k * 16, k * 16 + 16)
                    last = three(bank[5][:, 16 * t:16 * t + 16], (wbaH[:, c], wbaL[:, c]),
                                 (hH[:, k, t * P:(t + 1) * P], hL[:, k, t * P:(t + 1) * P]),
                                 k == 0, k == KT - 1, swap=True)
            last.then_inc(*tick("dn_pe", "dn.ba"))
            stream2("dn_qkv")
            pe.wait_ge(*at("dn.g"))
            mm(bank[4][:, 0:32], dconst[:, 0:P], tok[:, 1, :], start=True, stop=True)
            mm(bank[4][:, 32:64], dconst[:, P:2 * P], tok[:, 1, :], start=True, stop=True)\
                .then_inc(*tick("dn_pe", "dn.gc"))

            def key_norms(i, s):
                for a in range(4):
                    pe.wait_ge(*at(f"dn.sq{s}.{a}", i))
                    for t in range(TT):
                        last = mm(bank[7][:, bass.ds(i * 32 + (16 * s + 4 * a + t), 1)],
                                  sq[:, a % 2, t * P:(t + 1) * P], ones[:, 0:1], start=True, stop=True)
                    last.then_inc(*tick("sums_pe", f"dn.sum{s}.{a}"))
            stream2("dn_z", more=key_norms)
            pe.wait_ge(evac, TILE0["dn_out"])
            pe.wait_ge(*at("dn.rowset"))
            nc.tensor.transpose(bank[4][0:96, 0:P], tok[:, 8:11, :].rearrange("p a b -> p (a b)"), ident)\
                .then_inc(*tick("dn_pe", "dn.rows_turned"))
            pe.wait_ge(*at("dn.rows"))
            for h0 in range(0, H, 2):
                pair = [(h0 + p, [bank[4 * p + b] for b in range(4)], tmp(p)) for p in range(2)]
                for h, b, m in pair:
                    if h >= 2:
                        pe.wait_ge(*at(f"dn.w{h - 2}"))
                    for kind in range(3):
                        for t in range(TT):
                            r = 32 * kind + 4 * h + t
                            last = mm(b[kind][:, t * P:(t + 1) * P], ident[0:96, r:r + 1].to_broadcast([96, P]),
                                      rowsT[0:96, :], start=True, stop=True)
                    last.then_inc(*tick("dn_pe", f"dn.spread{h}"))
                for h, b, m in pair:
                    pe.wait_ge(*at(f"dn.qn{h}"))
                    for t in range(TT):
                        c = slice(t * P, (t + 1) * P)
                        mm(b[0][:, c], qkv[:, 8 + h, c], m["t1"][:, c], start=True, stop=True)
                        mm(b[1][:, c], qkv[:, 8 + h, c], m["x"][:, c], start=True, stop=True)
                    pe.wait_ge(*at(f"dn.diff{h}"))
                    pe.wait_ge(*at(f"dn.e{h}"))
                    for t in range(TT):
                        c = slice(t * P, (t + 1) * P)
                        nc.tensor.transpose(b[3][:, c], qkv[:, 8 + h, c], ident)
                        last = nc.tensor.transpose(b[2][:, c], qkv[:, 16 + h, c], ident)
                    last.then_inc(*tick("dn_pe", f"dn.gram{h}"))
                for h, b, m in pair:
                    pe.wait_ge(*at(f"dn.y{h}.0"))
                    for t in range(TT):
                        c = slice(t * P, (t + 1) * P)
                        last = nc.tensor.transpose(b[0][:, c], m["y"][:, c], ident)
                    last.then_inc(*tick("dn_pe", f"dn.xt{h}"))
                for s in range(1, 6):
                    for h, b, m in pair:
                        pe.wait_ge(*at(f"dn.x{h}.{s - 1}"))
                        if s == 1:
                            pe.wait_ge(*at(f"dn.attn{h}"))
                        for t in range(TT):
                            c = slice(t * P, (t + 1) * P)
                            last = mm(b[1][:, c], m["lt"][:, c], m["x"][:, c], start=True, stop=True)
                        last.then_inc(*tick("dn_pe", f"dn.lx{h}.{s}"))
                    for h, b, m in pair:
                        pe.wait_ge(*at(f"dn.t{h}.{s}"))
                        if s == 1:
                            pe.wait_ge(*at(f"dn.tok{h}"))
                        for t in range(TT):
                            c = slice(t * P, (t + 1) * P)
                            if s < 5:
                                mm(b[2][:, c], m["y"][:, c], m["t1"][:, c], start=True, stop=True)
                            last = mm(b[3][:, c], m["t1"][:, c], m["y"][:, c], start=True, stop=True)
                        last.then_inc(*tick("dn_pe", f"dn.xx{h}.{s}"))
                for h, b, m in pair:
                    pe.wait_ge(*at(f"dn.y{h}.5"))
                    for t in range(TT):
                        c = slice(t * P, (t + 1) * P)
                        mm(b[0][:, c], m["y"][:, c], qkv[:, 16 + h, c], start=True, stop=True)
                        last = mm(b[1][:, c], m["r"][:, c], m["y"][:, c], start=True, stop=True)
                    last.then_inc(*tick("dn_pe", f"dn.uw{h}"))
            pe.wait_ge(*at(f"dn.w{H - 2}"))
            pe.wait_ge(*at(f"dn.w{H - 1}"))
            for n in range(8):
                t, r = n // 2, slice(64 * (n % 2), 64 * (n % 2) + 64)
                ck = slice(64 * n, 64 * n + 64)
                for g in range(2):
                    pe.wait_ge(*at(f"scan.state{n - 1}.{g}"))
                    for hh in range(4):
                        h = 4 * g + hh
                        last = mm(bank[g][r, hh * P:(hh + 1) * P], qkv[:, 8 + h, ck], S[:, h, :], start=True, stop=True)
                    last.then_inc(*tick("scan_pe", f"scan.ws{n}.{g}"))
                if n >= 2:
                    pe.wait_ge(*at(f"scan.o{n - 2}"))
                for h in range(H):
                    mm(bank[4 + n % 2][:, 64 * h:64 * h + 64], S[:, h, :], qkv[:, h, ck],
                       start=h == 0, stop=False, skip_group_check=True)
                for g in range(2):
                    pe.wait_ge(*at(f"scan.vn{n}.{g}"))
                    for hh in range(4):
                        h = 4 * g + hh
                        mm(bank[4 + n % 2][:, 64 * h:64 * h + 64], vN[r, h, :],
                           attnT[r, h, t * P + r.start:t * P + r.stop], start=False, stop=True, skip_group_check=True)
                        last = mm(bank[2 + g][:, hh * P:(hh + 1) * P], kdec[r, h, t * P:(t + 1) * P], vN[r, h, :],
                                  start=True, stop=True)
                    last.then_inc(*tick("scan_pe", f"scan.kv{n}.{g}"))
            for h in range(H):
                sums("gated", h, 4 * h, True, True)
            for h in range(H):
                pe.wait_ge(*at(f"gated.diag{h}"))
                mm(bank[4 + h % 2][:], ones, y[:, h % 2, :], start=True, stop=True)\
                    .then_inc(*tick("spread_pe", f"gated.spread{h}"))
            pe.wait_ge(*at(f"gated.h{H - 1}"))
            stream2("dn_out")
            norm_summed("mlp2", "dn_out", 2)
            pe.wait_ge(*at(f"mlp2.h{KT - 1}"))
            for g in range(2):
                stream2(f"mlp_up{g}")
                pe.wait_ge(*at(f"mlp_up{g}.lo3", looped(f"mlp_up{g}", 2) - 1))
                stream_down(f"mlp_down{g}", MLP_GROUP)
            stream_down("mlp_down2", MLP_GROUP)
            norm_summed("final", "mlp_down2", 4)
            for t in range(TT):
                for half_ in range(2):
                    b = (2 * t + half_) % 4
                    if t >= 2:
                        pe.wait_ge(*at(f"out.copied{t - 2}"))
                    for kk in range(4):
                        k = 4 * half_ + kk
                        if t == 0:
                            pe.wait_ge(*at(f"final.t{k}"))
                        last = nc.tensor.transpose(bank[b][:, kk * P:(kk + 1) * P], y[:, k, t * P:(t + 1) * P], ident)
                    last.then_inc(*tick("out_pe", f"out.turned{t}.{half_}"))

        @block.scalar
        def _(act):
            def a(out, in_, func, **kw):
                return nc.scalar.activation(out, in_, func, **kw)

            def hi(n, half_n, s):
                act.wait_ge(w_in[s], half_n * 16 + 16)
                a(wH[s][:], raw[s][:], ACT.Copy).then_inc(w_hi, 1)

            def hi_next(name, i, s, per=2, last=False):
                n0 = UNIT0[name] + s
                if last:
                    return
                each = TILES[name] // NUNITS[name]
                act.wait_ge(mm_done, i * (per * each) + (TILE0[name] + s * each))
                hi(None, i * (per // 2) + (n0 + 1) // 2, (n0 + 1) % 2)

            def done(name, l):
                act.wait_ge(mm_done, l + (TILE0[name] + 1))

            def evacuated(name, l):
                act.wait_ge(evac, l + (TILE0[name] + 1))

            def squares(tag, k, src, ready=None):
                if ready is not None:
                    act.wait_ge(*at(ready))
                if k >= 2:
                    act.wait_ge(*at(f"{tag}.sum{k - 2}"))
                a(sq[:, k % 2, :], src, ACT.Square).then_inc(*tick("squares_act", f"{tag}.sq{k}"))

            def root(tag, kt, n, col=0, w=TT, out=0):
                act.wait_ge(*at(f"{tag}.sum{kt - 1}"))
                return a(small[:, out:out + w], bank[7][:, col:col + w], ACT.Sqrt, bias=eps, scale=1.0 / n)

            def his(tag, kt, H_=hH, slots=4, src=lambda k: y[:, k % 4, :], k0=0):
                for k in range(kt):
                    act.wait_ge(*at(f"{tag}.t{k0 + k}"))
                    a(H_[:, k0 + k, :], src(k), ACT.Copy).then_inc(*tick("norm_act", f"{tag}.hi{k0 + k}"))

            def norm_tiles(tag, src_ready):
                for k in range(KT):
                    squares(tag, k, x[:, k, :], src_ready(k))
                root(tag, KT, DM).then_inc(*tick("norm_act", f"{tag}.root"))
                his(tag, KT)

            def stream_plain(name, dst):
                with ev.loop(act, looped(name, 2)) as i:
                    for s in range(2):
                        hi_next(name, i, s)
                        for tl in range(2):
                            done(name, i * 4 + (2 * s + tl))
                            dst(i, 2 * s + tl, bank[2 * s + tl]).then_inc(evac, 1)

            def tile_out(name, i, a_, mode, t0=0):
                tag = f"{name}.tile{a_}"
                yt = y[:, bass.ds(i * 4 + (a_ + t0), 1), :]
                xt = x[:, bass.ds(i * 4 + (a_ + t0), 1), :]
                if mode == "y0":
                    done(name, i * 4 + a_)
                    a(yt, bank[a_][:].unsqueeze(1), ACT.Copy).then_inc(evac, 1)
                    return
                if mode == "x0":
                    return
                if mode == "y":
                    done(name, i * 4 + a_)
                    src = bank[a_][:].unsqueeze(1)
                else:
                    evacuated(name, i * 4 + a_)
                    src = yt if mode == "y1" else xt
                act.wait_ge(*(at(f"{name}.tile{a_ - 2}.ss", i) if a_ >= 2 else at(f"{name}.tile{a_ + 2}.ss", i - 1)))
                a(sq[:, a_ % 2, :].unsqueeze(1), src, ACT.Square).then_inc(*tick("out_act", f"{tag}.sq"))
                if mode == "y":
                    a(yt, src, ACT.Copy).then_inc(evac, 1)

            def stream_out2(name, mode):
                with ev.loop(act, looped(name, 2)) as i:
                    for s in range(2):
                        hi_next(name, i, s)
                        for tl in range(2):
                            tile_out(name, i, 2 * s + tl, mode)

            def stream_down(name, mode, last=False, t0=0):
                with ev.loop(act, looped(name, 4)) as i:
                    for a_ in range(4):
                        hi_next(name, i, a_, per=4, last=last and a_ == 3)
                        tile_out(name, i, a_, mode, t0)

            def attention(name, pbuf, W, out_rows, out_tile, diff=False):
                def exps(h):
                    act.wait_ge(*at(f"{name}.minus_max{h}"))
                    for i in range(TT):
                        for w in range(W):
                            p_ = ptile(h, i, pbuf(h, w))
                            c = 16 * (h % 2) + 4 * w + i
                            a(p_, p_, ACT.Exp, bias=small[:, c:c + 1], accum_out=small[:, c + 32:c + 33])\
                                .then_inc(*tick(f"{name}_act", f"{name}.exp{h}.{i}.{w}"))

                def copies(h):
                    for i in range(TT):
                        ti = h * TT + i
                        act.wait_ge(*at(f"{name}.turned{ti}"))
                        if h >= 2:
                            act.wait_ge(*at(f"{name}.values{h - 2}"))
                        a(PT[:, h % 2, 0:i + 1, i * P:(i + 1) * P],
                          bank[4 + ti % 2][:, 0:P * (i + 1)].rearrange("p (j n) -> p j n", n=P), ACT.Copy)\
                            .then_inc(*tick(f"{name}_act", f"{name}.copied{ti}"))

                def out(h):
                    act.wait_ge(*at(f"{name}.values{h}"))
                    if diff:
                        a(qO[:, h, :], bank[6 + h % 2][:], ACT.Copy).then_inc(*tick(f"{name}_act", f"{name}.out{h}"))
                    else:
                        r = out_rows(h)
                        a(hH[r, out_tile(h), :], bank[6 + h % 2][r, :], ACT.Copy)\
                            .then_inc(*tick(f"{name}_act", f"{name}.hi{h}"))

                exps(0)
                for h in range(H):
                    if h + 1 < H:
                        exps(h + 1)
                    copies(h)
                    if h >= 1:
                        out(h - 1)
                out(H - 1)

            act.wait_ge(*at("in.eps"))
            for k in range(KT):
                act.wait_ge(*at(f"x0.turned{k}"))
                a(x[:, k, :], bank[k % 4][:], ACT.Copy).then_inc(*tick("input_act", f"x0.{k}"))
            for n in range(2):
                hi(n, 0, n)
            norm_tiles("mix_pre0", lambda k: f"x0.{k}")

            act.dma_start(rope[:], dram["rope"]).then_inc(*tick("loaded_rope", "in.rope", 16))
            act.wait_ge(*at("in.vec"))

            def e_tile(l, dst, src, **kw):
                act.wait_ge(mm_done, l + 1)
                return a(dst, src, ACT.Copy, **kw).then_inc(evac, 1)

            for u in range(9):
                if u >= 1:
                    act.wait_ge(mm_done, 2 * u if u < 8 else 18)
                    hi(u + 1, (u + 1) // 2, (u + 1) % 2)
                if u == 0:
                    e_tile(0, misc[:], bank[0][:])
                    e_tile(1, y[:, 0, :], bank[1][:])
                elif u < 7:
                    for tl in range(2):
                        l = 2 * u + tl
                        b = bank[2 * (u % 2) + tl][:]
                        if u < 3:
                            e_tile(l, y[:, l - 1, :], b)
                        elif u < 5:
                            e_tile(l, qF[:, l - 6, :], b, scale=0.125)
                        else:
                            e_tile(l, kF[:, l - 10, :], b)
                else:
                    for t in range(TT):
                        e_tile(14 + 4 * (u - 7) + t, vF[:, t, 256 * (u - 7):256 * (u - 6)], bank[(2 + t) % 4][:, 0:256])
                if u == 2:
                    act.wait_ge(evac, 1)
                    a(prob[0:H, 0, 0:512], misc[0:H, :], ACT.Abs, bias=v("b_forget")[0:H, :])\
                        .then_inc(*tick("gate_act", "gate.abs"))
                    act.wait_ge(*at("gate.abs"))
                    a(prob[0:H, 0, 0:512], prob[0:H, 0, 0:512], ACT.Exp, scale=-1.0).then_inc(*tick("gate_act", "gate.exp"))
                    act.wait_ge(*at("gate.exp"))
                    a(prob[0:H, 0, 0:512], prob[0:H, 0, 0:512], ACT.Ln, bias=1.0).then_inc(*tick("gate_act", "gate.ln"))
                    act.wait_ge(evac, 6)
                    for k in range(2):
                        squares("cq", k, y[:, k, :])
                if u == 3:
                    for k in range(2, 5):
                        squares("cq", k, y[:, k, :])
                    root("cq", 5, 384)
                    root("cq", 5, 256, col=4, out=4).then_inc(*tick("norm_act", "cq.root"))
                if u == 6:
                    his("cq", 5, cqH, src=lambda k: y[:, k, :])
            for h in range(H):
                act.wait_ge(*at(f"gate.spread{h}"))
                a(cB[:, h, :], bank[4 + h % 4][:], ACT.Copy).then_inc(*tick("gate_act", f"gate.bias{h}"))

            def half(h):
                return slice(64 * (h % 2), 64 * (h % 2) + 64)
            attention("fox", lambda h, w: prob[:, h % 2, :], 1, half, lambda h: h // 2)
            for u in range(3):
                n = UNIT0["even_uq"] + u
                act.wait_ge(mm_done, TILE0["even_uq"] + 4 * u)
                hi(n + 1, (n + 1) // 2, (n + 1) % 2)
                if u < 2:
                    for hh in range(4):
                        h = 4 * u + hh
                        done("even_uq", h)
                        a(qM[0:96, h, :], bank[h % 4][0:96, :], ACT.Copy, scale=96.0 ** -0.5)\
                            .then_inc(evac, 1)
                else:
                    for h in range(H):
                        done("even_ukv", h)
                        a(kM[0:64, h, :], bank[h % 4][0:64, :], ACT.Copy).then_inc(evac, 1)
                    for t in range(TT):
                        done("even_ukv", H + t)
                        a(vM[:, t, :], bank[t % 4][:], ACT.Copy).then_inc(evac, 1)
            attention("mla", lambda h, w: prob[:, h % 2, :], 1, half, lambda h: 4 + h // 2)
            stream_out2("even_out", "y")

            def norm_summed(tag):
                root(tag, KT, DM).then_inc(*tick("norm_act", f"{tag}.root"))

            def ffn(l):
                norm_summed(f"mix_post{l}")
                norm_tiles(f"ffn_pre{l}", lambda k: f"mix_post{l}.x{k}")
                for g in range(2):
                    name = f"ffn{l}_up{g}"
                    m0 = FF_GROUPS[0] * g
                    with ev.loop(act, looped(name, 2)) as i:
                        for s in range(2):
                            hi_next(name, i, s)
                            m = i * 2 + (m0 + s)
                            done(name, i * 4 + 2 * s)
                            a(ft[:, s, :], bank[2 * s][:], ACT.Identity, bias=vr(f"conv{l}", m + 3 * FF_T),
                              scale=vr(f"conv{l}", m + 2 * FF_T)).then_inc(*tick(f"ffn_act", f"{name}.tap2.{s}"))
                            evacuated(name, i * 4 + 2 * s)
                            a(ft[:, 2 + s, :], ft[:, s, :], ACT.Gelu_apprx_tanh).then_inc(*tick("ffn_act", f"{name}.gelu{s}"))
                            evacuated(name, i * 4 + (2 * s + 1))
                            a(mH[:, bass.ds(i * 2 + s, 1), :], ft[:, 4 + s, :].unsqueeze(1), ACT.Copy)\
                                .then_inc(*tick("ffn_act", f"{name}.hi{s}"))
                    stream_down(f"ffn{l}_down{g}", "y0" if g == 0 else "y1")
                norm_summed(f"ffn_post{l}")

            ffn(0)

            norm_tiles("mix_pre1", lambda k: f"ffn_post0.x{k}")
            act.dma_start(dist[:], dram["dist"]).then_inc(*tick("loaded_dist", "in.dist", 16))
            act.wait_ge(*at("lam.dots"))
            a(lamt[:, 66:68], lamt[:, 64:66], ACT.Exp).then_inc(*tick("lam_act", "lam.exp"))
            stream_plain("odd_q", lambda i, a_, b: a(qO[:, bass.ds(i * 4 + a_, 1), :], b[:].unsqueeze(1), ACT.Copy, scale=0.125))
            stream_plain("odd_k", lambda i, a_, b: a(kO[:, bass.ds(i * 4 + a_, 1), :], b[:].unsqueeze(1), ACT.Copy))
            with ev.loop(act, looped("odd_v", 2)) as i:
                for s in range(2):
                    hi_next("odd_v", i, s)
                    for t in range(TT):
                        done("odd_v", i * 8 + (4 * s + t))
                        a(vO[:, t, bass.ds(i * 512 + 256 * s, 256)], bank[t][:, 0:256], ACT.Copy).then_inc(evac, 1)
            attention("diff", lambda h, w: probO[:, h % 2, w, :], 2, None, None, diff=True)
            for h in range(H):
                squares("subln", h, qO[:, h, :], f"diff.out{h}")
            root("subln", H, P, w=32).then_inc(*tick("norm_act", "subln.root"))
            his("subln", H, src=lambda k: y[:, 2 + k % 4, :])
            stream_out2("odd_out", "y")
            ffn(1)

            norm_tiles("mix2", lambda k: f"ffn_post1.x{k}")
            act.dma_start(dconst[:], dram["dconst"]).then_inc(*tick("loaded_dconst", "in.dconst", 16))
            act.dma_start(wba[:], dram["wba"]).then_inc(*tick("loaded_wba", "in.wba", 16))
            act.wait_ge(*at("in.wba"))
            a(wbaH[:], wba[:], ACT.Copy).then_inc(*tick("dn_act", "dn.wba_hi"))
            act.wait_ge(*at("dn.z"))
            ba = bank[5][:, 0:64].rearrange("p (t c) -> p t c", c=16)
            a(tok[:, 0, :].rearrange("p (h t) -> p t h", t=TT), ba[:, :, 0:8], ACT.Sigmoid).then_inc(*tick("dn_act", "dn.beta"))
            za = zed[:].rearrange("p t (w h) -> p t w h", w=2)
            a(za[:, :, 1, :], za[:, :, 0, :], ACT.Abs).then_inc(*tick("dn_act", "dn.abs"))
            act.wait_ge(*at("dn.abs"))
            a(za[:, :, 1, :], za[:, :, 1, :], ACT.Exp, scale=-1.0).then_inc(*tick("dn_act", "dn.expabs"))
            a(tok[:, 12, 0:8], v("a_log", 0, 8), ACT.Exp).then_inc(*tick("dn_act", "dn.expa"))
            act.wait_ge(*at("dn.expabs"))
            a(za[:, :, 1, :], za[:, :, 1, :], ACT.Ln, bias=1.0).then_inc(*tick("dn_act", "dn.ln"))
            with ev.loop(act, looped("dn_qkv", 2)) as i:
                for s in range(2):
                    hi_next("dn_qkv", i, s)
                    for tl in range(2):
                        c = 2 * s + tl
                        done("dn_qkv", i * 4 + c)
                        a(y[:, c, :], bank[c][:], ACT.Copy, scale=vr("dn_conv", i * 4 + (c + 72)))\
                            .then_inc(*tick("dn_conv_act", f"dn.tap3.{c}"))
                    for tl in range(2):
                        c = 2 * s + tl
                        evacuated("dn_qkv", i * 4 + c)
                        a(qkv[:, bass.ds(i * 4 + c, 1), :], y[:, c, :].unsqueeze(1), ACT.Silu)\
                            .then_inc(*tick("dn_conv_act", f"dn.silu{c}"))
            act.wait_ge(*at("dn.gc"))
            a(tok[:, 2, :], bank[4][:, 0:32], ACT.Copy).then_inc(*tick("dn_act", "dn.gc_copied"))
            a(tok[:, 3, :], bank[4][:, 32:64], ACT.Copy).then_inc(*tick("dn_act", "dn.tot_copied"))
            with ev.loop(act, looped("dn_z", 2)) as i:
                for s in range(2):
                    hi_next("dn_z", i, s)
                    for tl in range(2):
                        c = 2 * s + tl
                        done("dn_z", i * 4 + c)
                        a(zT[:, bass.ds(i * 4 + c, 1), :], bank[c][:].unsqueeze(1), ACT.Silu).then_inc(evac, 1)
                    for a_ in range(4):
                        k = 4 * s + a_
                        before = (k - 2) % 8
                        act.wait_ge(*at(f"dn.sum{before // 4}.{before % 4}", i if k >= 2 else i - 1))
                        a(sq[:, a_ % 2, :].unsqueeze(1), qkv[:, bass.ds(i * 8 + k, 1), :], ACT.Square)\
                            .then_inc(*tick("dn_sq_act", f"dn.sq{s}.{a_}"))
            act.wait_ge(*at("dn.sum1.3", looped("dn_z", 2) - 1))
            a(tok[:, 14:16, :].rearrange("p a b -> p (a b)"), bank[7][:, 0:64], ACT.Sqrt, bias=eps)\
                .then_inc(*tick("dn_act", "dn.root"))
            a(tok[:, 4, :], tok[:, 2, :], ACT.Exp).then_inc(*tick("dn_act", "dn.egc"))
            act.wait_ge(*at("dn.left"))
            a(tok[:, 5, :], tok[:, 5, :], ACT.Exp).then_inc(*tick("dn_act", "dn.eleft"))
            act.wait_ge(*at("dn.rows_turned"))
            a(rowsT[0:96, :], bank[4][0:96, 0:P], ACT.Copy).then_inc(*tick("dn_act", "dn.rows"))
            for h0 in range(0, H, 2):
                pair = [(h0 + p, [bank[4 * p + b] for b in range(4)], tmp(p)) for p in range(2)]
                for h, b, m in pair:
                    act.wait_ge(*at(f"dn.spread{h}"))
                    if h >= 2:
                        act.wait_ge(*at(f"dn.qdec{h - 2}"))
                    a(m["e"], b[2][:], ACT.Exp).then_inc(*tick("dn_act", f"dn.e{h}"))
                    act.wait_ge(*at(f"dn.diff{h}"))
                    a(m["lt"], m["lt"], ACT.Exp).then_inc(*tick("dn_act", f"dn.dec{h}"))
                    act.wait_ge(*at(f"dn.e{h}"))
                    a(gl[:, h, :], m["e"][:, 63::64], ACT.Copy).then_inc(*tick("dn_act", f"dn.gl{h}"))
                for h, b, m in pair:
                    act.wait_ge(*at(f"dn.gram{h}"))
                    for t in range(TT):
                        c, r = slice(t * P, (t + 1) * P), 4 * h + t
                        a(m["r"][:, c], b[3][:, c], ACT.Copy, scale=tok[:, 6, r:r + 1])
                        a(kdec[:, h, c], b[3][:, c], ACT.Copy, scale=tok[:, 7, r:r + 1])
                        last = a(qkv[:, 16 + h, c], b[2][:, c], ACT.Copy, scale=tok[:, 0, r:r + 1])
                    last.then_inc(*tick("dn_act", f"dn.tok{h}"))
                for h, b, m in pair:
                    act.wait_ge(*at(f"dn.xt{h}"))
                    act.wait_ge(*at(f"dn.qdec{h}"))
                    a(m["x"], b[0][:], ACT.Copy).then_inc(*tick("dn_act", f"dn.x{h}.0"))
                for h, b, m in pair:
                    act.wait_ge(*at(f"dn.uw{h}"))
                    a(qkv[:, 16 + h, :], b[0][:], ACT.Copy)
                    a(qkv[:, 8 + h, :], b[1][:], ACT.Copy).then_inc(*tick("dn_act", f"dn.w{h}"))
            for n in range(8):
                act.wait_ge(*at(f"scan.kv{n}.1"))
                a(qkv[:, 0:H, 64 * n:64 * n + 64], bank[4 + n % 2][:].rearrange("p (h c) -> p h c", h=H), ACT.Copy)\
                    .then_inc(*tick("scan_act", f"scan.o{n}"))
            for h in range(H):
                squares("gated", h, qkv[:, h, :], "scan.o7")
            root("gated", H, P, w=32).then_inc(*tick("norm_act", "gated.root"))
            his("gated", H, src=lambda k: y[:, 4 + k % 4, :])
            stream_out2("dn_out", "x1")
            norm_summed("mlp2")
            his("mlp2", KT)
            for g in range(2):
                name = f"mlp_up{g}"
                with ev.loop(act, looped(name, 2)) as i:
                    for s in range(2):
                        hi_next(name, i, s)
                        for tl in range(2):
                            c = 2 * s + tl
                            done(name, i * 4 + c)
                            a(y[:, c, :], bank[c][:], ACT.Relu).then_inc(*tick("mlp_act", f"{name}.relu{c}"))
                            evacuated(name, i * 4 + c)
                            a(mH[:, bass.ds(i * 4 + c, 1), :], y[:, 4 + c, :].unsqueeze(1), ACT.Copy)\
                                .then_inc(*tick("mlp_act", f"{name}.hi{c}"))
                stream_down(f"mlp_down{g}", ("x0", "x1")[g])
            stream_down("mlp_down2", "x1", last=True, t0=4)
            norm_summed("final")
            for t in range(TT):
                act.wait_ge(*at(f"out.turned{t}.0"))
                a(xin[:, t, 0:512], bank[(2 * t) % 4][:], ACT.Copy)
                act.wait_ge(*at(f"out.turned{t}.1"))
                a(xin[:, t, 512:1024], bank[(2 * t + 1) % 4][:], ACT.Copy).then_inc(*tick("out_act", f"out.copied{t}"))

        @block.vector
        def _(dve):
            tt, ts, stt = nc.vector.tensor_tensor, nc.vector.tensor_scalar, nc.vector.scalar_tensor_tensor

            def chain(ins, name, event, i=None):
                ins.then_inc(*tick(name, event))
                dve.wait_ge(*at(event, i))

            def lo(n, s):
                dve.wait_ge(w_hi, n + 1)
                tt(wL[s][:], raw[s][:], wH[s][:].bitcast(F32), ALU.subtract).then_inc(w_split, 1)

            def lo_next(name, i, s, per=2, last=False):
                if not last:
                    n0 = UNIT0[name] + s
                    lo(i * per + (n0 + 1), (n0 + 1) % 2)

            def done(name, l):
                dve.wait_ge(mm_done, l + (TILE0[name] + 1))

            def diagonal(out, col):
                return tt(out.rearrange("p (t n) -> p t n", t=TT), ident.unsqueeze(1).to_broadcast([P, TT, P]),
                          stat[:, col:col + TT].unsqueeze(2).to_broadcast([P, TT, P]), ALU.mult)

            def inverse(tag):
                dve.wait_ge(*at(f"{tag}.root"))
                chain(nc.vector.reciprocal(stat[:, 0:TT], small[:, 0:TT]), "norm_dve", f"{tag}.inverse")
                diagonal(dg[:].rearrange("p t n -> p (t n)"), 0).then_inc(*tick("norm_dve", f"{tag}.diag"))
                dve.wait_ge(*at(f"{tag}.spread"))

            def lo_tile(tag, k, src, H_=hH, L_=hL):
                dve.wait_ge(*at(f"{tag}.hi{k}"))
                tt(L_[:, k, :], src, H_[:, k, :].bitcast(F32), ALU.subtract).then_inc(*tick("norm_dve", f"{tag}.h{k}"))

            def norm_pre(tag):
                inverse(tag)
                for k in range(KT + 1):
                    if k < KT:
                        stt(y[:, k % 4, :], x[:, k, :], v(tag, k), bank[6][:], ALU.mult, ALU.mult)\
                            .then_inc(*tick("norm_dve", f"{tag}.t{k}"))
                    if k >= 1:
                        lo_tile(tag, k - 1, y[:, (k - 1) % 4, :])

            def norm_post(tag):
                inverse(tag)
                for k in range(KT + 1):
                    if k < KT:
                        stt(y[:, k, :], y[:, k, :], v(tag, k), bank[6][:], ALU.mult, ALU.mult)\
                            .then_inc(*tick("norm_dve", f"{tag}.t{k}"))
                    if k % 2 == 1:
                        dve.wait_ge(*at(f"{tag}.t{k - 1}"))
                        tt(x[:, k - 1, :], x[:, k - 1, :], y[:, k - 1, :], ALU.add)\
                            .then_inc(*tick("norm_dve", f"{tag}.x{k - 1}"))

            def stream_plain(name):
                with ev.loop(dve, looped(name, 2)) as i:
                    for s in range(2):
                        lo_next(name, i, s)

            def clear_sums(name):
                for q in range(4):
                    last = nc.vector.memset(ss[:, q * P:(q + 1) * P], 0.0)
                    last.then_inc(*tick("sums_dve", f"{name}.clear{q}"))

            def tile_out(name, i, a_, mode, t0=0):
                tag = f"{name}.tile{a_}"
                if mode == "y0":
                    return
                if mode != "y":
                    done(name, i * 4 + a_)
                    dst = (x if mode[0] == "x" else y)[:, bass.ds(i * 4 + (a_ + t0), 1), :]
                    tt(dst, dst, bank[a_][:].unsqueeze(1), ALU.add).then_inc(evac, 1)
                    if mode == "x0":
                        return
                dve.wait_ge(*at(f"{tag}.sq", i))
                dve.wait_ge(*(at(f"{name}.tile{a_ - 1}.ss", i) if a_ else at(f"{name}.tile3.ss", i - 1)))
                tt(ss[:], ss[:], sq[:, a_ % 2, :], ALU.add).then_inc(*tick("sums_dve", f"{tag}.ss"))

            def stream_out2(name, mode):
                clear_sums(name)
                with ev.loop(dve, looped(name, 2)) as i:
                    for s in range(2):
                        lo_next(name, i, s)
                        for tl in range(2):
                            tile_out(name, i, 2 * s + tl, mode)

            def stream_down(name, mode, last=False, t0=0):
                if mode in ("y1", "x1") and t0 == 0:
                    clear_sums(name)
                with ev.loop(dve, looped(name, 4)) as i:
                    for a_ in range(4):
                        lo_next(name, i, a_, per=4, last=last and a_ == 3)
                        tile_out(name, i, a_, mode, t0)

            def attention(name, bias, pbuf, W, finish):
                def biased(h):
                    if name == "diff":
                        dve.wait_ge(*at(f"alibi{h}"))
                    for i in range(TT):
                        if h >= 2:
                            dve.wait_ge(*at(f"{name}.turned{(h - 2) * TT + i}"))
                        for w in range(W):
                            j = (h * TT + i) * W + w
                            n, c = P * (i + 1), 8 * (h % 2) + 4 * w + i
                            dve.wait_ge(*at(f"{name}.scores{j}"))
                            nc.vector.tensor_tensor_reduce(ptile(h, i, pbuf(h, w)), bank[j % 4][:, 0:n], bias(h, i), 1.0,
                                                           -3.0e38, ALU.add, ALU.max, stat[:, c:c + 1])\
                                .then_inc(*tick(f"{name}_dve", f"{name}.biased{j}"))
                    c = 16 * (h % 2)
                    dve.wait_ge(*at(f"{name}.biased{j}"))
                    if h >= 2:
                        dve.wait_ge(*at(f"{name}.exp{h - 2}.{TT - 1}.{W - 1}"))
                    ts(small[:, c:c + 4 * W], stat[:, c // 2:c // 2 + 4 * W], -1.0, None, ALU.mult)\
                        .then_inc(*tick(f"{name}_dve", f"{name}.minus_max{h}"))

                def divided(h):
                    c = 16 * (h % 2) + 32
                    q = 16 + 16 * (h % 2)
                    dve.wait_ge(*at(f"{name}.exp{h}.{TT - 1}.{W - 1}"))
                    chain(nc.vector.reciprocal(stat[:, q:q + 4 * W], small[:, c:c + 4 * W]), f"{name}_dve", f"{name}.inverse{h}")
                    if W == 2:
                        chain(ts(stat[:, q + 4:q + 8], stat[:, q + 4:q + 8], lamt[:, 68:69], None, ALU.mult), f"{name}_dve", f"{name}.lam{h}")
                    for i in range(TT):
                        p_ = ptile(h, i, pbuf(h, 0))
                        if W == 2:
                            p2 = ptile(h, i, pbuf(h, 1))
                            chain(ts(p2, p2, stat[:, q + 4 + i:q + 5 + i], None, ALU.mult), f"{name}_dve", f"{name}.second{h}.{i}")
                            ins = stt(p_, p_, stat[:, q + i:q + i + 1], p2, ALU.mult, ALU.add)
                        else:
                            ins = ts(p_, p_, stat[:, q + i:q + i + 1], None, ALU.mult)
                        ins.then_inc(*tick(f"{name}_dve", f"{name}.prob{h}.{i}"))

                biased(0)
                for h in range(H):
                    if h + 1 < H:
                        biased(h + 1)
                    divided(h)
                    if h >= 1:
                        finish(h - 1)
                finish(H - 1)

            nc.vector.memset(eps, EPS).then_inc(*tick("norm_dve", "in.eps"))
            lo(0, 0)
            lo(1, 1)
            dve.wait_ge(*at("in.vec"))
            dve.wait_ge(*at("in.const"))
            norm_pre("mix_pre0")

            for u in range(9):
                if u >= 1:
                    lo(u + 1, (u + 1) % 2)
                if u == 2:
                    z, l_, one, neg = prob[0:H, 0, 512:1024], prob[0:H, 0, 0:512], prob[0:H, 1, 0:512], prob[0:H, 1, 512:1024]
                    dve.wait_ge(evac, 1)
                    nc.vector.memset(one, 1.0)
                    chain(ts(z, misc[0:H, :], v("b_forget")[0:H, :], 0.0, ALU.add, ALU.min), "gate_dve", "gate.min")
                    dve.wait_ge(*at("gate.ln"))
                    chain(tt(z, z, l_, ALU.subtract), "gate_dve", "gate.logf")
                    chain(nc.vector.tensor_tensor_scan(l_, one, z, 0.0, ALU.mult, ALU.add), "gate_dve", "gate.summed")
                    ts(neg, l_, -1.0, None, ALU.mult).then_inc(*tick("gate_dve", "gate.rows"))
                if u == 4:
                    dve.wait_ge(*at("cq.root"))
                    chain(nc.vector.reciprocal(stat[:, 0:8], small[:, 0:8]), "norm_dve", "cq.inverse")
                    diagonal(dg[:].rearrange("p t n -> p (t n)"), 0).then_inc(*tick("norm_dve", "cq.diag"))
                    diagonal(ss[:], 4).then_inc(*tick("norm_dve", "ckv.diag"))
                if u == 6:
                    dve.wait_ge(*at("ckv.spread"))
                    for k in range(6):
                        if k < 5:
                            g = v("q_norm", k) if k < 3 else v("kv_norm", k - 3)
                            stt(y[:, k, :], y[:, k, :], g, bank[6 if k < 3 else 5][:], ALU.mult, ALU.mult)\
                                .then_inc(*tick("norm_dve", f"cq.t{k}"))
                        if k >= 1:
                            lo_tile("cq", k - 1, y[:, k - 1, :], cqH, cqL)

            def halves(name, tile0):
                def finish(h):
                    r = slice(64 * (h % 2), 64 * (h % 2) + 64)
                    dve.wait_ge(*at(f"{name}.hi{h}"))
                    k = tile0 + h // 2
                    tt(hL[r, k, :], bank[6 + h % 2][r, :], hH[r, k, :].bitcast(F32), ALU.subtract)\
                        .then_inc(*tick(f"{name}_dve", f"{name}.out{h}"))
                return finish
            dve.wait_ge(*at(f"gate.bias{H - 1}"))
            attention("fox", lambda h, i: cB[:, h, 0:P * (i + 1)], lambda h, w: prob[:, h % 2, :], 1, halves("fox", 0))
            cos, sin = rope[64:96, 0:512], rope[64:96, 512:1024]

            def rotary(r):
                dve.wait_ge(*at(f"rope.turned{r}"))
                if r >= 1:
                    dve.wait_ge(evac, TILE0["even_uq"] + r)
                src = misc[64:96, :] if r == 0 else qM[64:96, r - 1, :]
                t_ = y[64:96, r % 2, :]
                tt(t_, bank[4 + r % 2][64:96, :], sin, ALU.mult).then_inc(*tick("rope_dve", f"rope.sin{r}"))
                chain(tt(src, src, cos, ALU.mult), "rope_dve", f"rope.cos{r}")
                tt(src, src, t_, ALU.add).then_inc(*tick("rope_dve", "rope.key" if r == 0 else f"rope.q{r - 1}"))
            for u in range(3):
                n = UNIT0["even_uq"] + u
                lo(n + 1, (n + 1) % 2)
                if u == 1:
                    for r in range(H + 1):
                        rotary(r)
            attention("mla", lambda h, i: window[:, FAR - P * i:], lambda h, w: prob[:, h % 2, :], 1, halves("mla", 4))
            stream_out2("even_out", "y")

            def ffn(l):
                norm_post(f"mix_post{l}")
                norm_pre(f"ffn_pre{l}")
                for g in range(2):
                    name = f"ffn{l}_up{g}"
                    with ev.loop(dve, looped(name, 2)) as i:
                        for s in range(2):
                            lo_next(name, i, s)
                            m = i * 2 + (FF_GROUPS[0] * g + s)
                            gate, val, c = bank[2 * s], bank[2 * s + 1], ft[:, s, :]
                            dve.wait_ge(*at(f"{name}.tap2.{s}", i))
                            chain(stt(c[:, 1:], gate[:, 0:SEQ - 1], vr(f"conv{l}", m + FF_T), c[:, 1:], ALU.mult, ALU.add),
                                  "ffn_dve", f"{name}.tap1.{s}", i)
                            stt(c[:, 2:], gate[:, 0:SEQ - 2], vr(f"conv{l}", m), c[:, 2:], ALU.mult, ALU.add)\
                                .then_inc(evac, 1)
                            dve.wait_ge(*at(f"{name}.gelu{s}", i))
                            done(name, i * 4 + (2 * s + 1))
                            tt(ft[:, 4 + s, :], ft[:, 2 + s, :], val[:], ALU.mult)\
                                .then_inc(evac, 1)
                            dve.wait_ge(*at(f"{name}.hi{s}", i))
                            t1 = bass.ds(i * 2 + s, 1)
                            tt(mL[:, t1, :], ft[:, 4 + s, :].unsqueeze(1), mH[:, t1, :].bitcast(F32), ALU.subtract)\
                                .then_inc(*tick("ffn_dve", f"{name}.lo{s}"))
                    stream_down(f"ffn{l}_down{g}", "y0" if g == 0 else "y1")
                norm_post(f"ffn_post{l}")

            ffn(0)

            norm_pre("mix_pre1")
            lam = v("lam", 0, 256)
            for w, event in enumerate(("lam.first", "lam.dots")):
                o = 128 * w
                chain(nc.vector.tensor_tensor_reduce(lamt[:, 0:64], lam[:, o:o + 64], lam[:, o + 64:o + 128], 1.0, 0.0,
                                                     ALU.mult, ALU.add, lamt[:, 64 + w:65 + w]), "lam_dve", event)
            dve.wait_ge(*at("lam.exp"))
            chain(tt(lamt[:, 68:69], lamt[:, 67:68], lamt[:, 66:67], ALU.subtract), "lam_dve", "lam.difference")
            ts(lamt[:, 68:69], lamt[:, 68:69], -LAMBDA_INIT, None, ALU.add).then_inc(*tick("lam_dve", "lam.minus"))
            ts(lamt[:, 70:71], v("subln"), 1.0 - LAMBDA_INIT, None, ALU.mult).then_inc(*tick("lam_dve", "lam.gain"))
            for name in ("odd_q", "odd_k", "odd_v"):
                stream_plain(name)
            dve.wait_ge(*at("lam.gain"))
            attention("diff", lambda h, i: alibi[:, h % 2, FAR - P * i:], lambda h, w: probO[:, h % 2, w, :], 2, lambda h: None)

            def head_norms(tag, src, gain, then):
                dve.wait_ge(*at(f"{tag}.root"))
                chain(nc.vector.reciprocal(stat[:, 0:32], small[:, 0:32]), "norm_dve", f"{tag}.inverse")
                for h in range(H + 1):
                    if h < H:
                        if h >= 2:
                            dve.wait_ge(*at(f"{tag}.spread{h - 2}"))
                        diagonal(y[:, h % 2, :], 4 * h).then_inc(*tick("norm_dve", f"{tag}.diag{h}"))
                    if h >= 1:
                        dve.wait_ge(*at(f"{tag}.spread{h - 1}"))
                        then(h - 1, src(h - 1), gain, bank[4 + (h - 1) % 2][:])

            def subln(h, src, gain, inv):
                stt(y[:, 2 + h % 4, :], src, gain, inv, ALU.mult, ALU.mult).then_inc(*tick("norm_dve", f"subln.t{h}"))
                lo_tile("subln", h, y[:, 2 + h % 4, :])
            head_norms("subln", lambda h: qO[:, h, :], lamt[:, 70:71], subln)
            stream_out2("odd_out", "y")
            ffn(1)

            norm_pre("mix2")
            dve.wait_ge(*at("dn.wba_hi"))
            tt(wbaL[:], wba[:], wbaH[:].bitcast(F32), ALU.subtract).then_inc(*tick("dn_dve", "dn.wba"))
            dve.wait_ge(*at("dn.ba"))
            ba = bank[5][:, 0:64].rearrange("p (t c) -> p t c", c=16)
            za = zed[:].rearrange("p t (w h) -> p t w h", w=2)
            tt(za[:, :, 0, :], ba[:, :, 8:16], v("dt_bias", 0, 8).unsqueeze(1).to_broadcast([P, TT, 8]), ALU.add)\
                .then_inc(*tick("dn_dve", "dn.z"))
            dve.wait_ge(*at("dn.z"))
            dve.wait_ge(*at("dn.ln"))
            chain(stt(za[:, :, 0, :], za[:, :, 0, :], 0.0, za[:, :, 1, :], ALU.max, ALU.add), "dn_dve", "dn.softplus")
            stt(tok[:, 1, :].rearrange("p (h t) -> p t h", t=TT), za[:, :, 0, :], -1.0,
                tok[:, 12, 0:8].unsqueeze(1).to_broadcast([P, TT, 8]), ALU.mult, ALU.mult).then_inc(*tick("dn_dve", "dn.g"))
            with ev.loop(dve, looped("dn_qkv", 2)) as i:
                for s in range(2):
                    lo_next("dn_qkv", i, s)
                    for tl in range(2):
                        c = 2 * s + tl
                        dve.wait_ge(*at(f"dn.tap3.{c}", i))
                        for tap in (2, 1, 0):
                            d = 3 - tap
                            ins = stt(y[:, c, d:], bank[c][:, 0:SEQ - d], vr("dn_conv", i * 4 + (c + 24 * tap)), y[:, c, d:],
                                      ALU.mult, ALU.add)
                            if tap:
                                chain(ins, "dn_conv_dve", f"dn.tap{tap}.{c}", i)
                        ins.then_inc(evac, 1)
            dve.wait_ge(*at("dn.tot_copied"))
            tt(tok[:, 5, :], tok[:, 3, :], tok[:, 2, :], ALU.subtract).then_inc(*tick("dn_dve", "dn.left"))
            nc.vector.tensor_copy(tok[:, 10, :], tok[:, 2, :])
            stream_plain("dn_z")
            for g in range(2):
                nc.vector.memset(S[:, 4 * g:4 * g + 4, :], 0.0).then_inc(*tick("scan_dve", f"scan.state-1.{g}"))
            dve.wait_ge(*at("dn.root"))
            roots = tok[:, 14:16, :].rearrange("p a b -> p (a b)")
            chain(nc.vector.reciprocal(roots, roots), "dn_dve", "dn.inverse")
            tt(tok[:, 8, :], tok[:, 0, :], tok[:, 15, :], ALU.mult).then_inc(*tick("dn_dve", "dn.beta_k"))
            ts(tok[:, 9, :], tok[:, 14, :], float(P) ** -0.5, None, ALU.mult).then_inc(*tick("dn_dve", "dn.rowset"))
            dve.wait_ge(*at("dn.eleft"))
            dve.wait_ge(*at("dn.rowset"))
            tt(tok[:, 6, :], tok[:, 8, :], tok[:, 4, :], ALU.mult)
            tt(tok[:, 7, :], tok[:, 15, :], tok[:, 5, :], ALU.mult).then_inc(*tick("dn_dve", "dn.scalars"))
            dve.wait_ge(*at("dn.scalars"))
            tiles = [slice(t * P, (t + 1) * P) for t in range(TT)]

            def masked(m):
                return dconst[:, m * P:(m + 1) * P].unsqueeze(1).to_broadcast([P, TT, P])

            def blocks(ap):
                return ap.rearrange("p (t n) -> p t n", t=TT)
            for h0 in range(0, H, 2):
                pair = [(h0 + p, [bank[4 * p + b] for b in range(4)], tmp(p)) for p in range(2)]
                for h, b, m in pair:
                    dve.wait_ge(*at(f"dn.spread{h}"))
                    tt(m["t1"], qkv[:, 8 + h, :], b[0][:], ALU.mult)
                    tt(m["x"], qkv[:, h, :], b[1][:], ALU.mult).then_inc(*tick("dn_dve", f"dn.qn{h}"))
                    dve.wait_ge(*at(f"dn.e{h}"))
                    for t, c in enumerate(tiles):
                        last = ts(m["lt"][:, c], b[2][:, c], tok[:, 2, 4 * h + t:4 * h + t + 1], 0.0, ALU.subtract, ALU.min)
                    last.then_inc(*tick("dn_dve", f"dn.diff{h}"))
                for h, b, m in pair:
                    dve.wait_ge(*at(f"dn.gram{h}"))
                    dve.wait_ge(*at(f"dn.causal{h}"))
                    for t, c in enumerate(tiles):
                        r = 32 + 4 * h + t
                        stt(attnT[:, h, c], b[1][:, c], roots[:, r:r + 1], m["y"][:, c], ALU.mult, ALU.mult)
                        last = stt(m["lt"][:, c], b[0][:, c], roots[:, r:r + 1], m["lt"][:, c], ALU.mult, ALU.mult)
                    chain(last, "dn_dve", f"dn.attn{h}")
                    chain(tt(blocks(m["y"]), blocks(m["lt"]), masked(2), ALU.mult), "dn_dve", f"dn.first{h}")
                    tt(blocks(m["y"]), ident.unsqueeze(1).to_broadcast([P, TT, P]), blocks(m["y"]), ALU.subtract)\
                        .then_inc(*tick("dn_dve", f"dn.y{h}.0"))
                for s in range(1, 6):
                    for h, b, m in pair:
                        dve.wait_ge(*at(f"dn.lx{h}.{s}"))
                        tt(blocks(m["t1"]), blocks(b[1][:]), masked(2 + s), ALU.mult).then_inc(*tick("dn_dve", f"dn.t{h}.{s}"))
                    for h, b, m in pair:
                        dve.wait_ge(*at(f"dn.xx{h}.{s}"))
                        dve.wait_ge(*at(f"dn.y{h}.{s - 1}"))
                        if s < 5:
                            dve.wait_ge(*at(f"dn.x{h}.{s - 1}"))
                            tt(m["x"], m["x"], b[2][:], ALU.subtract).then_inc(*tick("dn_dve", f"dn.x{h}.{s}"))
                        tt(m["y"], m["y"], b[3][:], ALU.subtract).then_inc(*tick("dn_dve", f"dn.y{h}.{s}"))
            for n in range(8):
                t, r = n // 2, slice(64 * (n % 2), 64 * (n % 2) + 64)
                for g in range(2):
                    hs = slice(4 * g, 4 * g + 4)
                    dve.wait_ge(*at(f"scan.ws{n}.{g}"))
                    if n == 0:
                        dve.wait_ge(*at(f"dn.w{H - 1}"))
                    if n >= 1:
                        dve.wait_ge(*at(f"scan.kv{n - 1}.{g}"))
                    tt(vN[r, hs, :], qkv[r, 16 + 4 * g:20 + 4 * g, t * P:(t + 1) * P],
                       bank[g][r, :].rearrange("p (h d) -> p h d", h=4), ALU.subtract).then_inc(*tick("scan_dve", f"scan.vn{n}.{g}"))
                for g in range(2):
                    dve.wait_ge(*at(f"scan.kv{n}.{g}"))
                    dve.wait_ge(*at(f"scan.state{n - 1}.{g}"))
                    for hh in range(4):
                        h = 4 * g + hh
                        last = stt(S[:, h, :], S[:, h, :], gl[:, h, n:n + 1], bank[2 + g][:, hh * P:(hh + 1) * P], ALU.mult, ALU.add)
                    last.then_inc(*tick("scan_dve", f"scan.state{n}.{g}"))

            def gated(h, src, gain, inv):
                if h >= 2:
                    dve.wait_ge(*at(f"gated.t{h - 2}"))
                stt(y[:, 2 + h % 2, :], src, gain, inv, ALU.mult, ALU.mult).then_inc(*tick("norm_dve", f"gated.n{h}"))
                if h >= 1:
                    lo_tile("gated", h - 1, y[:, 4 + (h - 1) % 4, :])
            head_norms("gated", lambda h: qkv[:, h, :], v("dn_norm"), gated)
            lo_tile("gated", H - 1, y[:, 4 + (H - 1) % 4, :])
            stream_out2("dn_out", "x1")
            norm_pre("mlp2")
            for g in range(2):
                name = f"mlp_up{g}"
                with ev.loop(dve, looped(name, 2)) as i:
                    for s in range(2):
                        lo_next(name, i, s)
                        for tl in range(2):
                            c = 2 * s + tl
                            dve.wait_ge(*at(f"{name}.relu{c}", i))
                            tt(y[:, 4 + c, :], y[:, c, :], bank[c][:], ALU.mult)\
                                .then_inc(evac, 1)
                            dve.wait_ge(*at(f"{name}.hi{c}", i))
                            t1 = bass.ds(i * 4 + c, 1)
                            tt(mL[:, t1, :], y[:, 4 + c, :].unsqueeze(1), mH[:, t1, :].bitcast(F32), ALU.subtract)\
                                .then_inc(*tick("mlp_dve", f"{name}.lo{c}"))
                stream_down(f"mlp_down{g}", ("x0", "x1")[g])
            stream_down("mlp_down2", "x1", last=True, t0=4)
            inverse("final")
            for k in range(KT):
                stt(y[:, k, :], x[:, k, :], v("final", k), bank[6][:], ALU.mult, ALU.mult)\
                    .then_inc(*tick("norm_dve", f"final.t{k}"))

        @block.gpsimd
        def _(pool):
            def tt(*args):
                return nc.gpsimd.tensor_tensor(*args)

            def add_odd(tag):
                for k in range(1, KT, 2):
                    pool.wait_ge(*at(f"{tag}.t{k}"))
                    tt(x[:, k, :], x[:, k, :], y[:, k, :], ALU.add).then_inc(*tick("norm_pool", f"{tag}.x{k}"))

            pool.wait_ge(*at("rope.key"))
            nc.gpsimd.tensor_copy(kM[64:96, :, :], misc[64:96, :].unsqueeze(1).to_broadcast([32, H, SEQ]))\
                .then_inc(*tick("rope_pool", "rope.k"))
            add_odd("mix_post0")
            add_odd("ffn_post0")
            pool.wait_ge(*at("in.dist"))
            for h in range(H):
                if h >= 2:
                    pool.wait_ge(*at(f"diff.biased{(h - 2) * 8 + 7}"))
                nc.gpsimd.tensor_scalar(alibi[:, h % 2, :], dist[:], 2.0 ** -(h + 1), None, ALU.mult)\
                    .then_inc(*tick("alibi_pool", f"alibi{h}"))
            add_odd("mix_post1")
            add_odd("ffn_post1")
            for h0 in range(0, H, 2):
                for h in (h0, h0 + 1):
                    m = tmp(h % 2)
                    pool.wait_ge(*at(f"dn.dec{h}"))
                    tt(m["y"].rearrange("p (t n) -> p t n", t=TT), m["lt"].rearrange("p (t n) -> p t n", t=TT),
                       dconst[:, 0:P].unsqueeze(1).to_broadcast([P, TT, P]), ALU.mult).then_inc(*tick("dn_pool", f"dn.causal{h}"))
                    pool.wait_ge(*at(f"dn.qn{h}"))
                    pool.wait_ge(*at(f"dn.gl{h}"))
                    tt(qkv[:, h, :], m["x"], m["e"], ALU.mult).then_inc(*tick("dn_pool", f"dn.qdec{h}"))
            for h in range(H):
                pool.wait_ge(*at(f"gated.n{h}"))
                if h >= 4:
                    pool.wait_ge(*at(f"gated.h{h - 4}"))
                tt(y[:, 4 + h % 4, :], y[:, 2 + h % 2, :], zT[:, h, :], ALU.mult).then_inc(*tick("gated_pool", f"gated.t{h}"))

    return ev.found


def constants():
    i, j = np.arange(P)[:, None], np.arange(P)[None, :]
    u = np.arange(SEQ)[None, :]
    window = np.where(u <= FAR + i, 0.0, NEG)
    const = np.concatenate([np.eye(P), np.ones((P, P)), window], 1)
    dist = np.where(u <= FAR + i, u - (FAR + i), NEG)
    chunk = (i // 64) == (j // 64)
    masks = [chunk & (i <= j), chunk, (i % 2 == 0) & (j == i + 1)]
    masks += [((i // b) % 2 == 1) & (j // b == i // b - 1) for b in (2, 4, 8, 16, 32)]
    rope = np.zeros((P, 1056), np.float32)
    f = np.float32
    inv = f(10000.0) ** (-np.arange(0, 32, 2, dtype=f) / f(32))
    ang = np.arange(SEQ, dtype=f)[None, :] * inv[:, None]
    for half in range(2):
        rope[64 + 16 * half:80 + 16 * half, 0:512] = np.cos(ang)
        rope[64 + 16 * half:80 + 16 * half, 512:1024] = np.sin(ang)
    for m in range(16):
        rope[80 + m, 1024 + m] = -1.0
        rope[64 + m, 1040 + m] = 1.0
    return {"const": const.astype(f), "dist": dist.astype(f), "rope": rope,
            "dconst": np.concatenate(masks, 1).astype(f)}


def units(w, cols):
    k, m = w.shape
    return w.reshape(k // P, P, m // cols, cols).transpose(2, 1, 0, 3).reshape(m // cols, P, -1)


def kernel(**inputs):
    import concourse.bacc as bacc
    from concourse.bass_utils import run_bass_kernel_spmd as run

    a = {n: np.asarray(t) for n, t in inputs.items()}
    w = a["even_w_in"][0]
    cuts = np.cumsum([512, 512, 512, 8, 384, 256]).tolist()
    fq, fk, fv, _, cq, ckv, kr = np.split(w, cuts, axis=1)
    misc = np.concatenate([w[:, cuts[2]:cuts[2] + 64], kr, cq[:, 0:32]], 1)
    arrays = dict(constants())
    arrays["x"] = a["x"][0].reshape(TT, P, DM).transpose(1, 0, 2)
    arrays["even_in"] = units(np.concatenate([misc, cq, ckv, fq, fk, fv], 1), 256)
    arrays["even_uq"] = units(a["even_w_uq"][0], 384)
    arrays["even_ukv"] = units(a["even_w_ukv"][0], 1024)
    arrays["even_out"] = units(a["even_w_out"][0], 256)
    for n, part in zip("qkv", np.split(a["odd_w_in"][0], 3, axis=1)):
        arrays[f"odd_{n}"] = units(part, 256)
    arrays["odd_out"] = units(a["odd_w_out"][0], 256)
    for l in range(2):
        gate, val = np.split(a["ffn_w_up"][l], 2, axis=1)
        up = np.concatenate([gate.reshape(KT, P, FF_T, P), val.reshape(KT, P, FF_T, P)], 3)
        up = up.transpose(2, 1, 0, 3).reshape(FF_T, P, -1)
        cut = FF_GROUPS[0]
        arrays[f"ffn{l}_up0"], arrays[f"ffn{l}_up1"] = up[:cut], up[cut:]
        down = a["ffn_w_down"][l]
        arrays[f"ffn{l}_down0"], arrays[f"ffn{l}_down1"] = units(down[:cut * P], P), units(down[cut * P:], P)
    w = a["dn_w_in_2"][0]
    arrays["dn_qkv"], arrays["dn_z"] = units(w[:, :3072], 256), units(w[:, 3072:4096], 256)
    arrays["wba"] = units(w[:, 4096:], 16)[0]
    arrays["dn_out"] = units(a["dn_w_out_2"][0], 256)
    up, down = units(a["mlp_w_up_2"][0], 256), a["mlp_w_down_2"][0]
    half = MLP_GROUP * P
    arrays["mlp_up0"], arrays["mlp_up1"] = up[:8], up[8:]
    arrays["mlp_down0"] = units(down[:half], P)
    arrays["mlp_down1"], arrays["mlp_down2"] = np.split(units(down[half:], P), 2)

    def col(t):
        return t.reshape(-1, P).T

    def wide(t):
        return np.broadcast_to(t.reshape(1, -1), (P, t.size))
    pieces = []
    for l in range(2):
        pieces += [col(a[n][l]) for n in ("norm_mix_pre", "norm_mix_post", "norm_ffn_pre", "norm_ffn_post")]
    pieces += [col(a[n]) for n in ("norm_mix_2", "norm_mlp_2", "norm_final_2", "even_q_norm", "even_kv_norm")]
    for l in range(2):
        pieces += [col(a["ffn_conv_w"][l]), col(a["ffn_conv_b"][l])]
    forget = np.zeros((P, 1), np.float32)
    forget[0:H, 0] = a["even_b_forget"][0]
    pieces += [col(a["dn_conv_w_2"][0]), col(a["dn_norm_w_2"]), col(a["odd_subln"]), forget]
    pieces += [wide(a[n]) for n in ("dn_a_log_2", "dn_dt_bias_2", "odd_lambda_q1", "odd_lambda_k1",
                                    "odd_lambda_q2", "odd_lambda_k2")]
    arrays["vec"] = np.concatenate(pieces, 1)
    arrays = {n: np.ascontiguousarray(t) for n, t in arrays.items()}

    def program(known):
        nc = bacc.Bacc("TRN2", target_bir_lowering=False, num_devices=1)
        dram = {n: nc.dram_tensor(f"in_{n}", t.shape, F32, kind="ExternalInput").ap() for n, t in arrays.items()}
        dram["out"] = nc.dram_tensor("out", (SEQ, DM), F32, kind="ExternalOutput").ap()
        return nc, build(nc, dram, known)

    _, known = program(None)
    nc, _ = program(known)
    r = run(nc, [{f"in_{n}": t for n, t in arrays.items()}], core_ids=[0])
    return r.results[0]["out"].reshape(1, SEQ, DM)
```

```python
from contextlib import ExitStack

import numpy as np
import concourse.bass as bass
import concourse.mybir as mybir

F32 = mybir.dt.float32
F32R = mybir.dt.float32r
ACT = mybir.ActivationFunctionType
ALU = mybir.AluOpType
AX = mybir.AxisListType

P = 128
SEQ, DM = 512, 1024
KT = DM // P
TT = SEQ // P
H = 8
FF_T = 2816 // P
FF_GROUPS = (12, 10)
MLP_GROUP = 16
EPS = 1e-6
NEG = -1e30
FAR = 384
LAMBDA_INIT = 0.8 - 0.6 * float(np.exp(-0.3))
SLOT = 2048

STREAMS = [("even_in", 9, 2048), ("even_uq", 2, 1152), ("even_ukv", 1, 2048), ("even_out", 4, 2048)]
for _l in range(2):
    if _l == 1:
        STREAMS += [("odd_q", 4, 2048), ("odd_k", 4, 2048), ("odd_v", 4, 2048), ("odd_out", 4, 2048)]
    for _g in range(2):
        STREAMS += [(f"ffn{_l}_up{_g}", FF_GROUPS[_g], 2048), (f"ffn{_l}_down{_g}", KT, FF_GROUPS[_g] * P)]
STREAMS += [("dn_qkv", 12, 2048), ("dn_z", 4, 2048), ("dn_out", 4, 2048)]
STREAMS += [("mlp_up0", 8, 2048), ("mlp_down0", 8, 2048), ("mlp_up1", 8, 2048), ("mlp_down1", 4, 2048), ("mlp_down2", 4, 2048)]
UNITS = sum(u for _, u, _ in STREAMS)
UNIT0, _n = {}, 0
for _name, _u, _w in STREAMS:
    UNIT0[_name] = _n
    _n += _u
NUNITS = {name: u for name, u, _ in STREAMS}
WIDTH = {name: w for name, _, w in STREAMS}
TILES = {"even_in": 6 + 8 + 8, "even_uq": 8, "even_ukv": 8 + 4, "odd_v": 16}
for _name, _u, _w in STREAMS:
    TILES.setdefault(_name, _u if "down" in _name else 2 * _u)
TILE0, _n = {}, 0
for _name, _u, _w in STREAMS:
    TILE0[_name] = _n
    _n += TILES[_name]

VEC, _n = {}, 0
for _name, _w in [("mix_pre0", 8), ("mix_post0", 8), ("ffn_pre0", 8), ("ffn_post0", 8),
                  ("mix_pre1", 8), ("mix_post1", 8), ("ffn_pre1", 8), ("ffn_post1", 8),
                  ("mix2", 8), ("mlp2", 8), ("final", 8), ("q_norm", 3), ("kv_norm", 2),
                  ("conv0", 4 * FF_T), ("conv1", 4 * FF_T), ("dn_conv", 4 * 24), ("dn_norm", 1),
                  ("subln", 1), ("b_forget", 1), ("a_log", 8), ("dt_bias", 8), ("lam", 256)]:
    VEC[_name] = _n
    _n += _w
NVEC = _n


def peeled(i):
    return isinstance(i, int) and i == 0


class Events:

    def __init__(self, nc, ctx, known):
        self.nc, self.ctx, self.known = nc, ctx, known
        self.sems, self.count, self.found, self.open = {}, {}, {}, None

    def sem(self, name):
        if name not in self.sems:
            self.sems[name] = self.ctx.enter_context(self.nc.semaphore(name))
            self.count[name] = 0
        return self.sems[name]

    def tick(self, name, event=None, by=1):
        s = self.sem(name)
        self.count[name] += by
        if event is not None:
            assert self.open is not None or event not in self.found, event
            self.found.setdefault(event, (name, self.count[name], 0))
            if self.open is not None:
                self.open.append((event, self.count[name]))
        return s, by

    def at(self, event, i=None):
        if self.known is None:
            return self.sem("first_build"), 1
        name, value, stride = self.known[event]
        if i is None:
            return self.sem(name), value
        return self.sem(name), i * stride + value

    def loop(self, eng, n, peel=0):
        for i in range(peel):
            yield i
        before, self.open = dict(self.count), []
        with eng.Fori(peel, n) as i:
            yield i
        for name, c in self.count.items():
            per = c - before.get(name, 0)
            self.count[name] = before.get(name, 0) + (n - peel) * per
            for e, seen in self.open:
                if self.found[e][0] == name:
                    assert seen == self.found[e][1] + peel * per, e
                    self.found[e] = (name, self.found[e][1], per)
        self.open = None


def build(nc, dram, known):
    ctx = ExitStack()
    with ctx:
        ev = Events(nc, ctx, known)
        tick, at = ev.tick, ev.at
        sem = ev.sem

        place = [((nc.sbuf_base + 63) // 64) * 64]

        def sb(name, shape, dt=F32, where=None):
            size = 4 * int(np.prod(shape[1:]))
            if where is None:
                where = place[0]
                place[0] += size
            assert where + size <= nc.sbuf_usable_end, (name, where + size - nc.sbuf_usable_end)
            return nc.alloc_sbuf_tensor_at(name, shape, dt, offset=where)

        x = sb("x", [P, KT, SEQ])
        h_at = place[0]
        hH = sb("hH", [P, KT, SEQ], F32R)
        hL = sb("hL", [P, KT, SEQ], F32R)
        raw = [sb(f"raw{s}", [P, SLOT]) for s in range(2)]
        wH = [sb(f"wH{s}", [P, SLOT], F32R) for s in range(2)]
        wL = [sb(f"wL{s}", [P, SLOT], F32R) for s in range(2)]
        y = sb("y", [P, KT, SEQ])
        const = sb("const", [P, 768])
        vec = sb("vec", [P, NVEC])
        sq = sb("sq", [P, 2, SEQ])
        ss = sb("ss", [P, SEQ])
        dg = sb("dg", [P, TT, P])
        small = sb("small", [P, 64])
        stat = sb("stat", [P, 64])
        base = place[0]
        ident, ones, window = const[:, 0:P], const[:, P:2 * P], const[:, 2 * P:]
        eps = small[:, 60:61]
        rinv = dg[:].rearrange("p t n -> p (t n)")

        def stage(items):
            place[0] = base
            return [sb(*it) for it in items]

        xin, = stage([("xin", [P, TT, DM])])
        cqH, cqL, misc, rope, prob, gate_row = stage([
            ("cqH", [P, 5, SEQ], F32R), ("cqL", [P, 5, SEQ], F32R), ("misc", [P, SEQ]), ("rope", [P, 1056]),
            ("prob", [P, 2, 1280]), ("gate_row", [P, 64])])
        even2 = place[0]
        qF, kF, vF, cB = (sb(*it) for it in [("qF", [P, 4, SEQ]), ("kF", [P, 4, SEQ]), ("vF", [P, TT, 512]),
                                             ("cB", [P, H, SEQ])])
        place[0] = even2
        qM, kM, vM = (sb(*it) for it in [("qM", [P, H, SEQ]), ("kM", [P, H, SEQ]), ("vM", [P, TT, 512])])
        mH, mL, ft = stage([("mH", [P, MLP_GROUP, SEQ], F32R), ("mL", [P, MLP_GROUP, SEQ], F32R), ("ft", [P, 8, SEQ])])
        qO, kO, vO, dist, alibi, probO, lamt = stage([
            ("qO", [P, H, SEQ]), ("kO", [P, H, SEQ]), ("vO", [P, TT, DM]), ("dist", [P, SEQ]),
            ("alibi", [P, 2, SEQ]), ("probO", [P, 2, 2, 1280]), ("lamt", [P, 128])])
        qkv, zT, S, vN, dconst, wba, tok = stage([
            ("qkv", [P, 24, SEQ]), ("zT", [P, H, SEQ]), ("S", [P, H, P]), ("vN", [P, H, P]),
            ("dconst", [P, 8 * P]), ("wba", [P, P]), ("tok", [P, 16, 32])])
        wbaH, wbaL = sb("wbaH", [P, P], F32R), sb("wbaL", [P, P], F32R)
        rowsT, gl, zed = sb("rowsT", [P, P]), sb("gl", [P, H, 8]), sb("zed", [P, 4, 16])
        o_at = base + 4 * 8 * SEQ
        oH, oL = sb("oH", [P, KT, SEQ], F32R, o_at), sb("oL", [P, KT, SEQ], F32R, o_at + 4 * KT * SEQ)
        attnT = sb("attnT", [P, H, SEQ], F32, h_at)
        kdec = sb("kdec", [P, H, SEQ], F32, h_at + 4 * KT * SEQ)
        PT = y[:].rearrange("p (a j) n -> p a j n", a=2)

        bank = [ctx.enter_context(nc.psum_tensor(f"bank{b}", [P, 512], F32)) for b in range(8)]

        w_in = [sem(f"weights_loaded{s}") for s in range(2)]
        w_hi, w_split = sem("weights_hi"), sem("weights_split")
        mm_done, evac = sem("tile_done"), sem("tile_evacuated")
        block = ctx.enter_context(nc.Block())

        def v(name, k=0, n=1):
            return vec[:, VEC[name] + k:VEC[name] + k + n]

        def vr(name, i, n=1):
            return vec[:, bass.ds(i + VEC[name], n)]

        def ptile(h, i, buf):
            o = P * (i * (i + 1) // 2)
            return buf[:, o:o + P * (i + 1)]

        def looped(name, per):
            return NUNITS[name] // per

        def tmp(p):
            names = ["lt", "y", "x", "t1", "r", "e"]
            slots = [y[:, k, :] for k in range(KT)] + [sq[:, k, :] for k in range(2)] + [dg[:].rearrange("p t n -> p (t n)"), ss[:]]
            return {n: slots[6 * p + k] for k, n in enumerate(names)}

        @block.sync
        def _(sp):
            for k, (dst, src) in enumerate([(xin[:], "x"), (const[:], "const"), (vec[:], "vec")]):
                sp.dma_start(dst, dram[src]).then_inc(*tick(f"loaded_{src}", f"in.{src}", 16))

            def load(name, n, j, s):
                w = WIDTH[name]
                sp.dma_start(raw[s][:, 0:w].unsqueeze(1),
                             dram[name].rearrange("u p c -> p u c")[:, bass.ds(j, 1), :]).then_inc(w_in[s], 16)

            for name, units, _w in STREAMS:
                n0 = UNIT0[name]
                if name.startswith("even_") and name != "even_out":
                    for j in range(units):
                        n = n0 + j
                        if n >= 2:
                            sp.wait_ge(w_split, n - 1)
                        load(name, n, j, n % 2)
                else:
                    with sp.Fori(0, units // 2) as i:
                        for s in range(2):
                            sp.wait_ge(w_split, i * 2 + (n0 + s - 1))
                            load(name, n0 + s, i * 2 + s, s)
            for t in range(TT):
                sp.wait_ge(*at(f"out.copied{t}"))
                sp.dma_start(dram["out"][t * P:(t + 1) * P, :], xin[:, t, :]).then_inc(*tick("stored", f"out.stored{t}", 16))
            sp.wait_ge(*at(f"out.stored{TT - 1}"))

        @block.tensor
        def _(pe):
            mm = nc.tensor.matmul

            def three(out, w, xv, first, last, swap=False):
                (a, b), (c, d) = (xv, w) if swap else (w, xv)
                mm(out, a, c, start=first, stop=False)
                mm(out, a, d, start=False, stop=False)
                return mm(out, b, c, start=False, stop=last)

            def tile_wait(name, l):
                pe.wait_ge(evac, l + (TILE0[name] - 3))

            def begin(name):
                if TILE0[name]:
                    pe.wait_ge(evac, TILE0[name])

            def unit_tiles(s, kt, aH, aL, b0, tiles=2, cols=256, wait=None, k0=0):
                for tl in range(tiles):
                    if wait is not None:
                        wait(tl)
                    for k in range(kt):
                        c = slice(k * cols + tl * P, k * cols + tl * P + P)
                        last = three(bank[b0 + tl][:], (wH[s][:, c], wL[s][:, c]),
                                     (aH[:, k0 + k, :], aL[:, k0 + k, :]), k == 0, k == kt - 1)
                    last.then_inc(mm_done, 1)

            def first_unit(s, ready, then):
                for k in range(KT):
                    ready(k)
                    for tl in range(2):
                        c = slice(k * 256 + tl * P, k * 256 + tl * P + P)
                        last = three(bank[tl][:], (wH[s][:, c], wL[s][:, c]), (hH[:, k, :], hL[:, k, :]), k == 0, k == KT - 1)
                        if k == KT - 1:
                            last.then_inc(mm_done, 1)
                    then(k)

            def pre_first(tag, s):
                def then(k):
                    if k >= 1:
                        sums(tag, k - 1, 0, k == 1, False)
                    if k == KT - 1:
                        sums(tag, k, 0, False, True)
                first_unit(s, lambda k: pe.wait_ge(*at(f"{tag}.u{k}")), then)

            def stream2(name, aH=hH, aL=hL, more=None, first=None, peel=0):
                n0 = UNIT0[name]
                if first is None:
                    begin(name)
                for i in ev.loop(pe, looped(name, 2), peel=1 if first else peel):
                    for s in range(2):
                        pe.wait_ge(w_split, i * 2 + (n0 + s + 1))
                        if first and peeled(i) and s == 0:
                            begin(name)
                            if first == "mlp2":
                                first_unit(0, lambda k: pe.wait_ge(*at(f"dn_out.u{k % 4}", k // 4)), lambda k: None)
                                norm_sums("mlp2", "dn_out", 2)
                            else:
                                pre_first(first, 0)
                            continue

                        def wait(tl):
                            if first and peeled(i) and tl == 1:
                                spread(first)
                            tile_wait(name, i * 4 + (2 * s + tl))
                        unit_tiles(s, KT, aH, aL, 2 * s, wait=wait)
                        if more is not None:
                            more(i, s)

            def stream_down(name, kt):
                n0 = UNIT0[name]
                begin(name)
                for i in ev.loop(pe, looped(name, 4)):
                    for a in range(4):
                        pe.wait_ge(w_split, i * 4 + (n0 + a + 1))
                        tile_wait(name, i * 4 + a)
                        unit_tiles(a % 2, kt, mH, mL, a, tiles=1, cols=P)

            def unit_tokens(s, b0, l0, wait):
                for t in range(TT):
                    wait(l0 + t)
                    for k in range(KT):
                        c = slice(k * 256, k * 256 + 256)
                        last = three(bank[(b0 + t) % 4][:, 0:256], (wH[s][:, c], wL[s][:, c]),
                                     (hH[:, k, t * P:(t + 1) * P], hL[:, k, t * P:(t + 1) * P]),
                                     k == 0, k == KT - 1, swap=True)
                    last.then_inc(mm_done, 1)

            def sums(tag, k, col, first, ticked):
                pe.wait_ge(*at(f"{tag}.sq{k}"))
                for t in range(TT):
                    last = mm(bank[7][:, col + t:col + t + 1], sq[:, k % 2, t * P:(t + 1) * P], ones[:, 0:1],
                              start=first and t == 0, stop=ticked, skip_group_check=True)
                last.then_inc(*tick("sums_pe", f"{tag}.sum{k}"))

            def spread(tag, b=6):
                pe.wait_ge(*at(f"{tag}.diag"))
                mm(bank[b][:], ones, dg[:].rearrange("p t n -> p (t n)"), start=True, stop=True)\
                    .then_inc(*tick("spread_pe", f"{tag}.spread"))

            def norm_sums(tag, name, per):
                pe.wait_ge(*at(f"{name}.tile3.ss", looped(name, per) - 1))
                for t in range(TT):
                    last = mm(bank[7][:, t:t + 1], ss[:, t * P:(t + 1) * P], ones[:, 0:1], start=True, stop=True)
                last.then_inc(*tick("sums_pe", f"{tag}.sum{KT - 1}"))

            def norm_summed(tag, name, per):
                norm_sums(tag, name, per)
                spread(tag)

            def attention(name, q, k, val, pbuf, W, masked, rows, M):
                def scores(h):
                    for i in range(TT):
                        for w in range(W):
                            j = (h * TT + i) * W + w
                            if j >= 4:
                                pe.wait_ge(*at(f"{name}.biased{j - 4}"))
                            n = P * (i + 1)
                            last = mm(bank[j % 4][:, 0:n], q(h, w)[:, i * P:n], k(h, w)[:, 0:n],
                                      start=True, stop=not masked)
                            if masked:
                                last = mm(bank[j % 4][:, i * P:n], ident, window[:, FAR:], start=False, stop=True)
                            last.then_inc(*tick(f"{name}_pe", f"{name}.scores{j}"))

                def turn(h):
                    for i in range(TT):
                        ti = h * TT + i
                        pe.wait_ge(*at(f"{name}.prob{h}.{i}"))
                        if ti >= 2:
                            pe.wait_ge(*at(f"{name}.copied{ti - 2}"))
                        for j in range(i + 1):
                            last = nc.tensor.transpose(bank[4 + ti % 2][:, j * P:(j + 1) * P],
                                                       ptile(h, i, pbuf(h, 0))[:, j * P:(j + 1) * P], ident)
                        last.then_inc(*tick(f"{name}_pe", f"{name}.turned{ti}"))

                def values(h):
                    pe.wait_ge(*at(f"{name}.copied{h * TT + TT - 1}"))
                    if h >= 2:
                        pe.wait_ge(*at(f"{name}.out{h - 2}"))
                    for j in range(TT):
                        last = mm(bank[6 + h % 2][rows(h), j * P:], val(h, j), PT[:, h % 2, j, j * P:],
                                  start=j == 0, stop=j == TT - 1)
                    last.then_inc(*tick(f"{name}_pe", f"{name}.values{h}"))

                scores(0)
                scores(1)
                for h in range(H):
                    turn(h)
                    if h + 2 < H:
                        scores(h + 2)
                    values(h)

            pe.wait_ge(*at("in.x"))
            pe.wait_ge(*at("in.const"))
            for k in range(KT):
                if k >= 4:
                    pe.wait_ge(*at(f"x0.{k - 4}"))
                for t in range(TT):
                    last = nc.tensor.transpose(bank[2 + k % 4][:, t * P:(t + 1) * P], xin[:, t, k * P:(k + 1) * P], ident)
                last.then_inc(*tick("input_pe", f"x0.turned{k}"))

            pe.wait_ge(w_split, 1)
            pre_first("mix_pre0", 0)
            for u in range(1, 7):
                pe.wait_ge(w_split, u + 1)
                b0 = 2 * (u % 2)

                def wait(tl):
                    if u == 1 and tl == 1:
                        spread("mix_pre0")
                    if 2 * u + tl >= 4:
                        pe.wait_ge(evac, 2 * u + tl - 3)
                unit_tiles(u % 2, KT, hH, hL, b0, wait=wait)
                if u == 3:
                    for k in range(3):
                        sums("cq", k, 0, k == 0, k == 2)
                    for k in range(3, 5):
                        sums("cq", k, 4, k == 3, k == 4)
                if u == 5:
                    pe.wait_ge(*at("cq.diag"))
                    mm(bank[5][:], ones, y[:, 5, :], start=True, stop=True)\
                        .then_inc(*tick("spread_pe", "cq.spread"))
                    pe.wait_ge(*at("ckv.diag"))
                    mm(bank[4][:], ones, y[:, 6, :], start=True, stop=True).then_inc(*tick("spread_pe", "ckv.spread"))
            for c in range(2):
                u = 7 + c
                pe.wait_ge(w_split, u + 1)
                unit_tokens(u % 2, 2, 14 + 4 * c, lambda l: pe.wait_ge(evac, l - 3))
            pe.wait_ge(*at("gate.rows"))
            pe.wait_ge(*at("cq.h4"))
            for h in range(H):
                if h >= 4:
                    pe.wait_ge(*at(f"gate.bias{h - 4}"))
                mm(bank[4 + h % 4][:], ident[0:H, h:h + 1].to_broadcast([H, P]), prob[0:H, 1, 512:1024],
                   start=True, stop=True).then_inc(*tick("gate_pe", f"gate.spread{h}"))
            pe.wait_ge(evac, TILE0["even_uq"])
            pe.wait_ge(*at(f"gate.bias{H - 1}"))

            def half(h):
                return slice(64 * (h % 2), 64 * (h % 2) + 64)
            attention("fox", lambda h, w: qF[half(h), h // 2, :], lambda h, w: kF[half(h), h // 2, :],
                      lambda h, j: vF[:, j, 64 * h:64 * h + 64], lambda h, w: prob[:, h % 2, :], 1, True, half, 64)

            pe.wait_ge(*at(f"fox.out{H - 1}"))
            for u in range(2):
                n = UNIT0["even_uq"] + u
                pe.wait_ge(w_split, n + 1)
                for hh in range(4):
                    l = 4 * u + hh
                    if l >= 4:
                        tile_wait("even_uq", l)
                    for k in range(3):
                        c = slice(k * 384 + hh * 96, k * 384 + hh * 96 + 96)
                        last = three(bank[l % 4][0:96, :], (wH[n % 2][:, c], wL[n % 2][:, c]),
                                     (cqH[:, k, :], cqL[:, k, :]), k == 0, k == 2)
                    last.then_inc(mm_done, 1)

            def turn_rotary(r):
                if r == 0:
                    pe.wait_ge(*at("in.rope"))
                    src = misc[0:96, :]
                else:
                    pe.wait_ge(evac, TILE0["even_uq"] + r)
                    src = qM[0:96, r - 1, :]
                if r >= 2:
                    pe.wait_ge(*at(f"rope.sin{r - 2}"))
                mm(bank[4 + r % 2][64:96, :], rope[0:96, 1024:1056], src, start=True, stop=True)\
                    .then_inc(*tick("rope_pe", f"rope.turned{r}"))
            turn_rotary(0)
            turn_rotary(1)
            n = UNIT0["even_ukv"]
            pe.wait_ge(w_split, n + 1)
            for h in range(H):
                tile_wait("even_ukv", h)
                for k in range(2):
                    c = slice(k * DM + h * P, k * DM + h * P + P)
                    last = three(bank[h % 4][:], (wH[n % 2][:, c], wL[n % 2][:, c]),
                                 (cqH[:, 3 + k, :], cqL[:, 3 + k, :]), k == 0, k == 1)
                last.then_inc(mm_done, 1)
                if h + 2 <= H:
                    turn_rotary(h + 2)
            for t in range(TT):
                tile_wait("even_ukv", H + t)
                for k in range(2):
                    c = slice(k * DM, (k + 1) * DM)
                    wv = [w[n % 2][:, c].rearrange("p (h d) -> p h d", h=H)[:, :, 64:] for w in (wH, wL)]
                    tk = slice(t * P, (t + 1) * P)
                    last = three(bank[t % 4][:], wv, (cqH[:, 3 + k, tk], cqL[:, 3 + k, tk]), k == 0, k == 1, swap=True)
                last.then_inc(mm_done, 1)
            pe.wait_ge(evac, TILE0["even_out"])
            pe.wait_ge(*at("rope.k"))
            pe.wait_ge(*at(f"rope.q{H - 1}"))
            attention("mla", lambda h, w: qM[0:96, h, :], lambda h, w: kM[0:96, h, :],
                      lambda h, j: vM[:, j, 64 * h:64 * h + 64], lambda h, w: prob[:, h % 2, :], 1, False, half, 64)
            pe.wait_ge(*at(f"mla.out{H - 1}"))
            stream2("even_out")

            def ffn(l):
                norm_summed(f"mix_post{l}", "even_out" if l == 0 else "odd_out", 2)
                for g in range(2):
                    stream2(f"ffn{l}_up{g}", first=f"ffn_pre{l}" if g == 0 else None)
                    pe.wait_ge(*at(f"ffn{l}_up{g}.lo1", looped(f"ffn{l}_up{g}", 2) - 1))
                    stream_down(f"ffn{l}_down{g}", FF_GROUPS[g])
                norm_summed(f"ffn_post{l}", f"ffn{l}_down1", 4)

            ffn(0)

            stream2("odd_q", first="mix_pre1")
            stream2("odd_k")
            begin("odd_v")
            n0 = UNIT0["odd_v"]
            for i in ev.loop(pe, looped("odd_v", 2)):
                for s in range(2):
                    pe.wait_ge(w_split, i * 2 + (n0 + s + 1))
                    unit_tokens(s, 0, 4 * s, lambda l: tile_wait("odd_v", i * 8 + l))
            begin("odd_out")

            def two(w):
                return slice(64 * w, 64 * w + 64)
            attention("diff", lambda h, w: qO[two(w), h, :], lambda h, w: kO[two(w), h, :],
                      lambda h, j: vO[:, j, P * h:P * h + P], lambda h, w: probO[:, h % 2, w, :], 2, False,
                      lambda h: slice(0, P), P)
            pe.wait_ge(*at(f"diff.out{H - 1}"))
            for h in range(H):
                sums("subln", h, 4 * h, True, True)
            for h in range(H):
                pe.wait_ge(*at(f"subln.diag{h}"))
                mm(bank[4 + h % 2][:], ones, y[:, h % 2, :], start=True, stop=True)\
                    .then_inc(*tick("spread_pe", f"subln.spread{h}"))
            pe.wait_ge(*at(f"subln.h{H - 1}"))
            stream2("odd_out")
            ffn(1)

            stream2("dn_qkv", first="mix2")
            pe.wait_ge(*at("dn.wba"))
            for t in range(TT):
                for k in range(KT):
                    c = slice(k * 16, k * 16 + 16)
                    last = three(bank[5][:, 16 * t:16 * t + 16], (wbaH[:, c], wbaL[:, c]),
                                 (hH[:, k, t * P:(t + 1) * P], hL[:, k, t * P:(t + 1) * P]),
                                 k == 0, k == KT - 1, swap=True)
            last.then_inc(*tick("dn_pe", "dn.ba"))

            def key_norms(i, s):
                for a in range(4):
                    pe.wait_ge(*at(f"dn.sq{s}.{a}", i))
                    for t in range(TT):
                        last = mm(bank[7][:, bass.ds(i * 32 + (16 * s + 4 * a + t), 1)],
                                  y[:, 4 + a, t * P:(t + 1) * P], ones[:, 0:1], start=True, stop=True)
                last.then_inc(*tick("sums_pe", f"dn.sum{s}"))
                if peeled(i) and s == 1:
                    pe.wait_ge(*at("dn.g"))
                    mm(bank[4][:, 0:32], dconst[:, 0:P], tok[:, 1, :], start=True, stop=True)
                    mm(bank[4][:, 32:64], dconst[:, P:2 * P], tok[:, 1, :], start=True, stop=True)\
                        .then_inc(*tick("dn_pe", "dn.gc"))
            stream2("dn_z", more=key_norms, peel=1)
            pe.wait_ge(evac, TILE0["dn_out"])
            pe.wait_ge(*at("dn.rowset"))
            nc.tensor.transpose(bank[4][0:96, 0:P], tok[:, 8:11, :].rearrange("p a b -> p (a b)"), ident)\
                .then_inc(*tick("dn_pe", "dn.rows_turned"))
            pe.wait_ge(*at("dn.rows"))
            for h0 in range(0, H, 2):
                pair = [(h0 + p, [bank[4 * p + b] for b in range(4)], tmp(p)) for p in range(2)]
                for h, b, m in pair:
                    if h >= 2:
                        pe.wait_ge(*at(f"dn.w{h - 2}"))
                    for kind in range(3):
                        for t in range(TT):
                            r = 32 * kind + 4 * h + t
                            last = mm(b[kind][:, t * P:(t + 1) * P], ident[0:96, r:r + 1].to_broadcast([96, P]),
                                      rowsT[0:96, :], start=True, stop=True)
                    last.then_inc(*tick("dn_pe", f"dn.spread{h}"))
                for h, b, m in pair:
                    pe.wait_ge(*at(f"dn.qn{h}"))
                    for t in range(TT):
                        c = slice(t * P, (t + 1) * P)
                        mm(b[0][:, c], qkv[:, 8 + h, c], m["t1"][:, c], start=True, stop=True)
                        mm(b[1][:, c], qkv[:, 8 + h, c], m["x"][:, c], start=True, stop=True)
                    pe.wait_ge(*at(f"dn.diff{h}"))
                    pe.wait_ge(*at(f"dn.e{h}"))
                    for t in range(TT):
                        c = slice(t * P, (t + 1) * P)
                        nc.tensor.transpose(b[3][:, c], qkv[:, 8 + h, c], ident)
                        last = nc.tensor.transpose(b[2][:, c], qkv[:, 16 + h, c], ident)
                    last.then_inc(*tick("dn_pe", f"dn.gram{h}"))
                for h, b, m in pair:
                    pe.wait_ge(*at(f"dn.y{h}.0"))
                    for t in range(TT):
                        c = slice(t * P, (t + 1) * P)
                        last = nc.tensor.transpose(b[0][:, c], m["y"][:, c], ident)
                    last.then_inc(*tick("dn_pe", f"dn.xt{h}"))
                for s in range(1, 6):
                    for h, b, m in pair:
                        pe.wait_ge(*at(f"dn.x{h}.{s - 1}"))
                        if s == 1:
                            pe.wait_ge(*at(f"dn.attn{h}"))
                        for t in range(TT):
                            c = slice(t * P, (t + 1) * P)
                            last = mm(b[1][:, c], m["lt"][:, c], m["x"][:, c], start=True, stop=True)
                        last.then_inc(*tick("dn_pe", f"dn.lx{h}.{s}"))
                    for h, b, m in pair:
                        pe.wait_ge(*at(f"dn.t{h}.{s}"))
                        if s == 1:
                            pe.wait_ge(*at(f"dn.tok{h}"))
                        for t in range(TT):
                            c = slice(t * P, (t + 1) * P)
                            if s < 5:
                                mm(b[2][:, c], m["y"][:, c], m["t1"][:, c], start=True, stop=True)
                            last = mm(b[3][:, c], m["t1"][:, c], m["y"][:, c], start=True, stop=True)
                        last.then_inc(*tick("dn_pe", f"dn.xx{h}.{s}"))
                for h, b, m in pair:
                    pe.wait_ge(*at(f"dn.y{h}.5"))
                    for t in range(TT):
                        c = slice(t * P, (t + 1) * P)
                        mm(b[0][:, c], m["y"][:, c], qkv[:, 16 + h, c], start=True, stop=True)
                        last = mm(b[1][:, c], m["r"][:, c], m["y"][:, c], start=True, stop=True)
                    last.then_inc(*tick("dn_pe", f"dn.uw{h}"))
            pe.wait_ge(*at(f"dn.w{H - 2}"))
            pe.wait_ge(*at(f"dn.w{H - 1}"))
            for n in range(8):
                t, r = n // 2, slice(64 * (n % 2), 64 * (n % 2) + 64)
                ck = slice(64 * n, 64 * n + 64)
                for g in range(2):
                    pe.wait_ge(*at(f"scan.state{n - 1}.{g}"))
                    for hh in range(4):
                        h = 4 * g + hh
                        last = mm(bank[g][r, hh * P:(hh + 1) * P], qkv[:, 8 + h, ck], S[:, h, :], start=True, stop=True)
                    last.then_inc(*tick("scan_pe", f"scan.ws{n}.{g}"))
                if n >= 2:
                    pe.wait_ge(*at(f"scan.o{n - 2}"))
                for h in range(H):
                    mm(bank[4 + n % 2][:, 64 * h:64 * h + 64], S[:, h, :], qkv[:, h, ck],
                       start=h == 0, stop=False, skip_group_check=True)
                for g in range(2):
                    pe.wait_ge(*at(f"scan.vn{n}.{g}"))
                    for hh in range(4):
                        h = 4 * g + hh
                        mm(bank[4 + n % 2][:, 64 * h:64 * h + 64], vN[r, h, :],
                           attnT[r, h, t * P + r.start:t * P + r.stop], start=False, stop=True, skip_group_check=True)
                        last = mm(bank[2 + g][:, hh * P:(hh + 1) * P], kdec[r, h, t * P:(t + 1) * P], vN[r, h, :],
                                  start=True, stop=True)
                    last.then_inc(*tick("scan_pe", f"scan.kv{n}.{g}"))
            for h in range(H):
                sums("gated", h, 4 * h, True, True)
            for h in range(H):
                pe.wait_ge(*at(f"gated.diag{h}"))
                mm(bank[4 + h % 2][:], ones, y[:, h % 2, :], start=True, stop=True)\
                    .then_inc(*tick("spread_pe", f"gated.spread{h}"))
            pe.wait_ge(*at(f"gated.h{H - 1}"))
            stream2("dn_out", oH, oL)
            for g in range(2):
                stream2(f"mlp_up{g}", first="mlp2" if g == 0 else None)
                pe.wait_ge(*at(f"mlp_up{g}.lo3", looped(f"mlp_up{g}", 2) - 1))
                stream_down(f"mlp_down{g}", MLP_GROUP)
            stream_down("mlp_down2", MLP_GROUP)
            norm_summed("final", "mlp_down2", 4)
            for t in range(TT):
                for half_ in range(2):
                    b = (2 * t + half_) % 4
                    if t >= 2:
                        pe.wait_ge(*at(f"out.copied{t - 2}"))
                    for kk in range(4):
                        k = 4 * half_ + kk
                        if t == 0:
                            pe.wait_ge(*at(f"final.t{k}"))
                        last = nc.tensor.transpose(bank[b][:, kk * P:(kk + 1) * P], y[:, k, t * P:(t + 1) * P], ident)
                    last.then_inc(*tick("out_pe", f"out.turned{t}.{half_}"))

        @block.scalar
        def _(act):
            def a(out, in_, func, **kw):
                return nc.scalar.activation(out, in_, func, **kw)

            def hi(n, half_n, s):
                act.wait_ge(w_in[s], half_n * 16 + 16)
                a(wH[s][:], raw[s][:], ACT.Copy).then_inc(w_hi, 1)

            def hi_next(name, i, s, per=2, last=False, early=False):
                n0 = UNIT0[name] + s
                if last or early and peeled(i) and s == 0:
                    return
                each = TILES[name] // NUNITS[name]
                act.wait_ge(mm_done, i * (per * each) + (TILE0[name] + s * each))
                hi(None, i * (per // 2) + (n0 + 1) // 2, (n0 + 1) % 2)

            def done(name, l):
                act.wait_ge(mm_done, l + (TILE0[name] + 1))

            def evacuated(name, l):
                act.wait_ge(evac, l + (TILE0[name] + 1))

            def squares(tag, k, src, ready=None):
                if ready is not None:
                    act.wait_ge(*at(ready))
                if k >= 2:
                    act.wait_ge(*at(f"{tag}.sum{k - 2}"))
                a(sq[:, k % 2, :], src, ACT.Square).then_inc(*tick("squares_act", f"{tag}.sq{k}"))

            def root(tag, kt, n, col=0, w=TT, out=0):
                act.wait_ge(*at(f"{tag}.sum{kt - 1}"))
                return a(small[:, out:out + w], bank[7][:, col:col + w], ACT.Sqrt, bias=eps, scale=1.0 / n)

            def his(tag, kt, H_=hH, slots=4, src=lambda k: y[:, k % 4, :], k0=0):
                for k in range(kt):
                    act.wait_ge(*at(f"{tag}.t{k0 + k}"))
                    a(H_[:, k0 + k, :], src(k), ACT.Copy).then_inc(*tick("norm_act", f"{tag}.hi{k0 + k}"))

            def hi_early(name):
                act.wait_ge(mm_done, TILE0[name])
                n = UNIT0[name] + 1
                hi(None, n // 2, n % 2)

            def pre(tag, ready):
                for k in range(KT):
                    ready(k)
                    a(hH[:, k, :], x[:, k, :], ACT.Copy, scale=v(tag, k)).then_inc(*tick("norm_act", f"{tag}.hi{k}"))
                    squares(tag, k, x[:, k, :])
                root(tag, KT, DM).then_inc(*tick("norm_act", f"{tag}.root"))

            def stream_plain(name, early=False):
                for i in ev.loop(act, looped(name, 2), peel=int(early)):
                    for s in range(2):
                        hi_next(name, i, s, early=early)

            def tile_out(name, i, a_, mode, t0=0):
                tag = f"{name}.tile{a_}"
                yt = y[:, bass.ds(i * 4 + (a_ + t0), 1), :]
                xt = x[:, bass.ds(i * 4 + (a_ + t0), 1), :]
                if mode == "y0":
                    done(name, i * 4 + a_)
                    a(yt, bank[a_][:].unsqueeze(1), ACT.Copy).then_inc(evac, 1)
                    return
                if mode == "x0":
                    return
                if mode == "y":
                    done(name, i * 4 + a_)
                    src = bank[a_][:].unsqueeze(1)
                else:
                    evacuated(name, i * 4 + a_)
                    src = yt if mode == "y1" else xt
                act.wait_ge(*(at(f"{name}.tile{a_ - 2}.ss", i) if a_ >= 2 else at(f"{name}.tile{a_ + 2}.ss", i - 1)))
                a(sq[:, a_ % 2, :].unsqueeze(1), src, ACT.Square).then_inc(*tick("out_act", f"{tag}.sq"))
                if mode == "y":
                    a(yt, src, ACT.Copy).then_inc(evac, 1)
                if name == "dn_out":
                    a(hH[:, bass.ds(i * 4 + a_, 1), :], xt, ACT.Copy, scale=vr("mlp2", i * 4 + a_))\
                        .then_inc(*tick("out_act", f"{tag}.hi"))

            def stream_out2(name, mode):
                for i in ev.loop(act, looped(name, 2)):
                    for s in range(2):
                        hi_next(name, i, s)
                        for tl in range(2):
                            tile_out(name, i, 2 * s + tl, mode)

            def stream_down(name, mode, last=False, t0=0):
                for i in ev.loop(act, looped(name, 4)):
                    for a_ in range(4):
                        hi_next(name, i, a_, per=4, last=last and a_ == 3)
                        tile_out(name, i, a_, mode, t0)

            def attention(name, pbuf, W, out_rows, out_tile, diff=False):
                def exps(h):
                    act.wait_ge(*at(f"{name}.minus_max{h}"))
                    for i in range(TT):
                        for w in range(W):
                            p_ = ptile(h, i, pbuf(h, w))
                            c = 16 * (h % 2) + 4 * w + i
                            a(p_, p_, ACT.Exp, bias=small[:, c:c + 1], accum_out=small[:, c + 32:c + 33])\
                                .then_inc(*tick(f"{name}_act", f"{name}.exp{h}.{i}.{w}"))

                def copies(h):
                    for i in range(TT):
                        ti = h * TT + i
                        act.wait_ge(*at(f"{name}.turned{ti}"))
                        if h >= 2:
                            act.wait_ge(*at(f"{name}.values{h - 2}"))
                        a(PT[:, h % 2, 0:i + 1, i * P:(i + 1) * P],
                          bank[4 + ti % 2][:, 0:P * (i + 1)].rearrange("p (j n) -> p j n", n=P), ACT.Copy)\
                            .then_inc(*tick(f"{name}_act", f"{name}.copied{ti}"))

                def out(h):
                    act.wait_ge(*at(f"{name}.values{h}"))
                    if diff:
                        a(qO[:, h, :], bank[6 + h % 2][:], ACT.Copy).then_inc(*tick(f"{name}_act", f"{name}.out{h}"))
                    else:
                        r = out_rows(h)
                        a(hH[r, out_tile(h), :], bank[6 + h % 2][r, :], ACT.Copy)\
                            .then_inc(*tick(f"{name}_act", f"{name}.hi{h}"))

                exps(0)
                for h in range(H):
                    if h + 1 < H:
                        exps(h + 1)
                    copies(h)
                    if h >= 1:
                        out(h - 1)
                out(H - 1)

            act.wait_ge(*at("in.eps"))
            act.wait_ge(*at("in.vec"))

            def input_ready(k):
                if k == 2:
                    hi(0, 0, 0)
                act.wait_ge(*at(f"x0.{k}"))
            pre("mix_pre0", input_ready)
            hi(1, 0, 1)

            act.dma_start(rope[:], dram["rope"]).then_inc(*tick("loaded_rope", "in.rope", 16))

            for u in range(9):
                if u >= 1:
                    act.wait_ge(mm_done, 2 * u if u < 8 else 18)
                    hi(u + 1, (u + 1) // 2, (u + 1) % 2)
                if u == 2:
                    act.wait_ge(evac, 1)
                    a(prob[0:H, 0, 0:512], misc[0:H, :], ACT.Abs, bias=v("b_forget")[0:H, :])\
                        .then_inc(*tick("gate_act", "gate.abs"))
                    act.wait_ge(*at("gate.abs"))
                    a(prob[0:H, 0, 0:512], prob[0:H, 0, 0:512], ACT.Exp, scale=-1.0).then_inc(*tick("gate_act", "gate.exp"))
                    act.wait_ge(*at("gate.exp"))
                    a(prob[0:H, 0, 0:512], prob[0:H, 0, 0:512], ACT.Ln, bias=1.0).then_inc(*tick("gate_act", "gate.ln"))
                    act.wait_ge(evac, 6)
                    for k in range(2):
                        squares("cq", k, y[:, k, :])
                if u == 3:
                    for k in range(2, 5):
                        squares("cq", k, y[:, k, :])
                    root("cq", 5, 384)
                    root("cq", 5, 256, col=4, out=4).then_inc(*tick("norm_act", "cq.root"))
                if u == 6:
                    his("cq", 5, cqH, src=lambda k: y[:, k, :])
            for h in range(H):
                act.wait_ge(*at(f"gate.spread{h}"))
                a(cB[:, h, :], bank[4 + h % 4][:], ACT.Copy).then_inc(*tick("gate_act", f"gate.bias{h}"))

            def half(h):
                return slice(64 * (h % 2), 64 * (h % 2) + 64)
            attention("fox", lambda h, w: prob[:, h % 2, :], 1, half, lambda h: h // 2)
            for u in range(3):
                n = UNIT0["even_uq"] + u
                act.wait_ge(mm_done, TILE0["even_uq"] + 4 * u)
                hi(n + 1, (n + 1) // 2, (n + 1) % 2)
                if u < 2:
                    for hh in range(4):
                        h = 4 * u + hh
                        done("even_uq", h)
                        a(qM[0:96, h, :], bank[h % 4][0:96, :], ACT.Copy, scale=96.0 ** -0.5)\
                            .then_inc(evac, 1)
                else:
                    for h in range(H):
                        done("even_ukv", h)
                        a(kM[0:64, h, :], bank[h % 4][0:64, :], ACT.Copy).then_inc(evac, 1)
                    for t in range(TT):
                        done("even_ukv", H + t)
                        a(vM[:, t, :], bank[t % 4][:], ACT.Copy).then_inc(evac, 1)
            attention("mla", lambda h, w: prob[:, h % 2, :], 1, half, lambda h: 4 + h // 2)
            stream_out2("even_out", "y")

            def norm_summed(tag):
                root(tag, KT, DM).then_inc(*tick("norm_act", f"{tag}.root"))

            def ffn(l):
                norm_summed(f"mix_post{l}")
                hi_early(f"ffn{l}_up0")
                pre(f"ffn_pre{l}", lambda k: act.wait_ge(*at(f"mix_post{l}.x{k}")))
                for g in range(2):
                    name = f"ffn{l}_up{g}"
                    m0 = FF_GROUPS[0] * g
                    for i in ev.loop(act, looped(name, 2), peel=int(g == 0)):
                        for s in range(2):
                            hi_next(name, i, s, early=g == 0)
                            m = i * 2 + (m0 + s)
                            evacuated(name, i * 4 + 2 * s)
                            a(ft[:, s, :], ft[:, 6 + s, :], ACT.Identity, bias=vr(f"conv{l}", m + 3 * FF_T),
                              scale=vr(f"conv{l}", m + 2 * FF_T)).then_inc(*tick(f"ffn_act", f"{name}.tap2.{s}"))
                            act.wait_ge(*at(f"{name}.tap0.{s}", i))
                            a(ft[:, 2 + s, :], ft[:, s, :], ACT.Gelu_apprx_tanh).then_inc(*tick("ffn_act", f"{name}.gelu{s}"))
                            act.wait_ge(*at(f"{name}.mid{s}", i))
                            a(mH[:, bass.ds(i * 2 + s, 1), :], ft[:, 4 + s, :].unsqueeze(1), ACT.Copy)\
                                .then_inc(*tick("ffn_act", f"{name}.hi{s}"))
                    stream_down(f"ffn{l}_down{g}", "y0" if g == 0 else "y1")
                norm_summed(f"ffn_post{l}")

            ffn(0)

            hi_early("odd_q")
            pre("mix_pre1", lambda k: act.wait_ge(*at(f"ffn_post0.x{k}")))
            act.dma_start(dist[:], dram["dist"]).then_inc(*tick("loaded_dist", "in.dist", 16))
            act.wait_ge(*at("lam.dots"))
            a(lamt[:, 66:68], lamt[:, 64:66], ACT.Exp).then_inc(*tick("lam_act", "lam.exp"))
            stream_plain("odd_q", early=True)
            stream_plain("odd_k")
            stream_plain("odd_v")
            attention("diff", lambda h, w: probO[:, h % 2, w, :], 2, None, None, diff=True)
            for h in range(H):
                squares("subln", h, qO[:, h, :], f"diff.out{h}")
            root("subln", H, P, w=32).then_inc(*tick("norm_act", "subln.root"))
            his("subln", H, src=lambda k: y[:, 2 + k % 4, :])
            stream_out2("odd_out", "y")
            ffn(1)

            hi_early("dn_qkv")
            pre("mix2", lambda k: act.wait_ge(*at(f"ffn_post1.x{k}")))
            act.dma_start(dconst[:], dram["dconst"]).then_inc(*tick("loaded_dconst", "in.dconst", 16))
            act.dma_start(wba[:], dram["wba"]).then_inc(*tick("loaded_wba", "in.wba", 16))
            for i in ev.loop(act, looped("dn_qkv", 2), peel=1):
                for s in range(2):
                    hi_next("dn_qkv", i, s, early=True)
                    for tl in range(2):
                        c = 2 * s + tl
                        evacuated("dn_qkv", i * 4 + c)
                        a(y[:, c, :], y[:, 4 + c, :], ACT.Copy, scale=vr("dn_conv", i * 4 + (c + 72)))\
                            .then_inc(*tick("dn_conv_act", f"dn.tap3.{c}"))
                    for tl in range(2):
                        c = 2 * s + tl
                        act.wait_ge(*at(f"dn.tap0.{c}", i))
                        a(qkv[:, bass.ds(i * 4 + c, 1), :], y[:, c, :].unsqueeze(1), ACT.Silu)\
                            .then_inc(*tick("dn_conv_act", f"dn.silu{c}"))
                if peeled(i):
                    act.wait_ge(*at("in.wba"))
                    a(wbaH[:], wba[:], ACT.Copy).then_inc(*tick("dn_act", "dn.wba_hi"))
            act.wait_ge(*at("dn.z"))
            a(tok[:, 0, :].rearrange("p (h t) -> p t h", t=TT), zed[:, :, 8:16], ACT.Sigmoid).then_inc(*tick("dn_act", "dn.beta"))
            za = zed[:].rearrange("p t (w h) -> p t w h", w=2)
            act.wait_ge(*at("dn.beta"))
            a(za[:, :, 1, :], za[:, :, 0, :], ACT.Abs).then_inc(*tick("dn_act", "dn.abs"))
            act.wait_ge(*at("dn.abs"))
            a(za[:, :, 1, :], za[:, :, 1, :], ACT.Exp, scale=-1.0).then_inc(*tick("dn_act", "dn.expabs"))
            a(tok[:, 12, 0:8], v("a_log", 0, 8), ACT.Exp).then_inc(*tick("dn_act", "dn.expa"))
            act.wait_ge(*at("dn.expabs"))
            a(za[:, :, 1, :], za[:, :, 1, :], ACT.Ln, bias=1.0).then_inc(*tick("dn_act", "dn.ln"))
            for i in ev.loop(act, looped("dn_z", 2), peel=1):
                for s in range(2):
                    hi_next("dn_z", i, s)
                    for a_ in range(4):
                        if a_ == 0:
                            act.wait_ge(*(at("dn.sum0", i) if s else at("dn.sum1", i - 1)))
                        a(y[:, 4 + a_, :].unsqueeze(1), qkv[:, bass.ds(i * 8 + (4 * s + a_), 1), :], ACT.Square)\
                            .then_inc(*tick("dn_sq_act", f"dn.sq{s}.{a_}"))
                    for tl in range(2):
                        c = 2 * s + tl
                        evacuated("dn_z", i * 4 + c)
                        a(zT[:, bass.ds(i * 4 + c, 1), :], y[:, c, :].unsqueeze(1), ACT.Silu).then_inc(*tick("dn_z_act", f"dn.silu_z{c}"))
                if peeled(i):
                    act.wait_ge(*at("dn.gc"))
                    a(tok[:, 2, :], bank[4][:, 0:32], ACT.Copy).then_inc(*tick("dn_act", "dn.gc_copied"))
                    a(tok[:, 3, :], bank[4][:, 32:64], ACT.Copy).then_inc(*tick("dn_act", "dn.tot_copied"))
            act.wait_ge(*at("dn.sum1", looped("dn_z", 2) - 1))
            a(tok[:, 14:16, :].rearrange("p a b -> p (a b)"), bank[7][:, 0:64], ACT.Sqrt, bias=eps)\
                .then_inc(*tick("dn_act", "dn.root"))
            a(tok[:, 4, :], tok[:, 2, :], ACT.Exp).then_inc(*tick("dn_act", "dn.egc"))
            act.wait_ge(*at("dn.left"))
            a(tok[:, 5, :], tok[:, 5, :], ACT.Exp).then_inc(*tick("dn_act", "dn.eleft"))
            act.wait_ge(*at("dn.rows_turned"))
            a(rowsT[0:96, :], bank[4][0:96, 0:P], ACT.Copy).then_inc(*tick("dn_act", "dn.rows"))
            for h0 in range(0, H, 2):
                pair = [(h0 + p, [bank[4 * p + b] for b in range(4)], tmp(p)) for p in range(2)]
                for h, b, m in pair:
                    act.wait_ge(*at(f"dn.spread{h}"))
                    if h >= 2:
                        act.wait_ge(*at(f"dn.qdec{h - 2}"))
                    a(m["e"], b[2][:], ACT.Exp).then_inc(*tick("dn_act", f"dn.e{h}"))
                    act.wait_ge(*at(f"dn.diff{h}"))
                    a(m["lt"], m["lt"], ACT.Exp).then_inc(*tick("dn_act", f"dn.dec{h}"))
                    act.wait_ge(*at(f"dn.e{h}"))
                    a(gl[:, h, :], m["e"][:, 63::64], ACT.Copy).then_inc(*tick("dn_act", f"dn.gl{h}"))
                for h, b, m in pair:
                    act.wait_ge(*at(f"dn.gram{h}"))
                    for t in range(TT):
                        c, r = slice(t * P, (t + 1) * P), 4 * h + t
                        a(m["r"][:, c], b[3][:, c], ACT.Copy, scale=tok[:, 6, r:r + 1])
                        a(kdec[:, h, c], b[3][:, c], ACT.Copy, scale=tok[:, 7, r:r + 1])
                        last = a(qkv[:, 16 + h, c], b[2][:, c], ACT.Copy, scale=tok[:, 0, r:r + 1])
                    last.then_inc(*tick("dn_act", f"dn.tok{h}"))
                for h, b, m in pair:
                    act.wait_ge(*at(f"dn.xt{h}"))
                    act.wait_ge(*at(f"dn.qdec{h}"))
                    a(m["x"], b[0][:], ACT.Copy).then_inc(*tick("dn_act", f"dn.x{h}.0"))
                for h, b, m in pair:
                    act.wait_ge(*at(f"dn.uw{h}"))
                    a(qkv[:, 16 + h, :], b[0][:], ACT.Copy)
                    a(qkv[:, 8 + h, :], b[1][:], ACT.Copy).then_inc(*tick("dn_act", f"dn.w{h}"))
            for n in range(8):
                act.wait_ge(*at(f"scan.kv{n}.1"))
                a(qkv[:, 0:H, 64 * n:64 * n + 64], bank[4 + n % 2][:].rearrange("p (h c) -> p h c", h=H), ACT.Copy)\
                    .then_inc(*tick("scan_act", f"scan.o{n}"))
            for h in range(H):
                squares("gated", h, qkv[:, h, :], "scan.o7")
            root("gated", H, P, w=32).then_inc(*tick("norm_act", "gated.root"))
            his("gated", H, oH, src=lambda k: y[:, 4 + k % 4, :])
            stream_out2("dn_out", "x1")
            hi_early("mlp_up0")
            norm_summed("mlp2")
            for g in range(2):
                name = f"mlp_up{g}"
                for i in ev.loop(act, looped(name, 2), peel=int(g == 0)):
                    for s in range(2):
                        hi_next(name, i, s, early=g == 0)
                        for tl in range(2):
                            c = 2 * s + tl
                            act.wait_ge(*at(f"{name}.mid{c}", i))
                            a(mH[:, bass.ds(i * 4 + c, 1), :], y[:, 4 + c, :].unsqueeze(1), ACT.Copy)\
                                .then_inc(*tick("mlp_act", f"{name}.hi{c}"))
                stream_down(f"mlp_down{g}", ("x0", "x1")[g])
            stream_down("mlp_down2", "x1", last=True, t0=4)
            norm_summed("final")
            for t in range(TT):
                act.wait_ge(*at(f"out.turned{t}.0"))
                a(xin[:, t, 0:512], bank[(2 * t) % 4][:], ACT.Copy)
                act.wait_ge(*at(f"out.turned{t}.1"))
                a(xin[:, t, 512:1024], bank[(2 * t + 1) % 4][:], ACT.Copy).then_inc(*tick("out_act", f"out.copied{t}"))

        @block.vector
        def _(dve):
            tt, ts, stt = nc.vector.tensor_tensor, nc.vector.tensor_scalar, nc.vector.scalar_tensor_tensor

            def chain(ins, name, event, i=None):
                ins.then_inc(*tick(name, event))
                dve.wait_ge(*at(event, i))

            def lo(n, s):
                dve.wait_ge(w_hi, n + 1)
                tt(wL[s][:], raw[s][:], wH[s][:].bitcast(F32), ALU.subtract).then_inc(w_split, 1)

            def lo_next(name, i, s, per=2, last=False, early=False):
                if not (last or early and peeled(i) and s == 0):
                    n0 = UNIT0[name] + s
                    lo(i * per + (n0 + 1), (n0 + 1) % 2)

            def done(name, l):
                dve.wait_ge(mm_done, l + (TILE0[name] + 1))

            def diagonal(out, col):
                return tt(out.rearrange("p (t n) -> p t n", t=TT), ident.unsqueeze(1).to_broadcast([P, TT, P]),
                          stat[:, col:col + TT].unsqueeze(2).to_broadcast([P, TT, P]), ALU.mult)

            def inverse(tag):
                dve.wait_ge(*at(f"{tag}.root"))
                chain(nc.vector.reciprocal(stat[:, 0:TT], small[:, 0:TT]), "norm_dve", f"{tag}.inverse")
                diagonal(dg[:].rearrange("p t n -> p (t n)"), 0).then_inc(*tick("norm_dve", f"{tag}.diag"))
                dve.wait_ge(*at(f"{tag}.spread"))

            def inverse_kept(tag):
                inverse(tag)
                chain(nc.vector.tensor_copy(rinv, bank[6][:]), "norm_dve", f"{tag}.kept")

            def lo_tile(tag, k, src, H_=hH, L_=hL):
                dve.wait_ge(*at(f"{tag}.hi{k}"))
                tt(L_[:, k, :], src, H_[:, k, :].bitcast(F32), ALU.subtract).then_inc(*tick("norm_dve", f"{tag}.h{k}"))

            def lo_early(name):
                n = UNIT0[name] + 1
                lo(n, n % 2)

            def lo_pre(tag, k):
                dve.wait_ge(*at(f"{tag}.hi{k}"))
                stt(hL[:, k, :], x[:, k, :], v(tag, k), hH[:, k, :].bitcast(F32), ALU.mult, ALU.subtract)\
                    .then_inc(*tick("norm_dve", f"{tag}.u{k}"))

            def post_pre(post, tag, name):
                dve.wait_ge(*at(f"{post}.root"))
                chain(nc.vector.reciprocal(stat[:, 0:TT], small[:, 0:TT]), "norm_dve", f"{post}.inverse")
                diagonal(dg[:].rearrange("p t n -> p (t n)"), 0).then_inc(*tick("norm_dve", f"{post}.diag"))
                lo_early(name)
                dve.wait_ge(*at(f"{post}.spread"))
                for k in range(KT + 3):
                    if k < KT:
                        stt(y[:, k, :], y[:, k, :], v(post, k), bank[6][:], ALU.mult, ALU.mult)\
                            .then_inc(*tick("norm_dve", f"{post}.t{k}"))
                    if k >= 3:
                        lo_pre(tag, k - 3)
                inverse_kept(tag)

            def stream_scaled(name, dst, early=False, scale=1.0):
                for i in ev.loop(dve, looped(name, 2), peel=int(early or name == "dn_z")):
                    for s in range(2):
                        lo_next(name, i, s, early=early)
                        for tl in range(2):
                            c = 2 * s + tl
                            done(name, i * 4 + c)
                            if name == "dn_z":
                                if not peeled(i):
                                    dve.wait_ge(*at(f"dn.silu_z{c}", i - 1))
                            stt(dst(i, c), bank[c][:].unsqueeze(1), scale, rinv.unsqueeze(1), ALU.mult, ALU.mult)\
                                .then_inc(evac, 1)

            def clear_sums(name):
                for q in range(4):
                    last = nc.vector.memset(ss[:, q * P:(q + 1) * P], 0.0)
                    last.then_inc(*tick("sums_dve", f"{name}.clear{q}"))

            def tile_out(name, i, a_, mode, t0=0):
                tag = f"{name}.tile{a_}"
                if mode == "y0":
                    return
                if mode != "y":
                    done(name, i * 4 + a_)
                    dst = (x if mode[0] == "x" else y)[:, bass.ds(i * 4 + (a_ + t0), 1), :]
                    tt(dst, dst, bank[a_][:].unsqueeze(1), ALU.add).then_inc(evac, 1)
                    if mode == "x0":
                        return
                dve.wait_ge(*at(f"{tag}.sq", i))
                dve.wait_ge(*(at(f"{name}.tile{a_ - 1}.ss", i) if a_ else at(f"{name}.tile3.ss", i - 1)))
                tt(ss[:], ss[:], sq[:, a_ % 2, :], ALU.add).then_inc(*tick("sums_dve", f"{tag}.ss"))
                if name == "dn_out":
                    dve.wait_ge(*at(f"{tag}.hi", i))
                    k = bass.ds(i * 4 + a_, 1)
                    stt(hL[:, k, :], dst, vr("mlp2", i * 4 + a_), hH[:, k, :].bitcast(F32), ALU.mult, ALU.subtract)\
                        .then_inc(*tick("out_dve", f"{name}.u{a_}"))

            def stream_out2(name, mode):
                clear_sums(name)
                for i in ev.loop(dve, looped(name, 2)):
                    for s in range(2):
                        lo_next(name, i, s)
                        for tl in range(2):
                            tile_out(name, i, 2 * s + tl, mode)

            def stream_down(name, mode, last=False, t0=0):
                if mode in ("y1", "x1") and t0 == 0:
                    clear_sums(name)
                for i in ev.loop(dve, looped(name, 4)):
                    for a_ in range(4):
                        lo_next(name, i, a_, per=4, last=last and a_ == 3)
                        tile_out(name, i, a_, mode, t0)

            def attention(name, bias, pbuf, W, finish):
                def biased(h):
                    if name == "diff":
                        dve.wait_ge(*at(f"alibi{h}"))
                    for i in range(TT):
                        if h >= 2:
                            dve.wait_ge(*at(f"{name}.turned{(h - 2) * TT + i}"))
                        for w in range(W):
                            j = (h * TT + i) * W + w
                            n, c = P * (i + 1), 8 * (h % 2) + 4 * w + i
                            dve.wait_ge(*at(f"{name}.scores{j}"))
                            nc.vector.tensor_tensor_reduce(ptile(h, i, pbuf(h, w)), bank[j % 4][:, 0:n], bias(h, i), 1.0,
                                                           -3.0e38, ALU.add, ALU.max, stat[:, c:c + 1])\
                                .then_inc(*tick(f"{name}_dve", f"{name}.biased{j}"))
                    c = 16 * (h % 2)
                    dve.wait_ge(*at(f"{name}.biased{j}"))
                    if h >= 2:
                        dve.wait_ge(*at(f"{name}.exp{h - 2}.{TT - 1}.{W - 1}"))
                    ts(small[:, c:c + 4 * W], stat[:, c // 2:c // 2 + 4 * W], -1.0, None, ALU.mult)\
                        .then_inc(*tick(f"{name}_dve", f"{name}.minus_max{h}"))

                def divided(h):
                    c = 16 * (h % 2) + 32
                    q = 16 + 16 * (h % 2)
                    dve.wait_ge(*at(f"{name}.exp{h}.{TT - 1}.{W - 1}"))
                    chain(nc.vector.reciprocal(stat[:, q:q + 4 * W], small[:, c:c + 4 * W]), f"{name}_dve", f"{name}.inverse{h}")
                    if W == 2:
                        chain(ts(stat[:, q + 4:q + 8], stat[:, q + 4:q + 8], lamt[:, 68:69], None, ALU.mult), f"{name}_dve", f"{name}.lam{h}")
                    for i in range(TT):
                        p_ = ptile(h, i, pbuf(h, 0))
                        if W == 2:
                            p2 = ptile(h, i, pbuf(h, 1))
                            chain(ts(p2, p2, stat[:, q + 4 + i:q + 5 + i], None, ALU.mult), f"{name}_dve", f"{name}.second{h}.{i}")
                            ins = stt(p_, p_, stat[:, q + i:q + i + 1], p2, ALU.mult, ALU.add)
                        else:
                            ins = ts(p_, p_, stat[:, q + i:q + i + 1], None, ALU.mult)
                        ins.then_inc(*tick(f"{name}_dve", f"{name}.prob{h}.{i}"))

                biased(0)
                for h in range(H):
                    if h + 1 < H:
                        biased(h + 1)
                    divided(h)
                    if h >= 1:
                        finish(h - 1)
                finish(H - 1)

            nc.vector.memset(eps, EPS).then_inc(*tick("norm_dve", "in.eps"))
            dve.wait_ge(*at("in.vec"))
            dve.wait_ge(*at("in.const"))
            for k in range(KT + 2):
                if k < KT:
                    dve.wait_ge(*at(f"x0.turned{k}"))
                    nc.vector.tensor_copy(x[:, k, :], bank[2 + k % 4][:]).then_inc(*tick("input_dve", f"x0.{k}"))
                if k == 4:
                    lo(0, 0)
                if k >= 2:
                    lo_pre("mix_pre0", k - 2)
            lo(1, 1)
            inverse_kept("mix_pre0")
            nc.vector.tensor_copy(stat[:, 56:60], stat[:, 0:TT]).then_inc(*tick("norm_dve", "mix_pre0.tokens"))

            def e_tile(l, dst, b, scale=1.0):
                dve.wait_ge(mm_done, l + 1)
                stt(dst, b, scale, rinv, ALU.mult, ALU.mult).then_inc(evac, 1)

            for u in range(9):
                if u >= 1:
                    lo(u + 1, (u + 1) % 2)
                for tl in range(2 if u < 7 else 0):
                    l = 2 * u + tl
                    b = bank[2 * (u % 2) + tl][:]
                    if l == 0:
                        e_tile(l, misc[:], b)
                    elif l < 6:
                        e_tile(l, y[:, l - 1, :], b)
                    elif l < 10:
                        e_tile(l, qF[:, l - 6, :], b, 0.125)
                    else:
                        e_tile(l, kF[:, l - 10, :], b)
                if u >= 7:
                    dve.wait_ge(*at("mix_pre0.tokens"))
                    for t in range(TT):
                        l = 14 + 4 * (u - 7) + t
                        dve.wait_ge(mm_done, l + 1)
                        ts(vF[:, t, 256 * (u - 7):256 * (u - 6)], bank[(2 + t) % 4][:, 0:256], stat[:, 56 + t:57 + t], None,
                           ALU.mult).then_inc(evac, 1)
                if u == 2:
                    z, l_, one, neg = prob[0:H, 0, 512:1024], prob[0:H, 0, 0:512], prob[0:H, 1, 0:512], prob[0:H, 1, 512:1024]
                    dve.wait_ge(evac, 1)
                    nc.vector.memset(one, 1.0)
                    chain(ts(z, misc[0:H, :], v("b_forget")[0:H, :], 0.0, ALU.add, ALU.min), "gate_dve", "gate.min")
                    dve.wait_ge(*at("gate.ln"))
                    chain(tt(z, z, l_, ALU.subtract), "gate_dve", "gate.logf")
                    chain(nc.vector.tensor_tensor_scan(l_, one, z, 0.0, ALU.mult, ALU.add), "gate_dve", "gate.summed")
                    ts(neg, l_, -1.0, None, ALU.mult).then_inc(*tick("gate_dve", "gate.rows"))
                if u == 4:
                    dve.wait_ge(*at("cq.root"))
                    chain(nc.vector.reciprocal(stat[:, 0:8], small[:, 0:8]), "norm_dve", "cq.inverse")
                    diagonal(y[:, 5, :], 0).then_inc(*tick("norm_dve", "cq.diag"))
                    diagonal(y[:, 6, :], 4).then_inc(*tick("norm_dve", "ckv.diag"))
                if u == 6:
                    dve.wait_ge(*at("ckv.spread"))
                    for k in range(6):
                        if k < 5:
                            g = v("q_norm", k) if k < 3 else v("kv_norm", k - 3)
                            stt(y[:, k, :], y[:, k, :], g, bank[5 if k < 3 else 4][:], ALU.mult, ALU.mult)\
                                .then_inc(*tick("norm_dve", f"cq.t{k}"))
                        if k >= 1:
                            lo_tile("cq", k - 1, y[:, k - 1, :], cqH, cqL)

            def halves(name, tile0):
                def finish(h):
                    r = slice(64 * (h % 2), 64 * (h % 2) + 64)
                    dve.wait_ge(*at(f"{name}.hi{h}"))
                    k = tile0 + h // 2
                    tt(hL[r, k, :], bank[6 + h % 2][r, :], hH[r, k, :].bitcast(F32), ALU.subtract)\
                        .then_inc(*tick(f"{name}_dve", f"{name}.out{h}"))
                return finish
            dve.wait_ge(*at(f"gate.bias{H - 1}"))
            attention("fox", lambda h, i: cB[:, h, 0:P * (i + 1)], lambda h, w: prob[:, h % 2, :], 1, halves("fox", 0))
            cos, sin = rope[64:96, 0:512], rope[64:96, 512:1024]

            def rotary(r):
                dve.wait_ge(*at(f"rope.turned{r}"))
                if r >= 1:
                    dve.wait_ge(evac, TILE0["even_uq"] + r)
                src = misc[64:96, :] if r == 0 else qM[64:96, r - 1, :]
                t_ = y[64:96, r % 2, :]
                tt(t_, bank[4 + r % 2][64:96, :], sin, ALU.mult).then_inc(*tick("rope_dve", f"rope.sin{r}"))
                chain(tt(src, src, cos, ALU.mult), "rope_dve", f"rope.cos{r}")
                tt(src, src, t_, ALU.add).then_inc(*tick("rope_dve", "rope.key" if r == 0 else f"rope.q{r - 1}"))
            for u in range(3):
                n = UNIT0["even_uq"] + u
                lo(n + 1, (n + 1) % 2)
                if u == 1:
                    for r in range(H + 1):
                        rotary(r)
            attention("mla", lambda h, i: window[:, FAR - P * i:], lambda h, w: prob[:, h % 2, :], 1, halves("mla", 4))
            stream_out2("even_out", "y")

            def ffn(l):
                post_pre(f"mix_post{l}", f"ffn_pre{l}", f"ffn{l}_up0")
                for g in range(2):
                    name = f"ffn{l}_up{g}"
                    for i in ev.loop(dve, looped(name, 2), peel=int(g == 0)):
                        for s in range(2):
                            lo_next(name, i, s, early=g == 0)
                            m = i * 2 + (FF_GROUPS[0] * g + s)
                            c, gate, mid = ft[:, s, :], ft[:, 6 + s, :], ft[:, 4 + s, :]
                            done(name, i * 4 + 2 * s)
                            tt(gate, bank[2 * s][:], rinv, ALU.mult).then_inc(evac, 1)
                            dve.wait_ge(*at(f"{name}.tap2.{s}", i))
                            chain(stt(c[:, 1:], gate[:, 0:SEQ - 1], vr(f"conv{l}", m + FF_T), c[:, 1:], ALU.mult, ALU.add),
                                  "ffn_dve", f"{name}.tap1.{s}", i)
                            stt(c[:, 2:], gate[:, 0:SEQ - 2], vr(f"conv{l}", m), c[:, 2:], ALU.mult, ALU.add)\
                                .then_inc(*tick("ffn_dve", f"{name}.tap0.{s}"))
                            done(name, i * 4 + (2 * s + 1))
                            tt(mid, bank[2 * s + 1][:], rinv, ALU.mult).then_inc(evac, 1)
                            dve.wait_ge(*at(f"{name}.gelu{s}", i))
                            dve.wait_ge(evac, i * 4 + (2 * s + 2 + TILE0[name]))
                            tt(mid, ft[:, 2 + s, :], mid, ALU.mult).then_inc(*tick("ffn_dve", f"{name}.mid{s}"))
                            dve.wait_ge(*at(f"{name}.hi{s}", i))
                            t1 = bass.ds(i * 2 + s, 1)
                            tt(mL[:, t1, :], ft[:, 4 + s, :].unsqueeze(1), mH[:, t1, :].bitcast(F32), ALU.subtract)\
                                .then_inc(*tick("ffn_dve", f"{name}.lo{s}"))
                    stream_down(f"ffn{l}_down{g}", "y0" if g == 0 else "y1")
                if l == 0:
                    post_pre("ffn_post0", "mix_pre1", "odd_q")
                else:
                    post_pre("ffn_post1", "mix2", "dn_qkv")

            ffn(0)

            nc.vector.tensor_copy(stat[:, 56:60], stat[:, 0:TT]).then_inc(*tick("norm_dve", "mix_pre1.tokens"))
            lam = v("lam", 0, 256)
            for w, event in enumerate(("lam.first", "lam.dots")):
                o = 128 * w
                chain(nc.vector.tensor_tensor_reduce(lamt[:, 0:64], lam[:, o:o + 64], lam[:, o + 64:o + 128], 1.0, 0.0,
                                                     ALU.mult, ALU.add, lamt[:, 64 + w:65 + w]), "lam_dve", event)
            dve.wait_ge(*at("lam.exp"))
            chain(tt(lamt[:, 68:69], lamt[:, 67:68], lamt[:, 66:67], ALU.subtract), "lam_dve", "lam.difference")
            ts(lamt[:, 68:69], lamt[:, 68:69], -LAMBDA_INIT, None, ALU.add).then_inc(*tick("lam_dve", "lam.minus"))
            ts(lamt[:, 70:71], v("subln"), 1.0 - LAMBDA_INIT, None, ALU.mult).then_inc(*tick("lam_dve", "lam.gain"))
            stream_scaled("odd_q", lambda i, c: qO[:, bass.ds(i * 4 + c, 1), :], early=True, scale=0.125)
            stream_scaled("odd_k", lambda i, c: kO[:, bass.ds(i * 4 + c, 1), :])
            dve.wait_ge(*at("mix_pre1.tokens"))
            for i in ev.loop(dve, looped("odd_v", 2)):
                for s in range(2):
                    lo_next("odd_v", i, s)
                    for t in range(TT):
                        done("odd_v", i * 8 + (4 * s + t))
                        ts(vO[:, t, bass.ds(i * 512 + 256 * s, 256)], bank[t][:, 0:256], stat[:, 56 + t:57 + t], None, ALU.mult)\
                            .then_inc(evac, 1)
            dve.wait_ge(*at("lam.gain"))
            attention("diff", lambda h, i: alibi[:, h % 2, FAR - P * i:], lambda h, w: probO[:, h % 2, w, :], 2, lambda h: None)

            def head_norms(tag, src, gain, then):
                dve.wait_ge(*at(f"{tag}.root"))
                chain(nc.vector.reciprocal(stat[:, 0:32], small[:, 0:32]), "norm_dve", f"{tag}.inverse")
                for h in range(H + 1):
                    if h < H:
                        if h >= 2:
                            dve.wait_ge(*at(f"{tag}.spread{h - 2}"))
                        diagonal(y[:, h % 2, :], 4 * h).then_inc(*tick("norm_dve", f"{tag}.diag{h}"))
                    if h >= 1:
                        dve.wait_ge(*at(f"{tag}.spread{h - 1}"))
                        then(h - 1, src(h - 1), gain, bank[4 + (h - 1) % 2][:])

            def subln(h, src, gain, inv):
                stt(y[:, 2 + h % 4, :], src, gain, inv, ALU.mult, ALU.mult).then_inc(*tick("norm_dve", f"subln.t{h}"))
                lo_tile("subln", h, y[:, 2 + h % 4, :])
            head_norms("subln", lambda h: qO[:, h, :], lamt[:, 70:71], subln)
            stream_out2("odd_out", "y")
            ffn(1)

            nc.vector.tensor_copy(stat[:, 56:60], stat[:, 0:TT]).then_inc(*tick("norm_dve", "mix2.tokens"))
            for i in ev.loop(dve, looped("dn_qkv", 2), peel=1):
                for s in range(2):
                    lo_next("dn_qkv", i, s, early=True)
                    for tl in range(2):
                        c = 2 * s + tl
                        done("dn_qkv", i * 4 + c)
                        tt(y[:, 4 + c, :], bank[c][:], rinv, ALU.mult).then_inc(evac, 1)
                    for tl in range(2):
                        c = 2 * s + tl
                        dve.wait_ge(*at(f"dn.tap3.{c}", i))
                        for tap in (2, 1, 0):
                            d = 3 - tap
                            ins = stt(y[:, c, d:], y[:, 4 + c, 0:SEQ - d], vr("dn_conv", i * 4 + (c + 24 * tap)), y[:, c, d:],
                                      ALU.mult, ALU.add)
                            if tap:
                                chain(ins, "dn_conv_dve", f"dn.tap{tap}.{c}", i)
                        ins.then_inc(*tick("dn_conv_dve", f"dn.tap0.{c}"))
                if peeled(i):
                    dve.wait_ge(*at("dn.wba_hi"))
                    tt(wbaL[:], wba[:], wbaH[:].bitcast(F32), ALU.subtract).then_inc(*tick("dn_dve", "dn.wba"))
            dve.wait_ge(*at("dn.ba"))
            dve.wait_ge(*at("mix2.tokens"))
            ba = bank[5][:, 0:64].rearrange("p (t c) -> p t c", c=16)
            za = zed[:].rearrange("p t (w h) -> p t w h", w=2)
            for t in range(TT):
                stt(zed[:, t, 0:8], ba[:, t, 8:16], stat[:, 56 + t:57 + t], v("dt_bias", 0, 8), ALU.mult, ALU.add)
                last = ts(zed[:, t, 8:16], ba[:, t, 0:8], stat[:, 56 + t:57 + t], None, ALU.mult)
            last.then_inc(*tick("dn_dve", "dn.z"))
            dve.wait_ge(*at("dn.z"))
            dve.wait_ge(*at("dn.ln"))
            chain(stt(za[:, :, 0, :], za[:, :, 0, :], 0.0, za[:, :, 1, :], ALU.max, ALU.add), "dn_dve", "dn.softplus")
            stt(tok[:, 1, :].rearrange("p (h t) -> p t h", t=TT), za[:, :, 0, :], -1.0,
                tok[:, 12, 0:8].unsqueeze(1).to_broadcast([P, TT, 8]), ALU.mult, ALU.mult).then_inc(*tick("dn_dve", "dn.g"))
            stream_scaled("dn_z", lambda i, c: y[:, c:c + 1, :])
            dve.wait_ge(*at("dn.tot_copied"))
            tt(tok[:, 5, :], tok[:, 3, :], tok[:, 2, :], ALU.subtract).then_inc(*tick("dn_dve", "dn.left"))
            nc.vector.tensor_copy(tok[:, 10, :], tok[:, 2, :])
            for g in range(2):
                nc.vector.memset(S[:, 4 * g:4 * g + 4, :], 0.0).then_inc(*tick("scan_dve", f"scan.state-1.{g}"))
            dve.wait_ge(*at("dn.root"))
            roots = tok[:, 14:16, :].rearrange("p a b -> p (a b)")
            chain(nc.vector.reciprocal(roots, roots), "dn_dve", "dn.inverse")
            tt(tok[:, 8, :], tok[:, 0, :], tok[:, 15, :], ALU.mult).then_inc(*tick("dn_dve", "dn.beta_k"))
            ts(tok[:, 9, :], tok[:, 14, :], float(P) ** -0.5, None, ALU.mult).then_inc(*tick("dn_dve", "dn.rowset"))
            dve.wait_ge(*at("dn.eleft"))
            dve.wait_ge(*at("dn.rowset"))
            tt(tok[:, 6, :], tok[:, 8, :], tok[:, 4, :], ALU.mult)
            tt(tok[:, 7, :], tok[:, 15, :], tok[:, 5, :], ALU.mult).then_inc(*tick("dn_dve", "dn.scalars"))
            dve.wait_ge(*at("dn.scalars"))
            tiles = [slice(t * P, (t + 1) * P) for t in range(TT)]

            def masked(m):
                return dconst[:, m * P:(m + 1) * P].unsqueeze(1).to_broadcast([P, TT, P])

            def blocks(ap):
                return ap.rearrange("p (t n) -> p t n", t=TT)
            for h0 in range(0, H, 2):
                pair = [(h0 + p, [bank[4 * p + b] for b in range(4)], tmp(p)) for p in range(2)]
                for h, b, m in pair:
                    dve.wait_ge(*at(f"dn.spread{h}"))
                    tt(m["t1"], qkv[:, 8 + h, :], b[0][:], ALU.mult)
                    tt(m["x"], qkv[:, h, :], b[1][:], ALU.mult).then_inc(*tick("dn_dve", f"dn.qn{h}"))
                    dve.wait_ge(*at(f"dn.e{h}"))
                    for t, c in enumerate(tiles):
                        last = ts(m["lt"][:, c], b[2][:, c], tok[:, 2, 4 * h + t:4 * h + t + 1], 0.0, ALU.subtract, ALU.min)
                    last.then_inc(*tick("dn_dve", f"dn.diff{h}"))
                for h, b, m in pair:
                    dve.wait_ge(*at(f"dn.gram{h}"))
                    dve.wait_ge(*at(f"dn.causal{h}"))
                    for t, c in enumerate(tiles):
                        r = 32 + 4 * h + t
                        stt(attnT[:, h, c], b[1][:, c], roots[:, r:r + 1], m["y"][:, c], ALU.mult, ALU.mult)
                        last = stt(m["lt"][:, c], b[0][:, c], roots[:, r:r + 1], m["lt"][:, c], ALU.mult, ALU.mult)
                    chain(last, "dn_dve", f"dn.attn{h}")
                    chain(tt(blocks(m["y"]), blocks(m["lt"]), masked(2), ALU.mult), "dn_dve", f"dn.first{h}")
                    tt(blocks(m["y"]), ident.unsqueeze(1).to_broadcast([P, TT, P]), blocks(m["y"]), ALU.subtract)\
                        .then_inc(*tick("dn_dve", f"dn.y{h}.0"))
                for s in range(1, 6):
                    for h, b, m in pair:
                        dve.wait_ge(*at(f"dn.lx{h}.{s}"))
                        tt(blocks(m["t1"]), blocks(b[1][:]), masked(2 + s), ALU.mult).then_inc(*tick("dn_dve", f"dn.t{h}.{s}"))
                    for h, b, m in pair:
                        dve.wait_ge(*at(f"dn.xx{h}.{s}"))
                        dve.wait_ge(*at(f"dn.y{h}.{s - 1}"))
                        if s < 5:
                            dve.wait_ge(*at(f"dn.x{h}.{s - 1}"))
                            tt(m["x"], m["x"], b[2][:], ALU.subtract).then_inc(*tick("dn_dve", f"dn.x{h}.{s}"))
                        tt(m["y"], m["y"], b[3][:], ALU.subtract).then_inc(*tick("dn_dve", f"dn.y{h}.{s}"))
            for n in range(8):
                t, r = n // 2, slice(64 * (n % 2), 64 * (n % 2) + 64)
                for g in range(2):
                    hs = slice(4 * g, 4 * g + 4)
                    dve.wait_ge(*at(f"scan.ws{n}.{g}"))
                    if n == 0:
                        dve.wait_ge(*at(f"dn.w{H - 1}"))
                    if n >= 1:
                        dve.wait_ge(*at(f"scan.kv{n - 1}.{g}"))
                    tt(vN[r, hs, :], qkv[r, 16 + 4 * g:20 + 4 * g, t * P:(t + 1) * P],
                       bank[g][r, :].rearrange("p (h d) -> p h d", h=4), ALU.subtract).then_inc(*tick("scan_dve", f"scan.vn{n}.{g}"))
                for g in range(2):
                    dve.wait_ge(*at(f"scan.kv{n}.{g}"))
                    dve.wait_ge(*at(f"scan.state{n - 1}.{g}"))
                    for hh in range(4):
                        h = 4 * g + hh
                        last = stt(S[:, h, :], S[:, h, :], gl[:, h, n:n + 1], bank[2 + g][:, hh * P:(hh + 1) * P], ALU.mult, ALU.add)
                    last.then_inc(*tick("scan_dve", f"scan.state{n}.{g}"))

            def gated(h, src, gain, inv):
                if h >= 2:
                    dve.wait_ge(*at(f"gated.t{h - 2}"))
                stt(y[:, 2 + h % 2, :], src, gain, inv, ALU.mult, ALU.mult).then_inc(*tick("norm_dve", f"gated.n{h}"))
                if h >= 1:
                    lo_tile("gated", h - 1, y[:, 4 + (h - 1) % 4, :], oH, oL)
            head_norms("gated", lambda h: qkv[:, h, :], v("dn_norm"), gated)
            lo_tile("gated", H - 1, y[:, 4 + (H - 1) % 4, :], oH, oL)
            stream_out2("dn_out", "x1")
            lo_early("mlp_up0")
            inverse_kept("mlp2")
            for g in range(2):
                name = f"mlp_up{g}"
                for i in ev.loop(dve, looped(name, 2), peel=int(g == 0)):
                    for s in range(2):
                        lo_next(name, i, s, early=g == 0)
                        for tl in range(2):
                            c = 2 * s + tl
                            done(name, i * 4 + c)
                            tt(y[:, c, :], bank[c][:], rinv, ALU.mult).then_inc(evac, 1)
                            dve.wait_ge(evac, i * 4 + (c + 1 + TILE0[name]))
                            stt(y[:, 4 + c, :], y[:, c, :], 0.0, y[:, c, :], ALU.max, ALU.mult)\
                                .then_inc(*tick("mlp_dve", f"{name}.mid{c}"))
                            dve.wait_ge(*at(f"{name}.hi{c}", i))
                            t1 = bass.ds(i * 4 + c, 1)
                            tt(mL[:, t1, :], y[:, 4 + c, :].unsqueeze(1), mH[:, t1, :].bitcast(F32), ALU.subtract)\
                                .then_inc(*tick("mlp_dve", f"{name}.lo{c}"))
                stream_down(f"mlp_down{g}", ("x0", "x1")[g])
            stream_down("mlp_down2", "x1", last=True, t0=4)
            inverse("final")
            for k in range(KT):
                stt(y[:, k, :], x[:, k, :], v("final", k), bank[6][:], ALU.mult, ALU.mult)\
                    .then_inc(*tick("norm_dve", f"final.t{k}"))

        @block.gpsimd
        def _(pool):
            def tt(*args):
                return nc.gpsimd.tensor_tensor(*args)

            def add(tag):
                for k in range(KT):
                    pool.wait_ge(*at(f"{tag}.t{k}"))
                    tt(x[:, k, :], x[:, k, :], y[:, k, :], ALU.add).then_inc(*tick("norm_pool", f"{tag}.x{k}"))

            pool.wait_ge(*at("rope.key"))
            nc.gpsimd.tensor_copy(kM[64:96, :, :], misc[64:96, :].unsqueeze(1).to_broadcast([32, H, SEQ]))\
                .then_inc(*tick("rope_pool", "rope.k"))
            add("mix_post0")
            add("ffn_post0")
            pool.wait_ge(*at("in.dist"))
            for h in range(H):
                if h >= 2:
                    pool.wait_ge(*at(f"diff.biased{(h - 2) * 8 + 7}"))
                nc.gpsimd.tensor_scalar(alibi[:, h % 2, :], dist[:], 2.0 ** -(h + 1), None, ALU.mult)\
                    .then_inc(*tick("alibi_pool", f"alibi{h}"))
            add("mix_post1")
            add("ffn_post1")
            for h0 in range(0, H, 2):
                for h in (h0, h0 + 1):
                    m = tmp(h % 2)
                    pool.wait_ge(*at(f"dn.dec{h}"))
                    tt(m["y"].rearrange("p (t n) -> p t n", t=TT), m["lt"].rearrange("p (t n) -> p t n", t=TT),
                       dconst[:, 0:P].unsqueeze(1).to_broadcast([P, TT, P]), ALU.mult).then_inc(*tick("dn_pool", f"dn.causal{h}"))
                    pool.wait_ge(*at(f"dn.qn{h}"))
                    pool.wait_ge(*at(f"dn.gl{h}"))
                    tt(qkv[:, h, :], m["x"], m["e"], ALU.mult).then_inc(*tick("dn_pool", f"dn.qdec{h}"))
            for h in range(H):
                pool.wait_ge(*at(f"gated.n{h}"))
                if h >= 4:
                    pool.wait_ge(*at(f"gated.h{h - 4}"))
                tt(y[:, 4 + h % 4, :], y[:, 2 + h % 2, :], zT[:, h, :], ALU.mult).then_inc(*tick("gated_pool", f"gated.t{h}"))

    return ev.found


def constants():
    i, j = np.arange(P)[:, None], np.arange(P)[None, :]
    u = np.arange(SEQ)[None, :]
    window = np.where(u <= FAR + i, 0.0, NEG)
    const = np.concatenate([np.eye(P), np.ones((P, P)), window], 1)
    dist = np.where(u <= FAR + i, u - (FAR + i), NEG)
    chunk = (i // 64) == (j // 64)
    masks = [chunk & (i <= j), chunk, (i % 2 == 0) & (j == i + 1)]
    masks += [((i // b) % 2 == 1) & (j // b == i // b - 1) for b in (2, 4, 8, 16, 32)]
    rope = np.zeros((P, 1056), np.float32)
    f = np.float32
    inv = f(10000.0) ** (-np.arange(0, 32, 2, dtype=f) / f(32))
    ang = np.arange(SEQ, dtype=f)[None, :] * inv[:, None]
    for half in range(2):
        rope[64 + 16 * half:80 + 16 * half, 0:512] = np.cos(ang)
        rope[64 + 16 * half:80 + 16 * half, 512:1024] = np.sin(ang)
    for m in range(16):
        rope[80 + m, 1024 + m] = -1.0
        rope[64 + m, 1040 + m] = 1.0
    return {"const": const.astype(f), "dist": dist.astype(f), "rope": rope,
            "dconst": np.concatenate(masks, 1).astype(f)}


def units(w, cols):
    k, m = w.shape
    return w.reshape(k // P, P, m // cols, cols).transpose(2, 1, 0, 3).reshape(m // cols, P, -1)


def kernel(**inputs):
    import concourse.bacc as bacc
    from concourse.bass_utils import run_bass_kernel_spmd as run

    a = {n: np.asarray(t) for n, t in inputs.items()}
    w = a["even_w_in"][0]
    cuts = np.cumsum([512, 512, 512, 8, 384, 256]).tolist()
    fq, fk, fv, _, cq, ckv, kr = np.split(w, cuts, axis=1)
    misc = np.concatenate([w[:, cuts[2]:cuts[2] + 64], kr, cq[:, 0:32]], 1)
    arrays = dict(constants())
    arrays["x"] = a["x"][0].reshape(TT, P, DM).transpose(1, 0, 2)
    arrays["even_in"] = units(np.concatenate([misc, cq, ckv, fq, fk, fv], 1), 256)
    arrays["even_uq"] = units(a["even_w_uq"][0], 384)
    arrays["even_ukv"] = units(a["even_w_ukv"][0], 1024)
    arrays["even_out"] = units(a["even_w_out"][0], 256)
    for n, part in zip("qkv", np.split(a["odd_w_in"][0], 3, axis=1)):
        arrays[f"odd_{n}"] = units(part, 256)
    arrays["odd_out"] = units(a["odd_w_out"][0], 256)
    for l in range(2):
        gate, val = np.split(a["ffn_w_up"][l], 2, axis=1)
        up = np.concatenate([gate.reshape(KT, P, FF_T, P), val.reshape(KT, P, FF_T, P)], 3)
        up = up.transpose(2, 1, 0, 3).reshape(FF_T, P, -1)
        cut = FF_GROUPS[0]
        arrays[f"ffn{l}_up0"], arrays[f"ffn{l}_up1"] = up[:cut], up[cut:]
        down = a["ffn_w_down"][l]
        arrays[f"ffn{l}_down0"], arrays[f"ffn{l}_down1"] = units(down[:cut * P], P), units(down[cut * P:], P)
    w = a["dn_w_in_2"][0]
    arrays["dn_qkv"], arrays["dn_z"] = units(w[:, :3072], 256), units(w[:, 3072:4096], 256)
    arrays["wba"] = units(w[:, 4096:], 16)[0]
    arrays["dn_out"] = units(a["dn_w_out_2"][0], 256)
    up, down = units(a["mlp_w_up_2"][0], 256), a["mlp_w_down_2"][0]
    half = MLP_GROUP * P
    arrays["mlp_up0"], arrays["mlp_up1"] = up[:8], up[8:]
    arrays["mlp_down0"] = units(down[:half], P)
    arrays["mlp_down1"], arrays["mlp_down2"] = np.split(units(down[half:], P), 2)

    def col(t):
        return t.reshape(-1, P).T

    def wide(t):
        return np.broadcast_to(t.reshape(1, -1), (P, t.size))
    pieces = []
    for l in range(2):
        pieces += [col(a[n][l]) for n in ("norm_mix_pre", "norm_mix_post", "norm_ffn_pre", "norm_ffn_post")]
    pieces += [col(a[n]) for n in ("norm_mix_2", "norm_mlp_2", "norm_final_2", "even_q_norm", "even_kv_norm")]
    for l in range(2):
        pieces += [col(a["ffn_conv_w"][l]), col(a["ffn_conv_b"][l])]
    forget = np.zeros((P, 1), np.float32)
    forget[0:H, 0] = a["even_b_forget"][0]
    pieces += [col(a["dn_conv_w_2"][0]), col(a["dn_norm_w_2"]), col(a["odd_subln"]), forget]
    pieces += [wide(a[n]) for n in ("dn_a_log_2", "dn_dt_bias_2", "odd_lambda_q1", "odd_lambda_k1",
                                    "odd_lambda_q2", "odd_lambda_k2")]
    arrays["vec"] = np.concatenate(pieces, 1)
    arrays = {n: np.ascontiguousarray(t) for n, t in arrays.items()}

    def program(known):
        nc = bacc.Bacc("TRN2", target_bir_lowering=False, num_devices=1)
        dram = {n: nc.dram_tensor(f"in_{n}", t.shape, F32, kind="ExternalInput").ap() for n, t in arrays.items()}
        dram["out"] = nc.dram_tensor("out", (SEQ, DM), F32, kind="ExternalOutput").ap()
        return nc, build(nc, dram, known)

    _, known = program(None)
    nc, _ = program(known)
    r = run(nc, [{f"in_{n}": t for n, t in arrays.items()}], core_ids=[0])
    return r.results[0]["out"].reshape(1, SEQ, DM)
```

```python
from contextlib import ExitStack

import numpy as np
import concourse.bass as bass
import concourse.mybir as mybir

F32 = mybir.dt.float32
F32R = mybir.dt.float32r
ACT = mybir.ActivationFunctionType
ALU = mybir.AluOpType
AX = mybir.AxisListType

P = 128
SEQ, DM = 512, 1024
KT = DM // P
TT = SEQ // P
H = 8
FF_T = 2816 // P
FF_GROUPS = (12, 10)
MLP_GROUP = 16
EPS = 1e-6
NEG = -1e30
FAR = 384
LAMBDA_INIT = 0.8 - 0.6 * float(np.exp(-0.3))
SLOT = 2048

STREAMS = [("even_in", 9, 2048), ("even_uq", 2, 1152), ("even_ukv", 1, 2048), ("even_out", 4, 2048)]
for _l in range(2):
    if _l == 1:
        STREAMS += [("odd_q", 4, 2048), ("odd_k", 4, 2048), ("odd_v", 4, 2048), ("odd_out", 4, 2048)]
    for _g in range(2):
        STREAMS += [(f"ffn{_l}_up{_g}", FF_GROUPS[_g], 2048), (f"ffn{_l}_down{_g}", KT, FF_GROUPS[_g] * P)]
STREAMS += [("dn_qkv", 12, 2048), ("dn_z", 4, 2048), ("dn_out", 4, 2048)]
STREAMS += [("mlp_up0", 8, 2048), ("mlp_down0", 8, 2048), ("mlp_up1", 8, 2048), ("mlp_down1", 4, 2048), ("mlp_down2", 4, 2048)]
UNITS = sum(u for _, u, _ in STREAMS)
UNIT0, _n = {}, 0
for _name, _u, _w in STREAMS:
    UNIT0[_name] = _n
    _n += _u
NUNITS = {name: u for name, u, _ in STREAMS}
WIDTH = {name: w for name, _, w in STREAMS}
TILES = {"even_in": 6 + 8 + 8, "even_uq": 8, "even_ukv": 8 + 4, "odd_v": 16}
for _name, _u, _w in STREAMS:
    TILES.setdefault(_name, _u if "down" in _name else 2 * _u)
TILE0, _n = {}, 0
for _name, _u, _w in STREAMS:
    TILE0[_name] = _n
    _n += TILES[_name]

VEC, _n = {}, 0
for _name, _w in [("mix_pre0", 8), ("mix_post0", 8), ("ffn_pre0", 8), ("ffn_post0", 8),
                  ("mix_pre1", 8), ("mix_post1", 8), ("ffn_pre1", 8), ("ffn_post1", 8),
                  ("mix2", 8), ("mlp2", 8), ("final", 8), ("q_norm", 3), ("kv_norm", 2),
                  ("conv0", 4 * FF_T), ("conv1", 4 * FF_T), ("dn_conv", 4 * 24), ("dn_norm", 1),
                  ("subln", 1), ("b_forget", 1), ("a_log", 8), ("dt_bias", 8), ("lam", 256)]:
    VEC[_name] = _n
    _n += _w
NVEC = _n


def peeled(i):
    return isinstance(i, int) and i == 0


class Events:

    def __init__(self, nc, ctx, known):
        self.nc, self.ctx, self.known = nc, ctx, known
        self.sems, self.count, self.found, self.open = {}, {}, {}, None

    def sem(self, name):
        if name not in self.sems:
            self.sems[name] = self.ctx.enter_context(self.nc.semaphore(name))
            self.count[name] = 0
        return self.sems[name]

    def tick(self, name, event=None, by=1):
        s = self.sem(name)
        self.count[name] += by
        if event is not None:
            assert self.open is not None or event not in self.found, event
            self.found.setdefault(event, (name, self.count[name], 0))
            if self.open is not None:
                self.open.append((event, self.count[name]))
        return s, by

    def at(self, event, i=None):
        if self.known is None:
            return self.sem("first_build"), 1
        name, value, stride = self.known[event]
        if i is None:
            return self.sem(name), value
        return self.sem(name), i * stride + value

    def loop(self, eng, n, peel=0):
        for i in range(peel):
            yield i
        before, self.open = dict(self.count), []
        with eng.Fori(peel, n) as i:
            yield i
        for name, c in self.count.items():
            per = c - before.get(name, 0)
            self.count[name] = before.get(name, 0) + (n - peel) * per
            for e, seen in self.open:
                if self.found[e][0] == name:
                    assert seen == self.found[e][1] + peel * per, e
                    self.found[e] = (name, self.found[e][1], per)
        self.open = None


def build(nc, dram, known):
    ctx = ExitStack()
    with ctx:
        ev = Events(nc, ctx, known)
        tick, at = ev.tick, ev.at
        sem = ev.sem

        place = [((nc.sbuf_base + 63) // 64) * 64]

        def sb(name, shape, dt=F32, where=None):
            size = 4 * int(np.prod(shape[1:]))
            if where is None:
                where = place[0]
                place[0] += size
            assert where + size <= nc.sbuf_usable_end, (name, where + size - nc.sbuf_usable_end)
            return nc.alloc_sbuf_tensor_at(name, shape, dt, offset=where)

        x = sb("x", [P, KT, SEQ])
        h_at = place[0]
        hH = sb("hH", [P, KT, SEQ], F32R)
        hL = sb("hL", [P, KT, SEQ], F32R)
        raw = [sb(f"raw{s}", [P, SLOT]) for s in range(2)]
        wH = [sb(f"wH{s}", [P, SLOT], F32R) for s in range(2)]
        wL = [sb(f"wL{s}", [P, SLOT], F32R) for s in range(2)]
        y = sb("y", [P, KT, SEQ])
        const = sb("const", [P, 768])
        vec = sb("vec", [P, NVEC])
        sq = sb("sq", [P, 2, SEQ])
        ss = sb("ss", [P, SEQ])
        dg = sb("dg", [P, TT, P])
        small = sb("small", [P, 64])
        stat = sb("stat", [P, 64])
        base = place[0]
        ident, ones, window = const[:, 0:P], const[:, P:2 * P], const[:, 2 * P:]
        eps = small[:, 60:61]
        sq_heads = sq[:].rearrange("p a (b n) -> p (a b) n", n=P)
        rinv = dg[:].rearrange("p t n -> p (t n)")

        def stage(items):
            place[0] = base
            return [sb(*it) for it in items]

        xin, = stage([("xin", [P, TT, DM])])
        cqH, cqL, misc, rope, prob, gate_row = stage([
            ("cqH", [P, 5, SEQ], F32R), ("cqL", [P, 5, SEQ], F32R), ("misc", [P, SEQ]), ("rope", [P, 1056]),
            ("prob", [P, 2, 1280]), ("gate_row", [P, 64])])
        even2 = place[0]
        qF, kF, vF, cB = (sb(*it) for it in [("qF", [P, 4, SEQ]), ("kF", [P, 4, SEQ]), ("vF", [P, TT, 512]),
                                             ("cB", [P, H, SEQ])])
        place[0] = even2
        qM, kM, vM = (sb(*it) for it in [("qM", [P, H, SEQ]), ("kM", [P, H, SEQ]), ("vM", [P, TT, 512])])
        mH, mL, ft = stage([("mH", [P, MLP_GROUP, SEQ], F32R), ("mL", [P, MLP_GROUP, SEQ], F32R), ("ft", [P, 8, SEQ])])
        qO, kO, vO, dist, alibi, probO, lamt = stage([
            ("qO", [P, H, SEQ]), ("kO", [P, H, SEQ]), ("vO", [P, TT, DM]), ("dist", [P, SEQ]),
            ("alibi", [P, 2, SEQ]), ("probO", [P, 2, 2, 1280]), ("lamt", [P, 128])])
        qkv, zT, S, vN, dconst, wba, tok = stage([
            ("qkv", [P, 24, SEQ]), ("zT", [P, H, SEQ]), ("S", [P, H, P]), ("vN", [P, H, P]),
            ("dconst", [P, 9 * P]), ("wba", [P, P]), ("tok", [P, 16, 32])])
        wbaH, wbaL = sb("wbaH", [P, P], F32R), sb("wbaL", [P, P], F32R)
        rowsT, gl, zed = sb("rowsT", [P, P]), sb("gl", [P, H, 8]), sb("zed", [P, 4, 16])
        o_at = base + 4 * 8 * SEQ
        oH, oL = sb("oH", [P, KT, SEQ], F32R, o_at), sb("oL", [P, KT, SEQ], F32R, o_at + 4 * KT * SEQ)
        attnT = sb("attnT", [P, H, SEQ], F32, h_at)
        kdec = sb("kdec", [P, H, SEQ], F32, h_at + 4 * KT * SEQ)
        PT = y[:].rearrange("p (a j) n -> p a j n", a=2)

        bank = [ctx.enter_context(nc.psum_tensor(f"bank{b}", [P, 512], F32)) for b in range(8)]

        w_in = [sem(f"weights_loaded{s}") for s in range(2)]
        w_hi, w_split = sem("weights_hi"), sem("weights_split")
        mm_done, evac = sem("tile_done"), sem("tile_evacuated")
        block = ctx.enter_context(nc.Block())

        def v(name, k=0, n=1):
            return vec[:, VEC[name] + k:VEC[name] + k + n]

        def vr(name, i, n=1):
            return vec[:, bass.ds(i + VEC[name], n)]

        def ptile(h, i, buf):
            o = P * (i * (i + 1) // 2)
            return buf[:, o:o + P * (i + 1)]

        def looped(name, per):
            return NUNITS[name] // per

        def tmp(p):
            names = ["lt", "y", "x", "t1", "r", "e"]
            slots = [y[:, k, :] for k in range(KT)] + [sq[:, k, :] for k in range(2)] + [dg[:].rearrange("p t n -> p (t n)"), ss[:]]
            return {n: slots[6 * p + k] for k, n in enumerate(names)}

        @block.sync
        def _(sp):
            def load(name, n, j, s):
                w = WIDTH[name]
                sp.dma_start(raw[s][:, 0:w].unsqueeze(1),
                             dram[name].rearrange("u p c -> p u c")[:, bass.ds(j, 1), :]).then_inc(w_in[s], 16)

            load("even_in", 0, 0, 0)
            for dst, src in [(xin[:], "x"), (const[:], "const"), (vec[:], "vec")]:
                sp.dma_start(dst, dram[src]).then_inc(*tick(f"loaded_{src}", f"in.{src}", 16))
            for name, units, _w in STREAMS:
                n0 = UNIT0[name]
                if name.startswith("even_") and name != "even_out":
                    for j in range(1 if n0 == 0 else 0, units):
                        n = n0 + j
                        if n >= 2:
                            sp.wait_ge(w_split, n - 1)
                        load(name, n, j, n % 2)
                else:
                    with sp.Fori(0, units // 2) as i:
                        for s in range(2):
                            sp.wait_ge(w_split, i * 2 + (n0 + s - 1))
                            load(name, n0 + s, i * 2 + s, s)
            for t in range(TT):
                for half in range(2):
                    sp.wait_ge(*at(f"out.copied{t}.{half}"))
                sp.dma_start(dram["out"][t * P:(t + 1) * P, :], xin[:, t, :]).then_inc(*tick("stored", f"out.stored{t}", 16))
            sp.wait_ge(*at(f"out.stored{TT - 1}"))

        @block.tensor
        def _(pe):
            mm = nc.tensor.matmul

            def three(out, w, xv, first, last, swap=False):
                (a, b), (c, d) = (xv, w) if swap else (w, xv)
                mm(out, a, c, start=first, stop=False)
                mm(out, a, d, start=False, stop=False)
                return mm(out, b, c, start=False, stop=last)

            def tile_wait(name, l):
                pe.wait_ge(evac, l + (TILE0[name] - 3))

            def unit_tiles(s, kt, aH, aL, b0, tiles=2, cols=256, wait=None, within=None):
                for tl in range(tiles):
                    if wait is not None:
                        wait(tl)
                    for k in range(kt):
                        if within is not None:
                            within(tl, k)
                        c = slice(k * cols + tl * P, k * cols + tl * P + P)
                        last = three(bank[b0 + tl][:], (wH[s][:, c], wL[s][:, c]),
                                     (aH[:, k, :], aL[:, k, :]), k == 0, k == kt - 1)
                    last.then_inc(mm_done, 1)

            def first_unit(s, ready, then, aH=hH, aL=hL):
                for k in range(KT):
                    ready(k)
                    for tl in range(2):
                        c = slice(k * 256 + tl * P, k * 256 + tl * P + P)
                        last = three(bank[tl][:], (wH[s][:, c], wL[s][:, c]), (aH[:, k, :], aL[:, k, :]), k == 0, k == KT - 1)
                        if k == KT - 1:
                            last.then_inc(mm_done, 1)
                    if then is not None:
                        then(k)

            def token_sums(tag, event, i=None):
                pe.wait_ge(*at(event, i))
                for t in range(TT):
                    last = mm(bank[7][:, t:t + 1], ss[:, t * P:(t + 1) * P], ones[:, 0:1], start=True, stop=True)
                last.then_inc(*tick("sums_pe", f"{tag}.sum{KT - 1}"))

            def pre_within(tag):
                def within(tl, k):
                    if tl == 0 and k == 3 and tag != "mlp2":
                        token_sums(tag, f"{tag}.ss")
                    if (tl, k) == ((0, 2) if tag == "mlp2" else (1, 0)):
                        spread(tag)
                return within

            def first_of(tag):
                if tag == "mlp2":
                    first_unit(0, lambda k: pe.wait_ge(*at(f"dn_out.u{k % 4}", k // 4)),
                               lambda k: token_sums(tag, "dn_out.tile3.ss", looped("dn_out", 2) - 1) if k == KT - 1 else None)
                elif tag in ("subln", "gated"):
                    def head_spread(h):
                        if h < H:
                            pe.wait_ge(*at(f"{tag}.diag{h}"))
                            mm(bank[4 + h % 4][:], ones, y[:, h % 4, :], start=True, stop=True)\
                                .then_inc(*tick("spread_pe", f"{tag}.spread{h}"))
                    for h in range(4):
                        head_spread(h)
                    first_unit(0, lambda h: pe.wait_ge(*at(f"{tag}.h{h}")), lambda h: head_spread(h + 4),
                               *((hH, hL) if tag == "subln" else (oH, oL)))
                else:
                    first_unit(0, lambda k: pe.wait_ge(*at(f"{tag}.u{k}")), None)

            def stream2(name, aH=hH, aL=hL, more=None, first=None, peel=0):
                n0 = UNIT0[name]
                for i in ev.loop(pe, looped(name, 2), peel=1 if first else peel):
                    for s in range(2):
                        pe.wait_ge(w_split, i * 2 + (n0 + s + 1))
                        if first and peeled(i) and s == 0:
                            tile_wait(name, 1)
                            first_of(first)
                            continue
                        unit_tiles(s, KT, aH, aL, 2 * s, wait=lambda tl: tile_wait(name, i * 4 + (2 * s + tl)),
                                   within=pre_within(first) if first not in (None, "subln", "gated") and peeled(i) else None)
                        if more is not None:
                            more(i, s)

            def stream_down(name, kt, up=None, per=2):
                n0 = UNIT0[name]

                def within(tl, k):
                    if k in (0, kt - per):
                        pe.wait_ge(*at(f"{up}.lo{per - 1}", looped(up, 2) - (2 if k == 0 else 1)))
                for i in ev.loop(pe, looped(name, 4), peel=1 if up and looped(name, 4) > 1 else 0):
                    for a in range(4):
                        pe.wait_ge(w_split, i * 4 + (n0 + a + 1))
                        tile_wait(name, i * 4 + a)
                        unit_tiles(a % 2, kt, mH, mL, a, tiles=1, cols=P, within=within if up and peeled(i) and a == 0 else None)

            def unit_tokens(s, b0, l0, wait):
                for t in range(TT):
                    wait(l0 + t)
                    for k in range(KT):
                        c = slice(k * 256, k * 256 + 256)
                        last = three(bank[(b0 + t) % 4][:, 0:256], (wH[s][:, c], wL[s][:, c]),
                                     (hH[:, k, t * P:(t + 1) * P], hL[:, k, t * P:(t + 1) * P]),
                                     k == 0, k == KT - 1, swap=True)
                    last.then_inc(mm_done, 1)

            def sums(tag, k, col, first, ticked, b=7):
                pe.wait_ge(*at(f"{tag}.sq{k}"))
                for t in range(TT):
                    last = mm(bank[b][:, col + t:col + t + 1], sq[:, k % 2, t * P:(t + 1) * P], ones[:, 0:1],
                              start=first and t == 0, stop=ticked, skip_group_check=True)
                last.then_inc(*tick("sums_pe", f"{tag}.sum{k}"))

            def spread(tag, b=6):
                pe.wait_ge(*at(f"{tag}.diag"))
                mm(bank[b][:], ones, dg[:].rearrange("p t n -> p (t n)"), start=True, stop=True)\
                    .then_inc(*tick("spread_pe", f"{tag}.spread"))

            def norm_summed(tag, name, per):
                token_sums(tag, f"{name}.tile3.ss", looped(name, per) - 1)
                spread(tag)

            def attention(name, q, k, val, pbuf, W, masked, rows, M):
                def scores(h, tiles=range(TT)):
                    for i in tiles if h < H else ():
                        for w in range(W):
                            j = (h * TT + i) * W + w
                            if j >= 4:
                                pe.wait_ge(*at(f"{name}.biased{j - 4}"))
                            n = P * (i + 1)
                            last = mm(bank[j % 4][:, 0:n], q(h, w)[:, i * P:n], k(h, w)[:, 0:n],
                                      start=True, stop=not masked)
                            if masked:
                                last = mm(bank[j % 4][:, i * P:n], ident, window[:, FAR:], start=False, stop=True)
                            last.then_inc(*tick(f"{name}_pe", f"{name}.scores{j}"))

                def turn(h):
                    for i in range(TT):
                        ti = h * TT + i
                        pe.wait_ge(*at(f"{name}.prob{h}.{i}"))
                        if ti >= 2:
                            pe.wait_ge(*at(f"{name}.copied{ti - 2}"))
                        for j in range(i + 1):
                            last = nc.tensor.transpose(bank[4 + ti % 2][:, j * P:(j + 1) * P],
                                                       ptile(h, i, pbuf(h, 0))[:, j * P:(j + 1) * P], ident)
                        last.then_inc(*tick(f"{name}_pe", f"{name}.turned{ti}"))

                def values(h):
                    pe.wait_ge(*at(f"{name}.copied{h * TT + TT - 1}"))
                    if h >= 2:
                        pe.wait_ge(*at(f"{name}.out{h - 2}"))
                    for j in range(TT):
                        last = mm(bank[6 + h % 2][rows(h), j * P:], val(h, j), PT[:, h % 2, j, j * P:],
                                  start=j == 0, stop=j == TT - 1)
                    last.then_inc(*tick(f"{name}_pe", f"{name}.values{h}"))

                scores(0)
                scores(1)
                for h in range(H):
                    if W == 1:
                        scores(h + 2)
                        turn(h)
                        if h >= 1:
                            values(h - 1)
                        continue
                    scores(h + 2, range(2))
                    turn(h)
                    scores(h + 2, range(2, TT))
                    values(h)
                    if h >= 2:
                        sums("subln", h - 2, FAR + 4 * (h - 2), True, True, 4)
                if W == 1:
                    values(H - 1)

            pe.wait_ge(*at("in.x"))
            pe.wait_ge(*at("in.const"))
            for k in range(KT):
                if k >= 4:
                    pe.wait_ge(*at(f"x0.{k - 4}"))
                for t in range(TT):
                    last = nc.tensor.transpose(bank[2 + k % 4][:, t * P:(t + 1) * P], xin[:, t, k * P:(k + 1) * P], ident)
                last.then_inc(*tick("input_pe", f"x0.turned{k}"))

            pe.wait_ge(w_split, 1)
            first_of("mix_pre0")
            for u in range(1, 7):
                pe.wait_ge(w_split, u + 1)
                b0 = 2 * (u % 2)

                def wait(tl):
                    if 2 * u + tl >= 4:
                        pe.wait_ge(evac, 2 * u + tl - 3)
                unit_tiles(u % 2, KT, hH, hL, b0, wait=wait, within=pre_within("mix_pre0") if u == 1 else None)
                if u == 3:
                    for k in range(3):
                        sums("cq", k, 0, k == 0, k == 2)
                    for k in range(3, 5):
                        sums("cq", k, 4, k == 3, k == 4)
                if u == 5:
                    pe.wait_ge(*at("cq.diag"))
                    mm(bank[5][:], ones, y[:, 5, :], start=True, stop=True)\
                        .then_inc(*tick("spread_pe", "cq.spread"))
                    pe.wait_ge(*at("ckv.diag"))
                    mm(bank[4][:], ones, y[:, 6, :], start=True, stop=True).then_inc(*tick("spread_pe", "ckv.spread"))
            for c in range(2):
                u = 7 + c
                pe.wait_ge(w_split, u + 1)
                unit_tokens(u % 2, 2, 14 + 4 * c, lambda l: pe.wait_ge(evac, l - 3))
            pe.wait_ge(*at("gate.rows"))
            pe.wait_ge(*at("cq.h4"))
            for h in range(H):
                if h >= 4:
                    pe.wait_ge(*at(f"gate.bias{h - 4}"))
                mm(bank[4 + h % 4][:], ident[0:H, h:h + 1].to_broadcast([H, P]), prob[0:H, 1, 512:1024],
                   start=True, stop=True).then_inc(*tick("gate_pe", f"gate.spread{h}"))
            pe.wait_ge(evac, TILE0["even_uq"])
            pe.wait_ge(*at(f"gate.bias{H - 1}"))

            def half(h):
                return slice(64 * (h % 2), 64 * (h % 2) + 64)
            attention("fox", lambda h, w: qF[half(h), h // 2, :], lambda h, w: kF[half(h), h // 2, :],
                      lambda h, j: vF[:, j, 64 * h:64 * h + 64], lambda h, w: prob[:, h % 2, :], 1, True, half, 64)

            pe.wait_ge(*at(f"fox.out{H - 1}"))
            for u in range(2):
                n = UNIT0["even_uq"] + u
                pe.wait_ge(w_split, n + 1)
                for hh in range(4):
                    l = 4 * u + hh
                    if l >= 4:
                        tile_wait("even_uq", l)
                    for k in range(3):
                        c = slice(k * 384 + hh * 96, k * 384 + hh * 96 + 96)
                        last = three(bank[l % 4][0:96, :], (wH[n % 2][:, c], wL[n % 2][:, c]),
                                     (cqH[:, k, :], cqL[:, k, :]), k == 0, k == 2)
                    last.then_inc(mm_done, 1)

            def turn_rotary(r):
                if r == 0:
                    pe.wait_ge(*at("in.rope"))
                    src = misc[0:96, :]
                else:
                    pe.wait_ge(evac, TILE0["even_uq"] + r)
                    src = qM[0:96, r - 1, :]
                if r >= 2:
                    pe.wait_ge(*at(f"rope.sin{r - 2}"))
                mm(bank[4 + r % 2][64:96, :], rope[0:96, 1024:1056], src, start=True, stop=True)\
                    .then_inc(*tick("rope_pe", f"rope.turned{r}"))
            turn_rotary(0)
            turn_rotary(1)
            n = UNIT0["even_ukv"]
            pe.wait_ge(w_split, n + 1)
            for h in range(H):
                tile_wait("even_ukv", h)
                for k in range(2):
                    c = slice(k * DM + h * P, k * DM + h * P + P)
                    last = three(bank[h % 4][:], (wH[n % 2][:, c], wL[n % 2][:, c]),
                                 (cqH[:, 3 + k, :], cqL[:, 3 + k, :]), k == 0, k == 1)
                last.then_inc(mm_done, 1)
                if h + 2 <= H:
                    turn_rotary(h + 2)
            for t in range(TT):
                tile_wait("even_ukv", H + t)
                for k in range(2):
                    c = slice(k * DM, (k + 1) * DM)
                    wv = [w[n % 2][:, c].rearrange("p (h d) -> p h d", h=H)[:, :, 64:] for w in (wH, wL)]
                    tk = slice(t * P, (t + 1) * P)
                    last = three(bank[t % 4][:], wv, (cqH[:, 3 + k, tk], cqL[:, 3 + k, tk]), k == 0, k == 1, swap=True)
                last.then_inc(mm_done, 1)
            pe.wait_ge(evac, TILE0["even_out"])
            pe.wait_ge(*at("rope.k"))
            pe.wait_ge(*at(f"rope.q{H - 1}"))
            attention("mla", lambda h, w: qM[0:96, h, :], lambda h, w: kM[0:96, h, :],
                      lambda h, j: vM[:, j, 64 * h:64 * h + 64], lambda h, w: prob[:, h % 2, :], 1, False, half, 64)
            pe.wait_ge(*at(f"mla.out{H - 1}"))
            stream2("even_out")

            def ffn(l):
                norm_summed(f"mix_post{l}", "even_out" if l == 0 else "odd_out", 2)
                for g in range(2):
                    stream2(f"ffn{l}_up{g}", first=f"ffn_pre{l}" if g == 0 else None)
                    stream_down(f"ffn{l}_down{g}", FF_GROUPS[g], up=f"ffn{l}_up{g}")
                norm_summed(f"ffn_post{l}", f"ffn{l}_down1", 4)

            ffn(0)

            stream2("odd_q", first="mix_pre1")
            stream2("odd_k")
            n0 = UNIT0["odd_v"]
            for i in ev.loop(pe, looped("odd_v", 2)):
                for s in range(2):
                    pe.wait_ge(w_split, i * 2 + (n0 + s + 1))
                    unit_tokens(s, 0, 4 * s, lambda l: tile_wait("odd_v", i * 8 + l))
            pe.wait_ge(evac, TILE0["odd_out"])

            def two(w):
                return slice(64 * w, 64 * w + 64)
            attention("diff", lambda h, w: qO[two(w), h, :], lambda h, w: kO[two(w), h, :],
                      lambda h, j: vO[:, j, P * h:P * h + P], lambda h, w: probO[:, h % 2, w, :], 2, False,
                      lambda h: slice(0, P), P)
            for h in (H - 2, H - 1):
                sums("subln", h, FAR + 4 * h, True, True, 4)
            stream2("odd_out", first="subln")
            ffn(1)

            stream2("dn_qkv", first="mix2")
            pe.wait_ge(*at("dn.wba"))
            for k in range(KT):
                c = slice(k * 16, k * 16 + 16)
                last = three(bank[5][0:16, :], (wbaH[:, c], wbaL[:, c]), (hH[:, k, :], hL[:, k, :]), k == 0, k == KT - 1)
            last.then_inc(*tick("dn_pe", "dn.ba_rows"))
            pe.wait_ge(*at("dn.ba_scaled"))
            for t in range(TT):
                last = nc.tensor.transpose(bank[4][:, 16 * t:16 * t + 16], vN[0:16, t, :], ident[0:16, 0:16])
            last.then_inc(*tick("dn_pe", "dn.ba"))

            def key_norms(i, s):
                for a in range(4):
                    pe.wait_ge(*at(f"dn.sq{s}.{a}", i))
                    for t in range(TT):
                        last = mm(bank[7][:, bass.ds(i * 32 + (16 * s + 4 * a + t), 1)],
                                  y[:, 4 + a, t * P:(t + 1) * P], ones[:, 0:1], start=True, stop=True)
                last.then_inc(*tick("sums_pe", f"dn.sum{s}"))
                if peeled(i) and s == 1:
                    pe.wait_ge(*at("dn.g"))
                    mm(bank[5][:, 0:32], dconst[:, 0:P], tok[:, 1, :], start=True, stop=True)
                    mm(bank[5][:, 32:64], dconst[:, P:2 * P], tok[:, 1, :], start=True, stop=True)\
                        .then_inc(*tick("dn_pe", "dn.gc"))
            stream2("dn_z", more=key_norms, peel=1)
            pe.wait_ge(evac, TILE0["dn_out"])
            pe.wait_ge(*at("dn.rowset"))
            nc.tensor.transpose(bank[4][0:96, 0:P], tok[:, 8:11, :].rearrange("p a b -> p (a b)"), ident)\
                .then_inc(*tick("dn_pe", "dn.rows_turned"))
            pe.wait_ge(*at("dn.rows"))
            for h0 in range(0, H, 2):
                pair = [(h0 + p, [bank[4 * p + b] for b in range(4)], tmp(p)) for p in range(2)]
                for h, b, m in pair:
                    if h >= 2:
                        pe.wait_ge(*at(f"dn.w{h - 2}"))
                    for kind in (0, 2):
                        for t in range(TT):
                            r = 32 * kind + 4 * h + t
                            last = mm(b[kind][:, t * P:(t + 1) * P], ident[0:96, r:r + 1].to_broadcast([96, P]),
                                      rowsT[0:96, :], start=True, stop=True)
                    last.then_inc(*tick("dn_pe", f"dn.spread{h}"))
                for h, b, m in pair:
                    for t in range(TT):
                        c = slice(t * P, (t + 1) * P)
                        mm(b[1][:, c], qkv[:, 8 + h, c], qkv[:, h, c], start=True, stop=True)
                for h, b, m in pair:
                    pe.wait_ge(*at(f"dn.qn{h}"))
                    for t in range(TT):
                        c = slice(t * P, (t + 1) * P)
                        last = mm(b[0][:, c], qkv[:, 8 + h, c], m["t1"][:, c], start=True, stop=True)
                    last.then_inc(*tick("dn_pe", f"dn.gram{h}"))

                def token_major(h, b):
                    pe.wait_ge(*at(f"dn.diff{h}"))
                    pe.wait_ge(*at(f"dn.e{h}"))
                    for t in range(TT):
                        c = slice(t * P, (t + 1) * P)
                        nc.tensor.transpose(b[3][:, c], qkv[:, 8 + h, c], ident)
                        last = nc.tensor.transpose(b[2][:, c], qkv[:, 16 + h, c], ident)
                    last.then_inc(*tick("dn_pe", f"dn.turned{h}"))
                token_major(*pair[0][:2])
                for s in range(1, 6):
                    for h, b, m in pair:
                        if s == 1:
                            pe.wait_ge(*at(f"dn.y{h}.0"))
                            for t in range(TT):
                                c = slice(t * P, (t + 1) * P)
                                last = nc.tensor.transpose(b[0][:, c], m["y"][:, c], ident)
                            last.then_inc(*tick("dn_pe", f"dn.xt{h}"))
                            if h == h0:
                                token_major(*pair[1][:2])
                        pe.wait_ge(*at(f"dn.x{h}.{s - 1}"))
                        if s == 1:
                            pe.wait_ge(*at(f"dn.attn{h}"))
                        for t in range(TT):
                            c = slice(t * P, (t + 1) * P)
                            last = mm(b[1][:, c], m["lt"][:, c], m["x"][:, c], start=True, stop=True)
                        last.then_inc(*tick("dn_pe", f"dn.lx{h}.{s}"))
                    for h, b, m in pair:
                        pe.wait_ge(*at(f"dn.t{h}.{s}"))
                        if s == 1:
                            pe.wait_ge(*at(f"dn.tok{h}"))
                            pe.wait_ge(*at(f"dn.values{h}"))
                        for t in range(TT):
                            c = slice(t * P, (t + 1) * P)
                            if s < 5:
                                mm(b[2][:, c], m["y"][:, c], m["t1"][:, c], start=True, stop=True)
                            last = mm(b[3][:, c], m["t1"][:, c], m["y"][:, c], start=True, stop=True)
                        last.then_inc(*tick("dn_pe", f"dn.xx{h}.{s}"))
                for h, b, m in pair:
                    pe.wait_ge(*at(f"dn.y{h}.5"))
                    for t in range(TT):
                        c = slice(t * P, (t + 1) * P)
                        mm(b[0][:, c], m["y"][:, c], qkv[:, 16 + h, c], start=True, stop=True)
                        last = mm(b[1][:, c], m["r"][:, c], m["y"][:, c], start=True, stop=True)
                    last.then_inc(*tick("dn_pe", f"dn.uw{h}"))
            pe.wait_ge(*at(f"dn.w{H - 2}"))
            pe.wait_ge(*at(f"dn.w{H - 1}"))
            pe.wait_ge(*at(f"dn.qdec{H - 1}"))

            def output_sums(t):
                pe.wait_ge(*at(f"gated.sq{t}"))
                for h in range(H):
                    last = mm(bank[7][:, 4 * h + t:4 * h + t + 1], sq_heads[:, h, :], ones[:, 0:1], start=True, stop=True)
                last.then_inc(*tick("sums_pe", f"gated.sum{t}"))

            for n in range(8):
                t, r = n // 2, slice(64 * (n % 2), 64 * (n % 2) + 64)
                ck = slice(64 * n, 64 * n + 64)
                for g in range(2):
                    if g and n >= 3 and n % 2:
                        output_sums(n // 2 - 1)
                    pe.wait_ge(*at(f"scan.state{n - 1}.{g}"))
                    for hh in range(4):
                        h = 4 * g + hh
                        last = mm(bank[g][r, hh * P:(hh + 1) * P], qkv[:, 8 + h, ck], S[:, h, :], start=True, stop=True)
                    last.then_inc(*tick("scan_pe", f"scan.ws{n}.{g}"))
                if n >= 2:
                    pe.wait_ge(*at(f"scan.o{n - 2}"))
                for h in range(H):
                    mm(bank[4 + n % 2][:, 64 * h:64 * h + 64], S[:, h, :], qkv[:, h, ck],
                       start=h == 0, stop=False, skip_group_check=True)
                for g in range(2):
                    pe.wait_ge(*at(f"scan.vn{n}.{g}"))
                    for hh in range(4):
                        h = 4 * g + hh
                        last = mm(bank[2 + g][:, hh * P:(hh + 1) * P], kdec[r, h, t * P:(t + 1) * P], vN[r, h, :],
                                  start=True, stop=True)
                    last.then_inc(*tick("scan_pe", f"scan.kv{n}.{g}"))
                for h in range(H):
                    last = mm(bank[4 + n % 2][:, 64 * h:64 * h + 64], vN[r, h, :],
                              attnT[r, h, t * P + r.start:t * P + r.stop], start=False, stop=True, skip_group_check=True)
                last.then_inc(*tick("scan_pe", f"scan.out{n}"))
            output_sums(TT - 1)
            stream2("dn_out", oH, oL, first="gated")
            for g in range(2):
                stream2(f"mlp_up{g}", first="mlp2" if g == 0 else None)
                stream_down(f"mlp_down{g}", MLP_GROUP, up=f"mlp_up{g}", per=4)
            stream_down("mlp_down2", MLP_GROUP)
            token_sums("final", "mlp_down2.tile3.ss", looped("mlp_down2", 4) - 1)
            pe.wait_ge(*at("mlp_down2.tile3.gain", looped("mlp_down2", 4) - 1))
            for t in range(TT):
                for half_ in range(2):
                    j = 2 * t + half_
                    if j == 7:
                        pe.wait_ge(*at("out.copied0.0"))
                    for kk in range(4):
                        last = nc.tensor.transpose(bank[(4 + j) % 7][:, kk * P:(kk + 1) * P],
                                                   y[:, 4 * half_ + kk, t * P:(t + 1) * P], ident)
                    last.then_inc(*tick("out_pe", f"out.turned{t}.{half_}"))

        @block.scalar
        def _(act):
            def a(out, in_, func, **kw):
                return nc.scalar.activation(out, in_, func, **kw)

            def hi(n, half_n, s):
                act.wait_ge(w_in[s], half_n * 16 + 16)
                a(wH[s][:], raw[s][:], ACT.Copy).then_inc(w_hi, 1)

            def hi_next(name, i, s, per=2, last=False, early=0):
                n0 = UNIT0[name] + s
                if last or peeled(i) and s < early:
                    return
                each = TILES[name] // NUNITS[name]
                act.wait_ge(mm_done, i * (per * each) + (TILE0[name] + s * each))
                hi(None, i * (per // 2) + (n0 + 1) // 2, (n0 + 1) % 2)

            def done(name, l):
                act.wait_ge(mm_done, l + (TILE0[name] + 1))

            def evacuated(name, l):
                act.wait_ge(evac, l + (TILE0[name] + 1))

            def squares(tag, k, src, ready=None):
                if ready is not None:
                    act.wait_ge(*at(ready))
                if k >= 2:
                    act.wait_ge(*at(f"{tag}.sum{k - 2}"))
                a(sq[:, k % 2, :], src, ACT.Square).then_inc(*tick("squares_act", f"{tag}.sq{k}"))

            def root(tag, kt, n, col=0, w=TT, out=0, b=7):
                act.wait_ge(*at(f"{tag}.sum{kt - 1}"))
                return a(small[:, out:out + w], bank[b][:, col:col + w], ACT.Sqrt, bias=eps, scale=1.0 / n)

            def his(tag, kt, H_=hH, slots=4, src=lambda k: y[:, k % 4, :], k0=0):
                for k in range(kt):
                    act.wait_ge(*at(f"{tag}.t{k0 + k}"))
                    a(H_[:, k0 + k, :], src(k), ACT.Copy).then_inc(*tick("norm_act", f"{tag}.hi{k0 + k}"))

            def hi_early(name, u=1):
                act.wait_ge(mm_done, TILE0[name] + (u - 1) * TILES[name] // NUNITS[name])
                n = UNIT0[name] + u
                hi(None, n // 2, n % 2)

            def pre(tag, ready, name=None):
                for k in range(KT):
                    ready(k)
                    a(hH[:, k, :], x[:, k, :], ACT.Copy, scale=v(tag, k)).then_inc(*tick("norm_act", f"{tag}.hi{k}"))
                    a(y[:, k, :], x[:, k, :], ACT.Square).then_inc(*tick("squares_act", f"{tag}.sq{k}"))
                if tag == "mix_pre0":
                    hi(1, 0, 1)
                root(tag, KT, DM).then_inc(*tick("norm_act", f"{tag}.root"))
                if name is not None:
                    hi_early(name, 2)

            def stream_plain(name, early=0):
                for i in ev.loop(act, looped(name, 2), peel=int(early > 0)):
                    for s in range(2):
                        hi_next(name, i, s, early=early)

            def tile_out(name, i, a_, mode, t0=0):
                tag = f"{name}.tile{a_}"
                yt = y[:, bass.ds(i * 4 + (a_ + t0), 1), :]
                xt = x[:, bass.ds(i * 4 + (a_ + t0), 1), :]
                if mode == "y0":
                    done(name, i * 4 + a_)
                    a(yt, bank[a_][:].unsqueeze(1), ACT.Copy).then_inc(evac, 1)
                    return
                if mode == "x0":
                    return
                if mode == "y":
                    done(name, i * 4 + a_)
                    src = bank[a_][:].unsqueeze(1)
                else:
                    evacuated(name, i * 4 + a_)
                    src = yt if mode == "y1" else xt
                act.wait_ge(*(at(f"{name}.tile{a_ - 2}.ss", i) if a_ >= 2 else at(f"{name}.tile{a_ + 2}.ss", i - 1)))
                a(sq[:, a_ % 2, :].unsqueeze(1), src, ACT.Square).then_inc(*tick("out_act", f"{tag}.sq"))
                if mode == "y":
                    a(yt, src, ACT.Copy).then_inc(evac, 1)
                if name in ("mlp_down1", "mlp_down2"):
                    k = i * 4 + (a_ + t0)
                    a(y[:, bass.ds(k, 1), :], xt, ACT.Copy, scale=vr("final", k)).then_inc(*tick("out_gain_act", f"{tag}.gain"))
                if name == "dn_out":
                    a(hH[:, bass.ds(i * 4 + a_, 1), :], xt, ACT.Copy, scale=vr("mlp2", i * 4 + a_))\
                        .then_inc(*tick("out_act", f"{tag}.hi"))

            def stream_out2(name, mode, early=0):
                for i in ev.loop(act, looped(name, 2), peel=early):
                    for s in range(2):
                        hi_next(name, i, s, early=early)
                        for tl in range(2):
                            tile_out(name, i, 2 * s + tl, mode)

            def stream_down(name, mode, last=False, t0=0):
                for i in ev.loop(act, looped(name, 4)):
                    for a_ in range(4):
                        hi_next(name, i, a_, per=4, last=last and a_ == 3)
                        tile_out(name, i, a_, mode, t0)

            def attention(name, pbuf, W, out_rows, out_tile, diff=False):
                def exps(h):
                    act.wait_ge(*at(f"{name}.minus_max{h}"))
                    for i in range(TT):
                        for w in range(W):
                            p_ = ptile(h, i, pbuf(h, w))
                            c = 16 * (h % 2) + 4 * w + i
                            a(p_, p_, ACT.Exp, bias=small[:, c:c + 1], accum_out=small[:, c + 32:c + 33])\
                                .then_inc(*tick(f"{name}_act", f"{name}.exp{h}.{i}.{w}"))

                def copies(h):
                    for i in range(TT):
                        ti = h * TT + i
                        act.wait_ge(*at(f"{name}.turned{ti}"))
                        if h >= 2:
                            act.wait_ge(*at(f"{name}.values{h - 2}"))
                        a(PT[:, h % 2, 0:i + 1, i * P:(i + 1) * P],
                          bank[4 + ti % 2][:, 0:P * (i + 1)].rearrange("p (j n) -> p j n", n=P), ACT.Copy)\
                            .then_inc(*tick(f"{name}_act", f"{name}.copied{ti}"))

                def out(h):
                    act.wait_ge(*at(f"{name}.values{h}"))
                    if diff:
                        a(qO[:, h, :], bank[6 + h % 2][:], ACT.Copy).then_inc(*tick(f"{name}_act", f"{name}.out{h}"))
                        squares("subln", h, qO[:, h, :], f"{name}.out{h}")
                    else:
                        r = out_rows(h)
                        a(hH[r, out_tile(h), :], bank[6 + h % 2][r, :], ACT.Copy)\
                            .then_inc(*tick(f"{name}_act", f"{name}.hi{h}"))

                exps(0)
                for h in range(H):
                    if h + 1 < H:
                        exps(h + 1)
                    if diff and h >= 1:
                        out(h - 1)
                    copies(h)
                    if not diff and h >= 1:
                        out(h - 1)
                    if diff and h == 2:
                        hi_early("odd_out")
                out(H - 1)

            hi(0, 0, 0)
            act.wait_ge(*at("in.eps"))
            act.wait_ge(*at("in.vec"))
            pre("mix_pre0", lambda k: act.wait_ge(*at(f"x0.{k}")))

            act.dma_start(rope[:], dram["rope"]).then_inc(*tick("loaded_rope", "in.rope", 16))

            for u in range(9):
                if u >= 1:
                    act.wait_ge(mm_done, 2 * u if u < 8 else 18)
                    hi(u + 1, (u + 1) // 2, (u + 1) % 2)
                if u == 2:
                    act.wait_ge(evac, 1)
                    a(prob[0:H, 0, 0:512], misc[0:H, :], ACT.Abs, bias=v("b_forget")[0:H, :])\
                        .then_inc(*tick("gate_act", "gate.abs"))
                    act.wait_ge(*at("gate.abs"))
                    a(prob[0:H, 0, 0:512], prob[0:H, 0, 0:512], ACT.Exp, scale=-1.0).then_inc(*tick("gate_act", "gate.exp"))
                    act.wait_ge(*at("gate.exp"))
                    a(prob[0:H, 0, 0:512], prob[0:H, 0, 0:512], ACT.Ln, bias=1.0).then_inc(*tick("gate_act", "gate.ln"))
                    act.wait_ge(evac, 6)
                    for k in range(2):
                        squares("cq", k, y[:, k, :])
                if u == 3:
                    for k in range(2, 5):
                        squares("cq", k, y[:, k, :])
                    root("cq", 5, 384)
                    root("cq", 5, 256, col=4, out=4).then_inc(*tick("norm_act", "cq.root"))
                if u == 6:
                    his("cq", 5, cqH, src=lambda k: y[:, k, :])
            for h in range(H):
                act.wait_ge(*at(f"gate.spread{h}"))
                a(cB[:, h, :], bank[4 + h % 4][:], ACT.Copy).then_inc(*tick("gate_act", f"gate.bias{h}"))

            def half(h):
                return slice(64 * (h % 2), 64 * (h % 2) + 64)
            attention("fox", lambda h, w: prob[:, h % 2, :], 1, half, lambda h: h // 2)
            for u in range(3):
                n = UNIT0["even_uq"] + u
                act.wait_ge(mm_done, TILE0["even_uq"] + 4 * u)
                hi(n + 1, (n + 1) // 2, (n + 1) % 2)
                if u < 2:
                    for hh in range(4):
                        h = 4 * u + hh
                        done("even_uq", h)
                        a(qM[0:96, h, :], bank[h % 4][0:96, :], ACT.Copy, scale=96.0 ** -0.5)\
                            .then_inc(evac, 1)
                else:
                    for h in range(H):
                        done("even_ukv", h)
                        a(kM[0:64, h, :], bank[h % 4][0:64, :], ACT.Copy).then_inc(evac, 1)
                    for t in range(TT):
                        done("even_ukv", H + t)
                        a(vM[:, t, :], bank[t % 4][:], ACT.Copy).then_inc(evac, 1)
            attention("mla", lambda h, w: prob[:, h % 2, :], 1, half, lambda h: 4 + h // 2)
            stream_out2("even_out", "y")

            def norm_summed(tag):
                root(tag, KT, DM).then_inc(*tick("norm_act", f"{tag}.root"))

            def ffn(l):
                norm_summed(f"mix_post{l}")
                hi_early(f"ffn{l}_up0")
                pre(f"ffn_pre{l}", lambda k: act.wait_ge(*at(f"mix_post{l}.x{k}")), f"ffn{l}_up0")
                for g in range(2):
                    name = f"ffn{l}_up{g}"
                    m0 = FF_GROUPS[0] * g
                    for i in ev.loop(act, looped(name, 2), peel=int(g == 0)):
                        for s in range(2):
                            hi_next(name, i, s, early=2 * (g == 0))
                            m = i * 2 + (m0 + s)
                            evacuated(name, i * 4 + 2 * s)
                            a(ft[:, s, :], ft[:, 6 + s, :], ACT.Identity, bias=vr(f"conv{l}", m + 3 * FF_T),
                              scale=vr(f"conv{l}", m + 2 * FF_T)).then_inc(*tick(f"ffn_act", f"{name}.tap2.{s}"))
                            act.wait_ge(*at(f"{name}.tap0.{s}", i))
                            a(ft[:, 2 + s, :], ft[:, s, :], ACT.Gelu_apprx_tanh).then_inc(*tick("ffn_act", f"{name}.gelu{s}"))
                            act.wait_ge(*at(f"{name}.mid{s}", i))
                            a(mH[:, bass.ds(i * 2 + s, 1), :], ft[:, 4 + s, :].unsqueeze(1), ACT.Copy)\
                                .then_inc(*tick("ffn_act", f"{name}.hi{s}"))
                    stream_down(f"ffn{l}_down{g}", "y0" if g == 0 else "y1")
                norm_summed(f"ffn_post{l}")

            ffn(0)

            hi_early("odd_q")
            pre("mix_pre1", lambda k: act.wait_ge(*at(f"ffn_post0.x{k}")), "odd_q")
            act.dma_start(dist[:], dram["dist"]).then_inc(*tick("loaded_dist", "in.dist", 16))
            act.wait_ge(*at("lam.dots"))
            a(lamt[:, 66:68], lamt[:, 64:66], ACT.Exp).then_inc(*tick("lam_act", "lam.exp"))
            stream_plain("odd_q", early=2)
            stream_plain("odd_k")
            stream_plain("odd_v")
            attention("diff", lambda h, w: probO[:, h % 2, w, :], 2, None, None, diff=True)
            root("subln", H, P, w=32, col=FAR, b=4).then_inc(*tick("norm_act", "subln.root"))
            his("subln", H, src=lambda k: y[:, 4 + k % 4, :])
            stream_out2("odd_out", "y", early=1)
            ffn(1)

            hi_early("dn_qkv")
            pre("mix2", lambda k: act.wait_ge(*at(f"ffn_post1.x{k}")), "dn_qkv")
            act.dma_start(dconst[:], dram["dconst"]).then_inc(*tick("loaded_dconst", "in.dconst", 16))
            act.dma_start(wba[:], dram["wba"]).then_inc(*tick("loaded_wba", "in.wba", 16))
            for i in ev.loop(act, looped("dn_qkv", 2), peel=1):
                for s in range(2):
                    hi_next("dn_qkv", i, s, early=2)
                    for tl in range(2):
                        c = 2 * s + tl
                        evacuated("dn_qkv", i * 4 + c)
                        a(y[:, c, :], y[:, 4 + c, :], ACT.Copy, scale=vr("dn_conv", i * 4 + (c + 72)))\
                            .then_inc(*tick("dn_conv_act", f"dn.tap3.{c}"))
                    for tl in range(2):
                        c = 2 * s + tl
                        act.wait_ge(*at(f"dn.tap0.{c}", i))
                        a(qkv[:, bass.ds(i * 4 + c, 1), :], y[:, c, :].unsqueeze(1), ACT.Silu)\
                            .then_inc(*tick("dn_conv_act", f"dn.silu{c}"))
                if peeled(i):
                    act.wait_ge(*at("in.wba"))
                    a(wbaH[:], wba[:], ACT.Copy).then_inc(*tick("dn_act", "dn.wba_hi"))
            act.wait_ge(*at("dn.z"))
            a(tok[:, 0, :].rearrange("p (h t) -> p t h", t=TT), zed[:, :, 8:16], ACT.Sigmoid).then_inc(*tick("dn_act", "dn.beta"))
            za = zed[:].rearrange("p t (w h) -> p t w h", w=2)
            act.wait_ge(*at("dn.beta"))
            a(za[:, :, 1, :], za[:, :, 0, :], ACT.Abs).then_inc(*tick("dn_act", "dn.abs"))
            act.wait_ge(*at("dn.abs"))
            a(za[:, :, 1, :], za[:, :, 1, :], ACT.Exp, scale=-1.0).then_inc(*tick("dn_act", "dn.expabs"))
            a(tok[:, 12, 0:8], v("a_log", 0, 8), ACT.Exp).then_inc(*tick("dn_act", "dn.expa"))
            act.wait_ge(*at("dn.expabs"))
            a(za[:, :, 1, :], za[:, :, 1, :], ACT.Ln, bias=1.0).then_inc(*tick("dn_act", "dn.ln"))
            for i in ev.loop(act, looped("dn_z", 2), peel=1):
                for s in range(2):
                    hi_next("dn_z", i, s)
                    for a_ in range(4):
                        if a_ == 0:
                            act.wait_ge(*(at("dn.sum0", i) if s else at("dn.sum1", i - 1)))
                        a(y[:, 4 + a_, :].unsqueeze(1), qkv[:, bass.ds(i * 8 + (4 * s + a_), 1), :], ACT.Square)\
                            .then_inc(*tick("dn_sq_act", f"dn.sq{s}.{a_}"))
                    for tl in range(2):
                        c = 2 * s + tl
                        evacuated("dn_z", i * 4 + c)
                        a(zT[:, bass.ds(i * 4 + c, 1), :], y[:, c, :].unsqueeze(1), ACT.Silu).then_inc(*tick("dn_z_act", f"dn.silu_z{c}"))
                if peeled(i):
                    act.wait_ge(*at("dn.gc"))
                    a(tok[:, 2, :], bank[5][:, 0:32], ACT.Copy).then_inc(*tick("dn_act", "dn.gc_copied"))
                    a(tok[:, 3, :], bank[5][:, 32:64], ACT.Copy).then_inc(*tick("dn_act", "dn.tot_copied"))
            act.wait_ge(*at("dn.sum1", looped("dn_z", 2) - 1))
            a(tok[:, 14:16, :].rearrange("p a b -> p (a b)"), bank[7][:, 0:64], ACT.Sqrt, bias=eps)\
                .then_inc(*tick("dn_act", "dn.root"))
            a(tok[:, 4, :], tok[:, 2, :], ACT.Exp).then_inc(*tick("dn_act", "dn.egc"))
            act.wait_ge(*at("dn.left"))
            a(tok[:, 5, :], tok[:, 5, :], ACT.Exp).then_inc(*tick("dn_act", "dn.eleft"))
            act.wait_ge(*at("dn.rows_turned"))
            a(rowsT[0:96, :], bank[4][0:96, 0:P], ACT.Copy).then_inc(*tick("dn_act", "dn.rows"))
            for h0 in range(0, H, 2):
                pair = [(h0 + p, [bank[4 * p + b] for b in range(4)], tmp(p)) for p in range(2)]
                for h, b, m in pair:
                    act.wait_ge(*at(f"dn.spread{h}"))
                    if h >= 2:
                        act.wait_ge(*at(f"dn.qdec{h - 2}"))
                    a(m["e"], b[2][:], ACT.Exp).then_inc(*tick("dn_act", f"dn.e{h}"))
                for h, b, m in pair:
                    act.wait_ge(*at(f"dn.diff{h}"))
                    a(m["x"], m["lt"], ACT.Exp).then_inc(*tick("dn_act", f"dn.dec{h}"))
                    act.wait_ge(*at(f"dn.e{h}"))
                    a(gl[:, h, :], m["e"][:, 63::64], ACT.Copy).then_inc(*tick("dn_act", f"dn.gl{h}"))
                for h, b, m in pair:
                    act.wait_ge(*at(f"dn.turned{h}"))
                    for t in range(TT):
                        c, r = slice(t * P, (t + 1) * P), 4 * h + t
                        a(m["r"][:, c], b[3][:, c], ACT.Copy, scale=tok[:, 6, r:r + 1])
                        last = a(kdec[:, h, c], b[3][:, c], ACT.Copy, scale=tok[:, 7, r:r + 1])
                    last.then_inc(*tick("dn_act", f"dn.tok{h}"))
                    act.wait_ge(*at(f"dn.xt{h}"))
                    act.wait_ge(*at(f"dn.attn{h}"))
                    a(m["x"], b[0][:], ACT.Copy).then_inc(*tick("dn_act", f"dn.x{h}.0"))
                for h, b, m in pair:
                    act.wait_ge(*at(f"dn.uw{h}"))
                    a(qkv[:, 16 + h, :], b[0][:], ACT.Copy)
                    a(qkv[:, 8 + h, :], b[1][:], ACT.Copy).then_inc(*tick("dn_act", f"dn.w{h}"))
            for n in range(8):
                act.wait_ge(*at(f"scan.out{n}"))
                a(qkv[:, 0:H, 64 * n:64 * n + 64], bank[4 + n % 2][:].rearrange("p (h c) -> p h c", h=H), ACT.Copy)\
                    .then_inc(*tick("scan_act", f"scan.o{n}"))
                if n == 2:
                    hi_early("dn_out")
                if n % 2:
                    t = n // 2
                    act.wait_ge(*at(f"scan.o{n}"))
                    if t >= 1:
                        act.wait_ge(*at(f"gated.sum{t - 1}"))
                    a(sq_heads, qkv[:, 0:H, t * P:(t + 1) * P], ACT.Square).then_inc(*tick("squares_act", f"gated.sq{t}"))
            act.wait_ge(*at("gated.sums_scaled"))
            a(small[:, 0:32], stat[:, 0:32], ACT.Sqrt, bias=eps, scale=1.0 / P).then_inc(*tick("norm_act", "gated.root"))
            his("gated", H, oH, src=lambda k: y[:, 4 + k % 4, :])
            stream_out2("dn_out", "x1", early=1)
            hi_early("mlp_up0")
            norm_summed("mlp2")
            hi_early("mlp_up0", 2)
            for g in range(2):
                name = f"mlp_up{g}"
                for i in ev.loop(act, looped(name, 2), peel=int(g == 0)):
                    for s in range(2):
                        hi_next(name, i, s, early=2 * (g == 0))
                        for tl in range(2):
                            c = 2 * s + tl
                            act.wait_ge(*at(f"{name}.mid{c}", i))
                            a(mH[:, bass.ds(i * 4 + c, 1), :], y[:, 4 + c, :].unsqueeze(1), ACT.Copy)\
                                .then_inc(*tick("mlp_act", f"{name}.hi{c}"))
                stream_down(f"mlp_down{g}", ("x0", "x1")[g])
            stream_down("mlp_down2", "x1", last=True, t0=4)
            norm_summed("final")
            act.wait_ge(*at("final.inverse"))
            for t in range(TT):
                act.wait_ge(*at(f"out.turned{t}.0"))
                a(xin[:, t, 0:512], bank[(4 + 2 * t) % 7][:], ACT.Copy, scale=stat[:, t:t + 1])\
                    .then_inc(*tick("out_scaled_act", f"out.copied{t}.0"))

        @block.vector
        def _(dve):
            tt, ts, stt = nc.vector.tensor_tensor, nc.vector.tensor_scalar, nc.vector.scalar_tensor_tensor

            def chain(ins, name, event, i=None):
                ins.then_inc(*tick(name, event))
                dve.wait_ge(*at(event, i))

            def lo(n, s):
                dve.wait_ge(w_hi, n + 1)
                tt(wL[s][:], raw[s][:], wH[s][:].bitcast(F32), ALU.subtract).then_inc(w_split, 1)

            def lo_next(name, i, s, per=2, last=False, early=0):
                if not (last or peeled(i) and s < early):
                    n0 = UNIT0[name] + s
                    lo(i * per + (n0 + 1), (n0 + 1) % 2)

            def done(name, l):
                dve.wait_ge(mm_done, l + (TILE0[name] + 1))

            def diagonal(out, col):
                return tt(out.rearrange("p (t n) -> p t n", t=TT), ident.unsqueeze(1).to_broadcast([P, TT, P]),
                          stat[:, col:col + TT].unsqueeze(2).to_broadcast([P, TT, P]), ALU.mult)

            def inverse(tag, name=None):
                dve.wait_ge(*at(f"{tag}.root"))
                chain(nc.vector.reciprocal(stat[:, 0:TT], small[:, 0:TT]), "norm_dve", f"{tag}.inverse")
                diagonal(dg[:].rearrange("p t n -> p (t n)"), 0).then_inc(*tick("norm_dve", f"{tag}.diag"))
                if name is not None:
                    lo_early(name, 2)
                dve.wait_ge(*at(f"{tag}.spread"))

            def inverse_kept(tag, name):
                inverse(tag, name)
                chain(nc.vector.tensor_copy(rinv, bank[6][:]), "norm_dve", f"{tag}.kept")

            def lo_tile(tag, k, src, H_=hH, L_=hL):
                dve.wait_ge(*at(f"{tag}.hi{k}"))
                tt(L_[:, k, :], src, H_[:, k, :].bitcast(F32), ALU.subtract).then_inc(*tick("norm_dve", f"{tag}.h{k}"))

            def lo_early(name, u=1):
                n = UNIT0[name] + u
                lo(n, n % 2)

            def lo_pre(tag, k):
                dve.wait_ge(*at(f"{tag}.hi{k}"))
                stt(hL[:, k, :], x[:, k, :], v(tag, k), hH[:, k, :].bitcast(F32), ALU.mult, ALU.subtract)\
                    .then_inc(*tick("norm_dve", f"{tag}.u{k}"))

            def post_pre(post, tag, name):
                dve.wait_ge(*at(f"{post}.root"))
                chain(nc.vector.reciprocal(stat[:, 0:TT], small[:, 0:TT]), "norm_dve", f"{post}.inverse")
                diagonal(dg[:].rearrange("p t n -> p (t n)"), 0).then_inc(*tick("norm_dve", f"{post}.diag"))
                dve.wait_ge(*at(f"{post}.spread"))
                for k in range(KT + 3):
                    if k < KT:
                        stt(y[:, k, :], y[:, k, :], v(post, k), bank[6][:], ALU.mult, ALU.mult)\
                            .then_inc(*tick("norm_dve", f"{post}.t{k}"))
                    if k == 1:
                        dve.wait_ge(*at(f"{post}.t0"))
                        tt(x[:, 0, :], x[:, 0, :], y[:, 0, :], ALU.add).then_inc(*tick("norm_dve", f"{post}.x0"))
                    if k >= 3:
                        lo_pre(tag, k - 3)
                lo_early(name)
                last_squares(tag)
                inverse_kept(tag, name)

            def last_squares(tag):
                dve.wait_ge(*at(f"{tag}.sq{KT - 1}"))
                chain(tt(ss[:], y[:, KT - 2, :], y[:, KT - 1, :], ALU.add), "norm_dve", f"{tag}.last_squares")
                dve.wait_ge(*at(f"{tag}.first_squares"))
                tt(ss[:], ss[:], y[:, 0, :], ALU.add).then_inc(*tick("norm_dve", f"{tag}.ss"))

            def stream_scaled(name, dst, early=0, scale=1.0):
                for i in ev.loop(dve, looped(name, 2), peel=int(early > 0 or name == "dn_z")):
                    for s in range(2):
                        lo_next(name, i, s, early=early)
                        for tl in range(2):
                            c = 2 * s + tl
                            done(name, i * 4 + c)
                            if name == "dn_z":
                                if not peeled(i):
                                    dve.wait_ge(*at(f"dn.silu_z{c}", i - 1))
                            stt(dst(i, c), bank[c][:].unsqueeze(1), scale, rinv.unsqueeze(1), ALU.mult, ALU.mult)\
                                .then_inc(evac, 1)

            def clear_sums(name):
                for q in range(4):
                    last = nc.vector.memset(ss[:, q * P:(q + 1) * P], 0.0)
                    last.then_inc(*tick("sums_dve", f"{name}.clear{q}"))

            def tile_out(name, i, a_, mode, t0=0):
                tag = f"{name}.tile{a_}"
                if mode == "y0":
                    return
                if mode != "y":
                    done(name, i * 4 + a_)
                    dst = (x if mode[0] == "x" else y)[:, bass.ds(i * 4 + (a_ + t0), 1), :]
                    tt(dst, dst, bank[a_][:].unsqueeze(1), ALU.add).then_inc(evac, 1)
                    if mode == "x0":
                        return
                dve.wait_ge(*at(f"{tag}.sq", i))
                dve.wait_ge(*(at(f"{name}.tile{a_ - 1}.ss", i) if a_ else at(f"{name}.tile3.ss", i - 1)))
                tt(ss[:], ss[:], sq[:, a_ % 2, :], ALU.add).then_inc(*tick("sums_dve", f"{tag}.ss"))
                if name == "dn_out":
                    dve.wait_ge(*at(f"{tag}.hi", i))
                    k = bass.ds(i * 4 + a_, 1)
                    stt(hL[:, k, :], dst, vr("mlp2", i * 4 + a_), hH[:, k, :].bitcast(F32), ALU.mult, ALU.subtract)\
                        .then_inc(*tick("out_dve", f"{name}.u{a_}"))

            def stream_out2(name, mode, early=0):
                clear_sums(name)
                for i in ev.loop(dve, looped(name, 2), peel=early):
                    for s in range(2):
                        lo_next(name, i, s, early=early)
                        for tl in range(2):
                            tile_out(name, i, 2 * s + tl, mode)

            def stream_down(name, mode, last=False, t0=0):
                if mode in ("y1", "x1") and t0 == 0:
                    clear_sums(name)
                for i in ev.loop(dve, looped(name, 4)):
                    for a_ in range(4):
                        lo_next(name, i, a_, per=4, last=last and a_ == 3)
                        tile_out(name, i, a_, mode, t0)

            def attention(name, bias, pbuf, W, finish):
                def biased(h):
                    if name == "diff":
                        dve.wait_ge(*at(f"alibi{h}"))
                    for i in range(TT):
                        if h >= 2:
                            dve.wait_ge(*at(f"{name}.turned{(h - 2) * TT + i}"))
                        for w in range(W):
                            j = (h * TT + i) * W + w
                            n, c = P * (i + 1), 8 * (h % 2) + 4 * w + i
                            dve.wait_ge(*at(f"{name}.scores{j}"))
                            nc.vector.tensor_tensor_reduce(ptile(h, i, pbuf(h, w)), bank[j % 4][:, 0:n], bias(h, i), 1.0,
                                                           -3.0e38, ALU.add, ALU.max, stat[:, c:c + 1])\
                                .then_inc(*tick(f"{name}_dve", f"{name}.biased{j}"))
                    c = 16 * (h % 2)
                    dve.wait_ge(*at(f"{name}.biased{j}"))
                    if h >= 2:
                        dve.wait_ge(*at(f"{name}.exp{h - 2}.{TT - 1}.{W - 1}"))
                    ts(small[:, c:c + 4 * W], stat[:, c // 2:c // 2 + 4 * W], -1.0, None, ALU.mult)\
                        .then_inc(*tick(f"{name}_dve", f"{name}.minus_max{h}"))

                def divided(h):
                    c = 16 * (h % 2) + 32
                    q = 16 + 16 * (h % 2)
                    dve.wait_ge(*at(f"{name}.exp{h}.{TT - 1}.{W - 1}"))
                    chain(nc.vector.reciprocal(stat[:, q:q + 4 * W], small[:, c:c + 4 * W]), f"{name}_dve", f"{name}.inverse{h}")
                    if W == 2:
                        chain(ts(stat[:, q + 4:q + 8], stat[:, q + 4:q + 8], lamt[:, 68:69], None, ALU.mult), f"{name}_dve", f"{name}.lam{h}")
                        for i in range(TT):
                            p2 = ptile(h, i, pbuf(h, 1))
                            ts(p2, p2, stat[:, q + 4 + i:q + 5 + i], None, ALU.mult).then_inc(*tick(f"{name}_dve", f"{name}.second{h}.{i}"))
                    for i in range(TT):
                        p_ = ptile(h, i, pbuf(h, 0))
                        if W == 2:
                            p2 = ptile(h, i, pbuf(h, 1))
                            dve.wait_ge(*at(f"{name}.second{h}.{i}"))
                            ins = stt(p_, p_, stat[:, q + i:q + i + 1], p2, ALU.mult, ALU.add)
                        else:
                            ins = ts(p_, p_, stat[:, q + i:q + i + 1], None, ALU.mult)
                        ins.then_inc(*tick(f"{name}_dve", f"{name}.prob{h}.{i}"))

                biased(0)
                for h in range(H):
                    if h + 1 < H:
                        biased(h + 1)
                    divided(h)
                    if h >= 2:
                        finish(h - 2)
                    if name == "diff" and h == 3:
                        lo_early("odd_out")
                finish(H - 2)
                finish(H - 1)

            nc.vector.memset(eps, EPS).then_inc(*tick("norm_dve", "in.eps"))
            lo(0, 0)
            dve.wait_ge(*at("in.vec"))
            dve.wait_ge(*at("in.const"))
            for k in range(KT + 2):
                if k < KT:
                    dve.wait_ge(*at(f"x0.turned{k}"))
                    nc.vector.tensor_copy(x[:, k, :], bank[2 + k % 4][:]).then_inc(*tick("input_dve", f"x0.{k}"))
                if k >= 2:
                    lo_pre("mix_pre0", k - 2)
            lo(1, 1)
            last_squares("mix_pre0")
            inverse_kept("mix_pre0", "even_in")
            nc.vector.tensor_copy(stat[:, 56:60], stat[:, 0:TT]).then_inc(*tick("norm_dve", "mix_pre0.tokens"))

            def e_tile(l, dst, b, scale=1.0):
                dve.wait_ge(mm_done, l + 1)
                stt(dst, b, scale, rinv, ALU.mult, ALU.mult).then_inc(evac, 1)

            for u in range(9):
                if u >= 2:
                    lo(u + 1, (u + 1) % 2)
                for tl in range(2 if u < 7 else 0):
                    l = 2 * u + tl
                    b = bank[2 * (u % 2) + tl][:]
                    if l == 0:
                        e_tile(l, misc[:], b)
                    elif l < 6:
                        e_tile(l, y[:, l - 1, :], b)
                    elif l < 10:
                        e_tile(l, qF[:, l - 6, :], b, 0.125)
                    else:
                        e_tile(l, kF[:, l - 10, :], b)
                if u >= 7:
                    dve.wait_ge(*at("mix_pre0.tokens"))
                    for t in range(TT):
                        l = 14 + 4 * (u - 7) + t
                        dve.wait_ge(mm_done, l + 1)
                        ts(vF[:, t, 256 * (u - 7):256 * (u - 6)], bank[(2 + t) % 4][:, 0:256], stat[:, 56 + t:57 + t], None,
                           ALU.mult).then_inc(evac, 1)
                if u == 2:
                    z, l_, one, neg = prob[0:H, 0, 512:1024], prob[0:H, 0, 0:512], prob[0:H, 1, 0:512], prob[0:H, 1, 512:1024]
                    dve.wait_ge(evac, 1)
                    nc.vector.memset(one, 1.0)
                    chain(ts(z, misc[0:H, :], v("b_forget")[0:H, :], 0.0, ALU.add, ALU.min), "gate_dve", "gate.min")
                    dve.wait_ge(*at("gate.ln"))
                    chain(tt(z, z, l_, ALU.subtract), "gate_dve", "gate.logf")
                    chain(nc.vector.tensor_tensor_scan(l_, one, z, 0.0, ALU.mult, ALU.add), "gate_dve", "gate.summed")
                    ts(neg, l_, -1.0, None, ALU.mult).then_inc(*tick("gate_dve", "gate.rows"))
                if u == 4:
                    dve.wait_ge(*at("cq.root"))
                    chain(nc.vector.reciprocal(stat[:, 0:8], small[:, 0:8]), "norm_dve", "cq.inverse")
                    diagonal(y[:, 5, :], 0).then_inc(*tick("norm_dve", "cq.diag"))
                    diagonal(y[:, 6, :], 4).then_inc(*tick("norm_dve", "ckv.diag"))
                if u == 6:
                    dve.wait_ge(*at("ckv.spread"))
                    for k in range(6):
                        if k < 5:
                            g = v("q_norm", k) if k < 3 else v("kv_norm", k - 3)
                            stt(y[:, k, :], y[:, k, :], g, bank[5 if k < 3 else 4][:], ALU.mult, ALU.mult)\
                                .then_inc(*tick("norm_dve", f"cq.t{k}"))
                        if k >= 1:
                            lo_tile("cq", k - 1, y[:, k - 1, :], cqH, cqL)

            def halves(name, tile0):
                def finish(h):
                    r = slice(64 * (h % 2), 64 * (h % 2) + 64)
                    dve.wait_ge(*at(f"{name}.hi{h}"))
                    k = tile0 + h // 2
                    tt(hL[r, k, :], bank[6 + h % 2][r, :], hH[r, k, :].bitcast(F32), ALU.subtract)\
                        .then_inc(*tick(f"{name}_dve", f"{name}.out{h}"))
                return finish
            dve.wait_ge(*at(f"gate.bias{H - 1}"))
            attention("fox", lambda h, i: cB[:, h, 0:P * (i + 1)], lambda h, w: prob[:, h % 2, :], 1, halves("fox", 0))
            cos, sin = rope[64:96, 0:512], rope[64:96, 512:1024]

            def rotary(r):
                dve.wait_ge(*at(f"rope.turned{r}"))
                if r >= 1:
                    dve.wait_ge(evac, TILE0["even_uq"] + r)
                src = misc[64:96, :] if r == 0 else qM[64:96, r - 1, :]
                t_ = y[64:96, r % 2, :]
                tt(t_, bank[4 + r % 2][64:96, :], sin, ALU.mult).then_inc(*tick("rope_dve", f"rope.sin{r}"))
                chain(tt(src, src, cos, ALU.mult), "rope_dve", f"rope.cos{r}")
                tt(src, src, t_, ALU.add).then_inc(*tick("rope_dve", "rope.key" if r == 0 else f"rope.q{r - 1}"))
            for u in range(3):
                n = UNIT0["even_uq"] + u
                lo(n + 1, (n + 1) % 2)
                if u == 1:
                    for r in range(H + 1):
                        rotary(r)
            attention("mla", lambda h, i: window[:, FAR - P * i:], lambda h, w: prob[:, h % 2, :], 1, halves("mla", 4))
            stream_out2("even_out", "y")

            def ffn(l):
                post_pre(f"mix_post{l}", f"ffn_pre{l}", f"ffn{l}_up0")
                for g in range(2):
                    name = f"ffn{l}_up{g}"
                    for i in ev.loop(dve, looped(name, 2), peel=int(g == 0)):
                        for s in range(2):
                            lo_next(name, i, s, early=2 * (g == 0))
                            m = i * 2 + (FF_GROUPS[0] * g + s)
                            c, gate, mid = ft[:, s, :], ft[:, 6 + s, :], ft[:, 4 + s, :]
                            done(name, i * 4 + 2 * s)
                            tt(gate, bank[2 * s][:], rinv, ALU.mult).then_inc(evac, 1)
                            dve.wait_ge(*at(f"{name}.tap2.{s}", i))
                            chain(stt(c[:, 1:], gate[:, 0:SEQ - 1], vr(f"conv{l}", m + FF_T), c[:, 1:], ALU.mult, ALU.add),
                                  "ffn_dve", f"{name}.tap1.{s}", i)
                            stt(c[:, 2:], gate[:, 0:SEQ - 2], vr(f"conv{l}", m), c[:, 2:], ALU.mult, ALU.add)\
                                .then_inc(*tick("ffn_dve", f"{name}.tap0.{s}"))
                            done(name, i * 4 + (2 * s + 1))
                            tt(mid, bank[2 * s + 1][:], rinv, ALU.mult).then_inc(evac, 1)
                            dve.wait_ge(*at(f"{name}.gelu{s}", i))
                            dve.wait_ge(evac, i * 4 + (2 * s + 2 + TILE0[name]))
                            tt(mid, ft[:, 2 + s, :], mid, ALU.mult).then_inc(*tick("ffn_dve", f"{name}.mid{s}"))
                            dve.wait_ge(*at(f"{name}.hi{s}", i))
                            t1 = bass.ds(i * 2 + s, 1)
                            tt(mL[:, t1, :], ft[:, 4 + s, :].unsqueeze(1), mH[:, t1, :].bitcast(F32), ALU.subtract)\
                                .then_inc(*tick("ffn_dve", f"{name}.lo{s}"))
                    stream_down(f"ffn{l}_down{g}", "y0" if g == 0 else "y1")
                if l == 0:
                    post_pre("ffn_post0", "mix_pre1", "odd_q")
                else:
                    post_pre("ffn_post1", "mix2", "dn_qkv")

            ffn(0)

            nc.vector.tensor_copy(stat[:, 56:60], stat[:, 0:TT]).then_inc(*tick("norm_dve", "mix_pre1.tokens"))
            lam = v("lam", 0, 256)
            for w, event in enumerate(("lam.first", "lam.dots")):
                o = 128 * w
                chain(nc.vector.tensor_tensor_reduce(lamt[:, 0:64], lam[:, o:o + 64], lam[:, o + 64:o + 128], 1.0, 0.0,
                                                     ALU.mult, ALU.add, lamt[:, 64 + w:65 + w]), "lam_dve", event)
            dve.wait_ge(*at("lam.exp"))
            chain(tt(lamt[:, 68:69], lamt[:, 67:68], lamt[:, 66:67], ALU.subtract), "lam_dve", "lam.difference")
            ts(lamt[:, 68:69], lamt[:, 68:69], -LAMBDA_INIT, None, ALU.add).then_inc(*tick("lam_dve", "lam.minus"))
            ts(lamt[:, 70:71], v("subln"), 1.0 - LAMBDA_INIT, None, ALU.mult).then_inc(*tick("lam_dve", "lam.gain"))
            stream_scaled("odd_q", lambda i, c: qO[:, bass.ds(i * 4 + c, 1), :], early=2, scale=0.125)
            stream_scaled("odd_k", lambda i, c: kO[:, bass.ds(i * 4 + c, 1), :])
            dve.wait_ge(*at("mix_pre1.tokens"))
            for i in ev.loop(dve, looped("odd_v", 2)):
                for s in range(2):
                    lo_next("odd_v", i, s)
                    for t in range(TT):
                        done("odd_v", i * 8 + (4 * s + t))
                        ts(vO[:, t, bass.ds(i * 512 + 256 * s, 256)], bank[t][:, 0:256], stat[:, 56 + t:57 + t], None, ALU.mult)\
                            .then_inc(evac, 1)
            dve.wait_ge(*at("lam.gain"))
            attention("diff", lambda h, i: alibi[:, h % 2, FAR - P * i:], lambda h, w: probO[:, h % 2, w, :], 2, lambda h: None)

            def head_norms(tag, src, gain, H_=hH, L_=hL):
                for h in range(H + 3):
                    if h < H:
                        if h >= 4:
                            dve.wait_ge(*at(f"{tag}.spread{h - 4}"))
                        diagonal(y[:, h % 4, :], 4 * h).then_inc(*tick("norm_dve", f"{tag}.diag{h}"))
                    if h >= 3:
                        lo_tile(tag, h - 3, y[:, 4 + (h - 3) % 4, :], H_, L_)
                    if 1 <= h <= H:
                        dve.wait_ge(*at(f"{tag}.spread{h - 1}"))
                        stt(y[:, 4 + (h - 1) % 4, :], src(h - 1), gain, bank[4 + (h - 1) % 4][:], ALU.mult, ALU.mult)\
                            .then_inc(*tick("norm_dve", f"{tag}.t{h - 1}"))

            dve.wait_ge(*at("subln.root"))
            chain(nc.vector.reciprocal(stat[:, 0:32], small[:, 0:32]), "norm_dve", "subln.inverse")
            head_norms("subln", lambda h: qO[:, h, :], lamt[:, 70:71])
            stream_out2("odd_out", "y", early=1)
            ffn(1)

            for i in ev.loop(dve, looped("dn_qkv", 2), peel=1):
                for s in range(2):
                    lo_next("dn_qkv", i, s, early=2)
                    for tl in range(2):
                        c = 2 * s + tl
                        done("dn_qkv", i * 4 + c)
                        tt(y[:, 4 + c, :], bank[c][:], rinv, ALU.mult).then_inc(evac, 1)
                    for tap in (2, 1, 0):
                        for c in (2 * s, 2 * s + 1):
                            d = 3 - tap
                            dve.wait_ge(*at(f"dn.tap{tap + 1}.{c}", i))
                            stt(y[:, c, d:], y[:, 4 + c, 0:SEQ - d], vr("dn_conv", i * 4 + (c + 24 * tap)), y[:, c, d:],
                                ALU.mult, ALU.add).then_inc(*tick("dn_conv_dve", f"dn.tap{tap}.{c}"))
                if peeled(i):
                    dve.wait_ge(*at("dn.wba_hi"))
                    tt(wbaL[:], wba[:], wbaH[:].bitcast(F32), ALU.subtract).then_inc(*tick("dn_dve", "dn.wba"))
            dve.wait_ge(*at("dn.ba_rows"))
            tt(vN[0:16, 0:TT, :].rearrange("p t n -> p (t n)"), bank[5][0:16, :], rinv[0:16, :], ALU.mult)\
                .then_inc(*tick("dn_dve", "dn.ba_scaled"))
            dve.wait_ge(*at("dn.ba"))
            ba = bank[4][:, 0:64].rearrange("p (t c) -> p t c", c=16)
            za = zed[:].rearrange("p t (w h) -> p t w h", w=2)
            tt(zed[:, :, 0:8], ba[:, :, 8:16], v("dt_bias", 0, 8).unsqueeze(1).to_broadcast([P, TT, 8]), ALU.add)
            nc.vector.tensor_copy(zed[:, :, 8:16], ba[:, :, 0:8]).then_inc(*tick("dn_dve", "dn.z"))
            dve.wait_ge(*at("dn.z"))
            dve.wait_ge(*at("dn.ln"))
            chain(stt(za[:, :, 0, :], za[:, :, 0, :], 0.0, za[:, :, 1, :], ALU.max, ALU.add), "dn_dve", "dn.softplus")
            stt(tok[:, 1, :].rearrange("p (h t) -> p t h", t=TT), za[:, :, 0, :], -1.0,
                tok[:, 12, 0:8].unsqueeze(1).to_broadcast([P, TT, 8]), ALU.mult, ALU.mult).then_inc(*tick("dn_dve", "dn.g"))
            stream_scaled("dn_z", lambda i, c: y[:, c:c + 1, :])
            dve.wait_ge(*at("dn.tot_copied"))
            tt(tok[:, 5, :], tok[:, 3, :], tok[:, 2, :], ALU.subtract).then_inc(*tick("dn_dve", "dn.left"))
            nc.vector.tensor_copy(tok[:, 10, :], tok[:, 2, :])
            for g in range(2):
                nc.vector.memset(S[:, 4 * g:4 * g + 4, :], 0.0).then_inc(*tick("scan_dve", f"scan.state-1.{g}"))
            dve.wait_ge(*at("dn.root"))
            roots = tok[:, 14:16, :].rearrange("p a b -> p (a b)")
            chain(nc.vector.reciprocal(roots, roots), "dn_dve", "dn.inverse")
            tt(tok[:, 8, :], tok[:, 0, :], tok[:, 15, :], ALU.mult).then_inc(*tick("dn_dve", "dn.beta_k"))
            ts(tok[:, 9, :], tok[:, 14, :], float(P) ** -0.5, None, ALU.mult).then_inc(*tick("dn_dve", "dn.rowset"))
            dve.wait_ge(*at("dn.eleft"))
            dve.wait_ge(*at("dn.rowset"))
            tt(tok[:, 6, :], tok[:, 8, :], tok[:, 4, :], ALU.mult)
            tt(tok[:, 11, :], tok[:, 9, :], tok[:, 9, :], ALU.mult)
            tt(tok[:, 7, :], tok[:, 15, :], tok[:, 5, :], ALU.mult).then_inc(*tick("dn_dve", "dn.scalars"))
            dve.wait_ge(*at("dn.scalars"))
            tiles = [slice(t * P, (t + 1) * P) for t in range(TT)]

            def masked(m):
                return dconst[:, m * P:(m + 1) * P].unsqueeze(1).to_broadcast([P, TT, P])

            def blocks(ap):
                return ap.rearrange("p (t n) -> p t n", t=TT)
            for h0 in range(0, H, 2):
                pair = [(h0 + p, [bank[4 * p + b] for b in range(4)], tmp(p)) for p in range(2)]
                for h, b, m in pair:
                    dve.wait_ge(*at(f"dn.spread{h}"))
                    tt(m["t1"], qkv[:, 8 + h, :], b[0][:], ALU.mult).then_inc(*tick("dn_dve", f"dn.qn{h}"))
                for h, b, m in pair:
                    dve.wait_ge(*at(f"dn.e{h}"))
                    for t, c in enumerate(tiles):
                        last = stt(m["lt"][:, c], b[2][:, c], tok[:, 2, 4 * h + t:4 * h + t + 1], dconst[:, 8 * P:9 * P],
                                   ALU.subtract, ALU.min)
                    last.then_inc(*tick("dn_dve", f"dn.diff{h}"))
                for h, b, m in pair:
                    dve.wait_ge(*at(f"dn.gram{h}"))
                    dve.wait_ge(*at(f"dn.dec{h}"))
                    for t, c in enumerate(tiles):
                        r = 32 + 4 * h + t
                        last = stt(m["lt"][:, c], b[0][:, c], roots[:, r:r + 1], m["x"][:, c], ALU.mult, ALU.mult)
                    chain(last, "dn_dve", f"dn.lower{h}")
                    chain(tt(blocks(m["y"]), blocks(m["lt"]), masked(2), ALU.mult), "dn_dve", f"dn.first{h}")
                    tt(blocks(m["y"]), ident.unsqueeze(1).to_broadcast([P, TT, P]), blocks(m["y"]), ALU.subtract)\
                        .then_inc(*tick("dn_dve", f"dn.y{h}.0"))
                    for t, c in enumerate(tiles):
                        r = 32 + 4 * h + t
                        last = stt(attnT[:, h, c], b[1][:, c], roots[:, r:r + 1], m["x"][:, c], ALU.mult, ALU.mult)
                    last.then_inc(*tick("dn_dve", f"dn.attn{h}"))
                for h, b, m in pair:
                    dve.wait_ge(*at(f"dn.turned{h}"))
                    tt(blocks(qkv[:, 16 + h, :]), blocks(b[2][:]), tok[:, 0, 4 * h:4 * h + 4].unsqueeze(2).to_broadcast([P, TT, P]),
                       ALU.mult).then_inc(*tick("dn_dve", f"dn.values{h}"))
                for s in range(1, 6):
                    for h, b, m in pair:
                        dve.wait_ge(*at(f"dn.lx{h}.{s}"))
                        tt(blocks(m["t1"]), blocks(b[1][:]), masked(2 + s), ALU.mult).then_inc(*tick("dn_dve", f"dn.t{h}.{s}"))
                    for h, b, m in pair:
                        dve.wait_ge(*at(f"dn.xx{h}.{s}"))
                        dve.wait_ge(*at(f"dn.y{h}.{s - 1}"))
                        if s < 5:
                            dve.wait_ge(*at(f"dn.x{h}.{s - 1}"))
                            tt(m["x"], m["x"], b[2][:], ALU.subtract).then_inc(*tick("dn_dve", f"dn.x{h}.{s}"))
                        tt(m["y"], m["y"], b[3][:], ALU.subtract).then_inc(*tick("dn_dve", f"dn.y{h}.{s}"))
            for n in range(8):
                t, r = n // 2, slice(64 * (n % 2), 64 * (n % 2) + 64)
                for g in range(2):
                    hs = slice(4 * g, 4 * g + 4)
                    dve.wait_ge(*at(f"scan.ws{n}.{g}"))
                    if n == 0:
                        dve.wait_ge(*at(f"dn.w{H - 1}"))
                    if n >= 1:
                        dve.wait_ge(*at(f"scan.kv{n - 1}.{g}"))
                    tt(vN[r, hs, :], qkv[r, 16 + 4 * g:20 + 4 * g, t * P:(t + 1) * P],
                       bank[g][r, :].rearrange("p (h d) -> p h d", h=4), ALU.subtract).then_inc(*tick("scan_dve", f"scan.vn{n}.{g}"))
                for g in range(2):
                    dve.wait_ge(*at(f"scan.kv{n}.{g}"))
                    dve.wait_ge(*at(f"scan.state{n - 1}.{g}"))
                    for hh in range(4):
                        h = 4 * g + hh
                        last = stt(S[:, h, :], S[:, h, :], gl[:, h, n:n + 1], bank[2 + g][:, hh * P:(hh + 1) * P], ALU.mult, ALU.add)
                    last.then_inc(*tick("scan_dve", f"scan.state{n}.{g}"))
                if n == 2:
                    lo_early("dn_out")

            dve.wait_ge(*at(f"gated.sum{TT - 1}"))
            tt(stat[:, 0:32], bank[7][:, 0:32], tok[:, 11, :], ALU.mult).then_inc(*tick("norm_dve", "gated.sums_scaled"))
            dve.wait_ge(*at("gated.root"))
            chain(nc.vector.reciprocal(stat[:, 0:32], small[:, 0:32]), "norm_dve", "gated.inverse")
            chain(tt(stat[:, 0:32], stat[:, 0:32], tok[:, 9, :], ALU.mult), "norm_dve", "gated.factor")
            dve.wait_ge(*at(f"gated.z{TT - 1}"))
            head_norms("gated", lambda h: qkv[:, h, :], v("dn_norm"), oH, oL)
            stream_out2("dn_out", "x1", early=1)
            lo_early("mlp_up0")
            inverse_kept("mlp2", "mlp_up0")
            for g in range(2):
                name = f"mlp_up{g}"
                for i in ev.loop(dve, looped(name, 2), peel=int(g == 0)):
                    for s in range(2):
                        lo_next(name, i, s, early=2 * (g == 0))
                        for tl in range(2):
                            c = 2 * s + tl
                            done(name, i * 4 + c)
                            tt(y[:, c, :], bank[c][:], rinv, ALU.mult).then_inc(evac, 1)
                            dve.wait_ge(evac, i * 4 + (c + 1 + TILE0[name]))
                            stt(y[:, 4 + c, :], y[:, c, :], 0.0, y[:, c, :], ALU.max, ALU.mult)\
                                .then_inc(*tick("mlp_dve", f"{name}.mid{c}"))
                            dve.wait_ge(*at(f"{name}.hi{c}", i))
                            t1 = bass.ds(i * 4 + c, 1)
                            tt(mL[:, t1, :], y[:, 4 + c, :].unsqueeze(1), mH[:, t1, :].bitcast(F32), ALU.subtract)\
                                .then_inc(*tick("mlp_dve", f"{name}.lo{c}"))
                stream_down(f"mlp_down{g}", ("x0", "x1")[g])
            stream_down("mlp_down2", "x1", last=True, t0=4)
            dve.wait_ge(*at("final.root"))
            chain(nc.vector.reciprocal(stat[:, 0:TT], small[:, 0:TT]), "norm_dve", "final.inverse")
            for t in range(TT):
                dve.wait_ge(*at(f"out.turned{t}.1"))
                ts(xin[:, t, 512:1024], bank[(5 + 2 * t) % 7][:], stat[:, t:t + 1], None, ALU.mult)\
                    .then_inc(*tick("out_scaled_dve", f"out.copied{t}.1"))

        @block.gpsimd
        def _(pool):
            def tt(*args):
                return nc.gpsimd.tensor_tensor(*args)

            def add(tag):
                for k in range(1, KT):
                    pool.wait_ge(*at(f"{tag}.t{k}"))
                    tt(x[:, k, :], x[:, k, :], y[:, k, :], ALU.add).then_inc(*tick("norm_pool", f"{tag}.x{k}"))

            def first_squares(tag):
                for k in range(1, KT - 2):
                    pool.wait_ge(*at(f"{tag}.sq{k}"))
                    if k > 1:
                        pool.wait_ge(*at(f"{tag}.squares{k - 1}"))
                    tt(y[:, 0, :], y[:, 0, :], y[:, k, :], ALU.add)\
                        .then_inc(*tick("squares_pool", f"{tag}.first_squares" if k == KT - 3 else f"{tag}.squares{k}"))

            first_squares("mix_pre0")
            pool.wait_ge(*at("rope.key"))
            nc.gpsimd.tensor_copy(kM[64:96, :, :], misc[64:96, :].unsqueeze(1).to_broadcast([32, H, SEQ]))\
                .then_inc(*tick("rope_pool", "rope.k"))
            add("mix_post0")
            first_squares("ffn_pre0")
            add("ffn_post0")
            first_squares("mix_pre1")
            pool.wait_ge(*at("in.dist"))

            def slope(h):
                if h >= 2:
                    pool.wait_ge(*at(f"diff.biased{(h - 2) * 8 + 7}"))
                nc.gpsimd.tensor_scalar(alibi[:, h % 2, :], dist[:], 2.0 ** -(h + 1), None, ALU.mult)\
                    .then_inc(*tick("alibi_pool", f"alibi{h}"))
            slope(0)
            slope(1)
            for h in range(2, H):
                slope(h)
            add("mix_post1")
            first_squares("ffn_pre1")
            add("ffn_post1")
            first_squares("mix2")
            for h0 in range(0, H, 2):
                for h in (h0, h0 + 1):
                    m = tmp(h % 2)
                    pool.wait_ge(*at(f"dn.gram{h}"))
                    pool.wait_ge(*at(f"dn.gl{h}"))
                    tt(qkv[:, h, :], qkv[:, h, :], m["e"], ALU.mult).then_inc(*tick("dn_pool", f"dn.qdec{h}"))
            for t in range(TT):
                pool.wait_ge(*at(f"gated.sq{t}"))
                tk = slice(t * P, (t + 1) * P)
                tt(qkv[:, 0:H, tk], qkv[:, 0:H, tk], zT[:, :, tk], ALU.mult).then_inc(*tick("gated_pool", f"gated.z{t}"))

    return ev.found


def constants():
    i, j = np.arange(P)[:, None], np.arange(P)[None, :]
    u = np.arange(SEQ)[None, :]
    window = np.where(u <= FAR + i, 0.0, NEG)
    const = np.concatenate([np.eye(P), np.ones((P, P)), window], 1)
    dist = np.where(u <= FAR + i, u - (FAR + i), NEG)
    chunk = (i // 64) == (j // 64)
    masks = [chunk & (i <= j), chunk, (i % 2 == 0) & (j == i + 1)]
    masks += [((i // b) % 2 == 1) & (j // b == i // b - 1) for b in (2, 4, 8, 16, 32)]
    masks += [np.where(masks[0], 0.0, NEG)]
    rope = np.zeros((P, 1056), np.float32)
    f = np.float32
    inv = f(10000.0) ** (-np.arange(0, 32, 2, dtype=f) / f(32))
    ang = np.arange(SEQ, dtype=f)[None, :] * inv[:, None]
    for half in range(2):
        rope[64 + 16 * half:80 + 16 * half, 0:512] = np.cos(ang)
        rope[64 + 16 * half:80 + 16 * half, 512:1024] = np.sin(ang)
    for m in range(16):
        rope[80 + m, 1024 + m] = -1.0
        rope[64 + m, 1040 + m] = 1.0
    return {"const": const.astype(f), "dist": dist.astype(f), "rope": rope,
            "dconst": np.concatenate(masks, 1).astype(f)}


def units(w, cols):
    k, m = w.shape
    return w.reshape(k // P, P, m // cols, cols).transpose(2, 1, 0, 3).reshape(m // cols, P, -1)


def kernel(**inputs):
    import concourse.bacc as bacc
    from concourse.bass_utils import run_bass_kernel_spmd as run

    a = {n: np.asarray(t) for n, t in inputs.items()}
    w = a["even_w_in"][0]
    cuts = np.cumsum([512, 512, 512, 8, 384, 256]).tolist()
    fq, fk, fv, _, cq, ckv, kr = np.split(w, cuts, axis=1)
    misc = np.concatenate([w[:, cuts[2]:cuts[2] + 64], kr, cq[:, 0:32]], 1)
    arrays = dict(constants())
    arrays["x"] = a["x"][0].reshape(TT, P, DM).transpose(1, 0, 2)
    arrays["even_in"] = units(np.concatenate([misc, cq, ckv, fq, fk, fv], 1), 256)
    arrays["even_uq"] = units(a["even_w_uq"][0], 384)
    arrays["even_ukv"] = units(a["even_w_ukv"][0], 1024)
    arrays["even_out"] = units(a["even_w_out"][0], 256)
    for n, part in zip("qkv", np.split(a["odd_w_in"][0], 3, axis=1)):
        arrays[f"odd_{n}"] = units(part, 256)
    arrays["odd_out"] = units(a["odd_w_out"][0], 256)
    for l in range(2):
        gate, val = np.split(a["ffn_w_up"][l], 2, axis=1)
        up = np.concatenate([gate.reshape(KT, P, FF_T, P), val.reshape(KT, P, FF_T, P)], 3)
        up = up.transpose(2, 1, 0, 3).reshape(FF_T, P, -1)
        cut = FF_GROUPS[0]
        arrays[f"ffn{l}_up0"], arrays[f"ffn{l}_up1"] = up[:cut], up[cut:]
        down = a["ffn_w_down"][l]
        arrays[f"ffn{l}_down0"], arrays[f"ffn{l}_down1"] = units(down[:cut * P], P), units(down[cut * P:], P)
    w = a["dn_w_in_2"][0]
    arrays["dn_qkv"], arrays["dn_z"] = units(w[:, :3072], 256), units(w[:, 3072:4096], 256)
    arrays["wba"] = units(w[:, 4096:], 16)[0]
    arrays["dn_out"] = units(a["dn_w_out_2"][0], 256)
    up, down = units(a["mlp_w_up_2"][0], 256), a["mlp_w_down_2"][0]
    half = MLP_GROUP * P
    arrays["mlp_up0"], arrays["mlp_up1"] = up[:8], up[8:]
    arrays["mlp_down0"] = units(down[:half], P)
    arrays["mlp_down1"], arrays["mlp_down2"] = np.split(units(down[half:], P), 2)

    def col(t):
        return t.reshape(-1, P).T

    def wide(t):
        return np.broadcast_to(t.reshape(1, -1), (P, t.size))
    pieces = []
    for l in range(2):
        pieces += [col(a[n][l]) for n in ("norm_mix_pre", "norm_mix_post", "norm_ffn_pre", "norm_ffn_post")]
    pieces += [col(a[n]) for n in ("norm_mix_2", "norm_mlp_2", "norm_final_2", "even_q_norm", "even_kv_norm")]
    for l in range(2):
        pieces += [col(a["ffn_conv_w"][l]), col(a["ffn_conv_b"][l])]
    forget = np.zeros((P, 1), np.float32)
    forget[0:H, 0] = a["even_b_forget"][0]
    pieces += [col(a["dn_conv_w_2"][0]), col(a["dn_norm_w_2"]), col(a["odd_subln"]), forget]
    pieces += [wide(a[n]) for n in ("dn_a_log_2", "dn_dt_bias_2", "odd_lambda_q1", "odd_lambda_k1",
                                    "odd_lambda_q2", "odd_lambda_k2")]
    arrays["vec"] = np.concatenate(pieces, 1)
    arrays = {n: np.ascontiguousarray(t) for n, t in arrays.items()}

    def program(known):
        nc = bacc.Bacc("TRN2", target_bir_lowering=False, num_devices=1)
        dram = {n: nc.dram_tensor(f"in_{n}", t.shape, F32, kind="ExternalInput").ap() for n, t in arrays.items()}
        dram["out"] = nc.dram_tensor("out", (SEQ, DM), F32, kind="ExternalOutput").ap()
        return nc, build(nc, dram, known)

    _, known = program(None)
    nc, _ = program(known)
    r = run(nc, [{f"in_{n}": t for n, t in arrays.items()}], core_ids=[0])
    return r.results[0]["out"].reshape(1, SEQ, DM)
```
